# Optimizing a Trainium2 kernel written in Bass

```python
import jax
import jax.numpy as jnp
from jax import lax
import numpy as np
import jax, jax.numpy as jnp

D_MODEL = 1024
BATCH = 1
SEQ = 256
DEPTH = 1

RW_HEAD_DIM = 64
RW_WIDTH = D_MODEL // 2
RW_HEADS = RW_WIDTH // RW_HEAD_DIM
RW_DECAY_RANK = 64
RW_ICLR_RANK = 64
RW_GATE_RANK = 128
RW_GN_EPS = 64e-5
RET_QK_DIM = 64
RET_QK_WIDTH = D_MODEL // 2
RET_HEADS = RET_QK_WIDTH // RET_QK_DIM
RET_V_DIM = 2 * RET_QK_DIM
RET_V_WIDTH = RET_HEADS * RET_V_DIM
RET_CHUNK = 128
ROPE_BASE = 10000.0
RET_GN_EPS = 1e-5
D_FF = 2816
CONV_WIDTH = 3
RMS_EPS = 1e-6

RW_SIZES = (RW_WIDTH, RW_WIDTH, RW_WIDTH, RW_DECAY_RANK, RW_ICLR_RANK, RW_GATE_RANK)
RET_SIZES = (RET_QK_WIDTH, RET_QK_WIDTH, RET_V_WIDTH, RET_V_WIDTH)
RW_COLS = sum(RW_SIZES)
RET_COLS = sum(RET_SIZES)
IN_SIZES = (RW_COLS, RET_COLS, D_MODEL, D_MODEL)
IN_COLS = sum(IN_SIZES)


def _split(z, sizes):
    return jnp.split(z, [int(s) for s in np.cumsum(sizes)[:-1]], axis=-1)

def rms_norm(x, g):
    xf = x.astype(jnp.float32)
    y = xf * lax.rsqrt(jnp.mean(xf * xf, axis=-1, keepdims=True) + RMS_EPS)
    return (y * g.astype(jnp.float32)).astype(x.dtype)

def group_norm_heads(z, eps):
    mu = jnp.mean(z, axis=-1, keepdims=True)
    var = jnp.mean(jnp.square(z - mu), axis=-1, keepdims=True)
    return (z - mu) * lax.rsqrt(var + eps)

def token_shift(p):
    return jnp.pad(p, ((0, 0), (1, 0), (0, 0)))[:, :-1]

def rwkv7_mixer(p, mu, w0, w2, a0, a2, g2, k_k, k_a, r_k, lnx_w, lnx_b):
    B, T, _ = p.shape
    H, N = RW_HEADS, RW_HEAD_DIM
    p = p.astype(jnp.float32)
    p = p + (token_shift(p) - p) * mu.astype(jnp.float32)
    r, k, v, wd, ad, gd = _split(p, RW_SIZES)
    w = -jax.nn.softplus(-(w0 + jnp.tanh(wd) @ w2)) - 0.5
    decay = jnp.exp(-jnp.exp(w))
    a = jax.nn.sigmoid(a0 + ad @ a2)
    g = jax.nn.sigmoid(gd) @ g2
    heads = lambda z: z.reshape(B, T, H, N).astype(jnp.float32)
    kk = heads(k * k_k)
    kk = kk / jnp.maximum(jnp.sqrt(jnp.sum(kk * kk, axis=-1, keepdims=True)), 1e-12)
    k = k * (1.0 + (a - 1.0) * k_a)
    r, k, v, decay, a = heads(r), heads(k), heads(v), heads(decay), heads(a)

    def step(S, inp):
        r_t, k_t, v_t, w_t, kk_t, a_t = inp
        sa = jnp.einsum('bhvk,bhk->bhv', S, -kk_t)
        S = (S * w_t[:, :, None, :]
             + sa[..., None] * (kk_t * a_t)[:, :, None, :]
             + v_t[..., None] * k_t[:, :, None, :])
        y = jnp.einsum('bhvk,bhk->bhv', S, r_t)
        return S, y

    xs = tuple(jnp.moveaxis(z, 1, 0) for z in (r, k, v, decay, kk, a))
    S0 = jnp.zeros((B, H, N, N), jnp.float32)
    _, y = lax.scan(step, S0, xs)
    y = jnp.moveaxis(y, 0, 1)
    y = group_norm_heads(y, RW_GN_EPS) * lnx_w.reshape(H, N) + lnx_b.reshape(H, N)
    bonus = jnp.sum(r * k * r_k.reshape(H, N), axis=-1, keepdims=True) * v
    return (y + bonus).reshape(B, T, RW_WIDTH) * g

def rotary(z, pos):
    half = z.shape[-1] // 2
    inv = ROPE_BASE ** (-jnp.arange(half, dtype=jnp.float32) / half)
    ang = pos.astype(jnp.float32)[..., None] * inv
    cos = jnp.cos(ang)[:, :, None, :]
    sin = jnp.sin(ang)[:, :, None, :]
    z1, z2 = z[..., :half], z[..., half:]
    return jnp.concatenate([z1 * cos - z2 * sin, z1 * sin + z2 * cos], axis=-1)

def retention_mixer(p, positions):
    B, T, _ = p.shape
    H, dk, dv, C = RET_HEADS, RET_QK_DIM, RET_V_DIM, RET_CHUNK
    q, k, v, g = _split(p.astype(jnp.float32), RET_SIZES)
    q = rotary(q.reshape(B, T, H, dk), positions)
    k = rotary(k.reshape(B, T, H, dk), positions) * (dk ** -0.5)
    v = v.reshape(B, T, H, dv)
    log_gamma = jnp.log1p(-jnp.exp2(-5.0 - jnp.arange(H, dtype=jnp.float32)))
    idx = jnp.arange(C, dtype=jnp.float32)
    rel = idx[:, None] - idx[None, :]
    decay_mask = jnp.where(rel[None] >= 0,
                           jnp.exp(jnp.maximum(rel, 0.0)[None] * log_gamma[:, None, None]), 0.0)
    q_decay = jnp.exp((idx + 1.0)[:, None] * log_gamma[None, :])[None, :, :, None]
    k_decay = jnp.exp((C - 1.0 - idx)[:, None] * log_gamma[None, :])[None, :, :, None]
    chunk_decay = jnp.exp(C * log_gamma)[None, :, None, None]
    n_chunks = T // C
    chunks = lambda z: jnp.moveaxis(z.reshape(B, n_chunks, C, H, z.shape[-1]), 1, 0)

    def step(R, inp):
        qc, kc, vc = inp
        s = jnp.einsum('bihd,bjhd->bhij', qc, kc) * decay_mask
        inner = jnp.einsum('bhij,bjhe->bihe', s, vc)
        cross = jnp.einsum('bihd,bhde->bihe', qc * q_decay, R)
        R = R * chunk_decay + jnp.einsum('bjhd,bjhe->bhde', kc * k_decay, vc)
        return R, inner + cross

    R0 = jnp.zeros((B, H, dk, dv), jnp.float32)
    _, o = lax.scan(step, R0, (chunks(q), chunks(k), chunks(v)))
    o = jnp.moveaxis(o, 0, 1).reshape(B, T, H, dv)
    o = group_norm_heads(o, RET_GN_EPS).reshape(B, T, RET_V_WIDTH)
    return jax.nn.silu(g) * o

def conv_ffn(h, w_up, conv_w, conv_b, w_down):
    u = h @ w_up
    T = u.shape[1]
    up = jnp.pad(u, ((0, 0), (CONV_WIDTH - 1, 0), (0, 0)))
    u = sum(up[:, i:i + T] * conv_w[i] for i in range(CONV_WIDTH)) + conv_b
    gate, val = jnp.split(u, 2, axis=-1)
    return (jax.nn.gelu(gate, approximate=True) * val) @ w_down

def first_inputs(seed: int = 0) -> dict:
    key = jax.random.key(seed)
    ks = jax.random.split(key, 26)
    f32 = jnp.float32
    L = DEPTH
    nrm = lambda k, shape, s: s * jax.random.normal(k, shape, f32)
    x = jax.random.normal(ks[0], (BATCH, SEQ, D_MODEL), f32)
    offsets = jax.random.randint(ks[1], (BATCH, 1), 0, 4096, dtype=jnp.int32)
    positions = offsets + jnp.arange(SEQ, dtype=jnp.int32)[None, :]
    return {
        "x": x,
        "positions": positions,
        "norm_mix_pre": 1.0 + nrm(ks[2], (L, D_MODEL), 0.1),
        "norm_mix_post": 1.0 + nrm(ks[3], (L, D_MODEL), 0.1),
        "norm_ffn_pre": 1.0 + nrm(ks[4], (L, D_MODEL), 0.1),
        "norm_ffn_post": 1.0 + nrm(ks[5], (L, D_MODEL), 0.1),
        "w_in": nrm(ks[6], (L, D_MODEL, IN_COLS), D_MODEL ** -0.5),
        "rw_mu": jax.random.uniform(ks[7], (L, RW_COLS), f32, 0.0, 1.0),
        "rw_w0": jax.random.uniform(ks[8], (L, RW_WIDTH), f32, -6.0, 1.0),
        "rw_w2": nrm(ks[9], (L, RW_DECAY_RANK, RW_WIDTH), 0.1 * RW_DECAY_RANK ** -0.5),
        "rw_a0": nrm(ks[10], (L, RW_WIDTH), 0.1),
        "rw_a2": nrm(ks[11], (L, RW_ICLR_RANK, RW_WIDTH), 0.5 * RW_ICLR_RANK ** -0.5),
        "rw_g2": nrm(ks[12], (L, RW_GATE_RANK, RW_WIDTH), RW_GATE_RANK ** -0.5),
        "rw_k_k": 0.85 + nrm(ks[13], (L, RW_WIDTH), 0.1),
        "rw_k_a": 1.0 + nrm(ks[14], (L, RW_WIDTH), 0.1),
        "rw_r_k": nrm(ks[15], (L, RW_WIDTH), 0.1),
        "rw_lnx_w": 1.0 + nrm(ks[16], (L, RW_WIDTH), 0.1),
        "rw_lnx_b": nrm(ks[17], (L, RW_WIDTH), 0.01),
        "w_branch_rw": nrm(ks[18], (L, RW_WIDTH, D_MODEL), RW_WIDTH ** -0.5),
        "w_branch_ret": nrm(ks[19], (L, RET_V_WIDTH, D_MODEL), RET_V_WIDTH ** -0.5),
        "w_out": nrm(ks[20], (L, D_MODEL, D_MODEL), D_MODEL ** -0.5),
        "ffn_w_up": nrm(ks[21], (L, D_MODEL, 2 * D_FF), D_MODEL ** -0.5),
        "ffn_conv_w": nrm(ks[22], (L, CONV_WIDTH, 2 * D_FF), CONV_WIDTH ** -0.5),
        "ffn_conv_b": nrm(ks[23], (L, 2 * D_FF), 0.01),
        "ffn_w_down": nrm(ks[24], (L, D_FF, D_MODEL), D_FF ** -0.5),
    }

def first_block(x, positions, norm_mix_pre, norm_mix_post, norm_ffn_pre, norm_ffn_post, w_in,
              rw_mu, rw_w0, rw_w2, rw_a0, rw_a2, rw_g2, rw_k_k, rw_k_a, rw_r_k, rw_lnx_w, rw_lnx_b,
              w_branch_rw, w_branch_ret, w_out, ffn_w_up, ffn_conv_w, ffn_conv_b, ffn_w_down):
    h = x
    for l in range(DEPTH):
        hn = rms_norm(h, norm_mix_pre[l])
        p = hn @ w_in[l]
        p_rw, p_ret, g_rw, g_ret = _split(p, IN_SIZES)
        y_rw = rwkv7_mixer(p_rw, rw_mu[l], rw_w0[l], rw_w2[l], rw_a0[l], rw_a2[l], rw_g2[l],
                           rw_k_k[l], rw_k_a[l], rw_r_k[l], rw_lnx_w[l], rw_lnx_b[l])
        y_ret = retention_mixer(p_ret, positions)
        merged = (jax.nn.sigmoid(g_rw.astype(jnp.float32)) * (y_rw @ w_branch_rw[l])
                  + jax.nn.sigmoid(g_ret.astype(jnp.float32)) * (y_ret @ w_branch_ret[l]))
        h = h + rms_norm(merged @ w_out[l], norm_mix_post[l])
        f = conv_ffn(rms_norm(h, norm_ffn_pre[l]), ffn_w_up[l], ffn_conv_w[l], ffn_conv_b[l], ffn_w_down[l])
        h = h + rms_norm(f, norm_ffn_post[l])
    return h.astype(x.dtype)


D_PLE = 256
D_MIX = 2 * D_MODEL
GM_WIDTH = D_MIX // 2
GM_HEADS = 8
GM_HEAD_DIM = GM_WIDTH // GM_HEADS
GM_CHUNK = 128
SSM_WIDTH = D_MIX - GM_WIDTH
SSM_HEAD_DIM = 64
SSM_HEADS = SSM_WIDTH // SSM_HEAD_DIM
SSM_GROUPS = 2
SSM_STATE = 128
SSM_CONV = 4
SSM_CHUNK = 128
SSM_CONV_DIM = SSM_WIDTH + 2 * SSM_GROUPS * SSM_STATE
D_FF_2 = 256 * ((8 * D_MODEL // 3 + 255) // 256)
EPS = 1e-6
IN_SPLITS = (GM_WIDTH, 2 * GM_WIDTH, 2 * GM_WIDTH + SSM_WIDTH, 2 * GM_WIDTH + SSM_WIDTH + SSM_CONV_DIM)
IN_PROJ_DIM = 2 * GM_WIDTH + SSM_WIDTH + SSM_CONV_DIM + SSM_HEADS


def rmsnorm(x, g):
    xf = x.astype(jnp.float32)
    y = xf * lax.rsqrt(jnp.mean(xf * xf, axis=-1, keepdims=True) + EPS)
    return (y * g.astype(jnp.float32)).astype(x.dtype)

def layernorm(x, g, b):
    xf = x.astype(jnp.float32)
    mu = jnp.mean(xf, axis=-1, keepdims=True)
    xc = xf - mu
    y = xc * lax.rsqrt(jnp.mean(xc * xc, axis=-1, keepdims=True) + EPS)
    return (y * g.astype(jnp.float32) + b.astype(jnp.float32)).astype(x.dtype)

def swiglu(x, w_gate, w_up, w_down):
    return (jax.nn.silu(x @ w_gate) * (x @ w_up)) @ w_down

def chunked_spatial_gating(u, v, ln_g, ln_b, w_s, b_s):
    bsz, L, _ = u.shape
    nc = L // GM_CHUNK
    v = layernorm(v, ln_g, ln_b).reshape(bsz, nc, GM_CHUNK, GM_HEADS, GM_HEAD_DIM)
    mask = jnp.tril(jnp.ones((GM_CHUNK, GM_CHUNK), dtype=bool))
    w = jnp.where(mask, w_s, jnp.zeros_like(w_s)).astype(v.dtype)
    mixed = jnp.einsum("hts,bcshd->bcthd", w, v) + b_s.T.astype(v.dtype)[None, None, :, :, None]
    return u * mixed.reshape(bsz, L, GM_WIDTH)

def causal_depthwise_conv(x, w, b):
    y = lax.conv_general_dilated(
        x, w[:, None, :].astype(x.dtype), window_strides=(1,), padding=[(SSM_CONV - 1, 0)],
        dimension_numbers=("NWC", "WIO", "NWC"), feature_group_count=x.shape[-1])
    return y + b.astype(x.dtype)

def segsum_exp(cs):
    T = cs.shape[-1]
    diff = cs[..., :, None] - cs[..., None, :]
    mask = jnp.tril(jnp.ones((T, T), dtype=bool))
    return jnp.exp(jnp.where(mask, diff, -jnp.inf))

def ssd_chunked(x, dt, a, bm, cm):
    bsz, L, H, P = x.shape
    nc = L // SSM_CHUNK
    k = H // SSM_GROUPS
    xdt = (x * dt[..., None]).reshape(bsz, nc, SSM_CHUNK, SSM_GROUPS, k, P)
    adt = (dt * a).reshape(bsz, nc, SSM_CHUNK, SSM_GROUPS, k).transpose(0, 3, 4, 1, 2)
    bm = bm.reshape(bsz, nc, SSM_CHUNK, SSM_GROUPS, SSM_STATE)
    cm = cm.reshape(bsz, nc, SSM_CHUNK, SSM_GROUPS, SSM_STATE)
    a_cs = jnp.cumsum(adt, axis=-1)
    decay = segsum_exp(a_cs)
    cb = jnp.einsum("bclgn,bcsgn->bgcls", cm, bm)
    y_diag = jnp.einsum("bgkcls,bcsgkp->bclgkp", cb[:, :, None] * decay, xdt)
    decay_states = jnp.exp(a_cs[..., -1:] - a_cs).transpose(0, 3, 4, 1, 2)
    states = jnp.einsum("bclgn,bclgkp->bcgkpn", bm, xdt * decay_states[..., None])
    chunk_tot = jnp.pad(a_cs[..., -1], ((0, 0), (0, 0), (0, 0), (1, 0)))
    decay_chunk = segsum_exp(jnp.cumsum(chunk_tot, axis=-1))
    states = jnp.concatenate([jnp.zeros_like(states[:, :1]), states], axis=1)
    new_states = jnp.einsum("bgkzc,bcgkpn->bzgkpn", decay_chunk, states)
    prev_states = new_states[:, :-1]
    out_decay = jnp.exp(a_cs).transpose(0, 3, 4, 1, 2)
    y_off = jnp.einsum("bclgn,bcgkpn->bclgkp", cm, prev_states) * out_decay[..., None]
    return (y_diag + y_off).reshape(bsz, L, H, P)

def mamba2_mixer(z, xbc, dt_raw, conv_w, conv_b, dt_bias, a_log, d_skip, norm_g):
    bsz, L, _ = z.shape
    f32 = jnp.float32
    xbc = jax.nn.silu(causal_depthwise_conv(xbc, conv_w, conv_b))
    xs, bm, cm = jnp.split(xbc, [SSM_WIDTH, SSM_WIDTH + SSM_GROUPS * SSM_STATE], axis=-1)
    xs = xs.reshape(bsz, L, SSM_HEADS, SSM_HEAD_DIM).astype(f32)
    bm = bm.reshape(bsz, L, SSM_GROUPS, SSM_STATE).astype(f32)
    cm = cm.reshape(bsz, L, SSM_GROUPS, SSM_STATE).astype(f32)
    dt = jax.nn.softplus(dt_raw.astype(f32) + dt_bias.astype(f32))
    a = -jnp.exp(a_log.astype(f32))
    y = ssd_chunked(xs, dt, a, bm, cm) + xs * d_skip.astype(f32)[:, None]
    y = y.reshape(bsz, L, SSM_WIDTH) * jax.nn.silu(z.astype(f32))
    y = y.reshape(bsz, L, SSM_GROUPS, SSM_WIDTH // SSM_GROUPS)
    y = y * lax.rsqrt(jnp.mean(y * y, axis=-1, keepdims=True) + EPS)
    return (y.reshape(bsz, L, SSM_WIDTH) * norm_g.astype(f32)).astype(z.dtype)

def second_inputs(seed: int = 0) -> dict:
    key = jax.random.key(seed)
    ks = iter(jax.random.split(key, 40))

    def nrm(shape, scale):
        return jax.random.normal(next(ks), shape, jnp.float32) * scale

    def gain(shape):
        return 1.0 + 0.1 * jax.random.normal(next(ks), shape, jnp.float32)

    L = DEPTH
    x = jax.random.normal(next(ks), (BATCH, SEQ, D_MODEL), jnp.float32)
    p = jax.random.normal(next(ks), (DEPTH, BATCH, SEQ, D_PLE), jnp.float32)
    dt0 = jnp.exp(jax.random.uniform(next(ks), (L, SSM_HEADS), jnp.float32)
                  * (np.log(0.1) - np.log(0.001)) + np.log(0.001))
    dt0 = jnp.maximum(dt0, 1e-4)
    dt_bias = dt0 + jnp.log(-jnp.expm1(-dt0))
    a_log = jnp.log(jax.random.uniform(next(ks), (L, SSM_HEADS), jnp.float32, 1.0, 16.0))
    return {
        "x": x,
        "p": p,
        "ffn1_norm": gain((L, D_MODEL)),
        "ffn1_w_gate": nrm((L, D_MODEL, D_FF_2), D_MODEL ** -0.5),
        "ffn1_w_up": nrm((L, D_MODEL, D_FF_2), D_MODEL ** -0.5),
        "ffn1_w_down": nrm((L, D_FF_2, D_MODEL), D_FF_2 ** -0.5),
        "mix_norm": gain((L, D_MODEL)),
        "w_in": nrm((L, D_MODEL, IN_PROJ_DIM), D_MODEL ** -0.5),
        "gm_ln_g": gain((L, GM_WIDTH)),
        "gm_ln_b": nrm((L, GM_WIDTH), 0.02),
        "gm_w_s": nrm((L, GM_HEADS, GM_CHUNK, GM_CHUNK), 0.5 * GM_CHUNK ** -0.5),
        "gm_b_s": gain((L, GM_HEADS, GM_CHUNK)),
        "gm_out_norm": gain((L, GM_WIDTH)),
        "conv_w": nrm((L, SSM_CONV, SSM_CONV_DIM), SSM_CONV ** -0.5),
        "conv_b": nrm((L, SSM_CONV_DIM), 0.02),
        "dt_bias": dt_bias,
        "a_log": a_log,
        "d_skip": gain((L, SSM_HEADS)),
        "ssm_norm": gain((L, SSM_WIDTH)),
        "w_out": nrm((L, D_MIX, D_MODEL), D_MIX ** -0.5),
        "ffn2_norm": gain((L, D_MODEL)),
        "ffn2_w_gate": nrm((L, D_MODEL, D_FF_2), D_MODEL ** -0.5),
        "ffn2_w_up": nrm((L, D_MODEL, D_FF_2), D_MODEL ** -0.5),
        "ffn2_w_down": nrm((L, D_FF_2, D_MODEL), D_FF_2 ** -0.5),
        "ple_norm": gain((L, D_MODEL)),
        "ple_w_gate": nrm((L, D_MODEL, D_MODEL), D_MODEL ** -0.5),
        "ple_b_gate": nrm((L, D_MODEL), 0.02),
        "ple_w_proj": nrm((L, D_PLE, D_MODEL), D_PLE ** -0.5),
        "final_norm": gain((D_MODEL,)),
    }

def second_block(x, p, ffn1_norm, ffn1_w_gate, ffn1_w_up, ffn1_w_down, mix_norm, w_in,
              gm_ln_g, gm_ln_b, gm_w_s, gm_b_s, gm_out_norm, conv_w, conv_b, dt_bias, a_log,
              d_skip, ssm_norm, w_out, ffn2_norm, ffn2_w_gate, ffn2_w_up, ffn2_w_down,
              ple_norm, ple_w_gate, ple_b_gate, ple_w_proj, final_norm):
    h = x
    for i in range(DEPTH):
        h = h + 0.5 * swiglu(rmsnorm(h, ffn1_norm[i]), ffn1_w_gate[i], ffn1_w_up[i], ffn1_w_down[i])
        n = rmsnorm(h, mix_norm[i])
        proj = n @ w_in[i]
        u, v, z, xbc, dt_raw = jnp.split(proj, IN_SPLITS, axis=-1)
        ya = chunked_spatial_gating(jax.nn.gelu(u, approximate=False), jax.nn.gelu(v, approximate=False),
                                    gm_ln_g[i], gm_ln_b[i], gm_w_s[i], gm_b_s[i])
        ya = rmsnorm(ya, gm_out_norm[i])
        yb = mamba2_mixer(z, xbc, dt_raw, conv_w[i], conv_b[i], dt_bias[i], a_log[i], d_skip[i], ssm_norm[i])
        h = h + jnp.concatenate([ya, yb], axis=-1) @ w_out[i]
        h = h + 0.5 * swiglu(rmsnorm(h, ffn2_norm[i]), ffn2_w_gate[i], ffn2_w_up[i], ffn2_w_down[i])
        gate = jax.nn.sigmoid(rmsnorm(h, ple_norm[i]) @ ple_w_gate[i] + ple_b_gate[i])
        h = h + gate * (p[i] @ ple_w_proj[i])
    return rmsnorm(h, final_norm)


def setup_inputs(seed=0):
    out = dict(first_inputs(seed))
    for name, value in second_inputs(seed + 1).items():
        if name != "x":
            out[name + "_2"] = value
    return out


def reference(
    x, positions, norm_mix_pre, norm_mix_post, norm_ffn_pre, norm_ffn_post, w_in, rw_mu, rw_w0,
    rw_w2, rw_a0, rw_a2, rw_g2, rw_k_k, rw_k_a, rw_r_k, rw_lnx_w, rw_lnx_b, w_branch_rw,
    w_branch_ret, w_out, ffn_w_up, ffn_conv_w, ffn_conv_b, ffn_w_down, p_2, ffn1_norm_2,
    ffn1_w_gate_2, ffn1_w_up_2, ffn1_w_down_2, mix_norm_2, w_in_2, gm_ln_g_2, gm_ln_b_2,
    gm_w_s_2, gm_b_s_2, gm_out_norm_2, conv_w_2, conv_b_2, dt_bias_2, a_log_2, d_skip_2,
    ssm_norm_2, w_out_2, ffn2_norm_2, ffn2_w_gate_2, ffn2_w_up_2, ffn2_w_down_2, ple_norm_2,
    ple_w_gate_2, ple_b_gate_2, ple_w_proj_2, final_norm_2,
):
    x = first_block(
        x, positions, norm_mix_pre, norm_mix_post, norm_ffn_pre, norm_ffn_post, w_in, rw_mu,
        rw_w0, rw_w2, rw_a0, rw_a2, rw_g2, rw_k_k, rw_k_a, rw_r_k, rw_lnx_w, rw_lnx_b,
        w_branch_rw, w_branch_ret, w_out, ffn_w_up, ffn_conv_w, ffn_conv_b, ffn_w_down,
    )
    return second_block(
        x, p_2, ffn1_norm_2, ffn1_w_gate_2, ffn1_w_up_2, ffn1_w_down_2, mix_norm_2, w_in_2,
        gm_ln_g_2, gm_ln_b_2, gm_w_s_2, gm_b_s_2, gm_out_norm_2, conv_w_2, conv_b_2, dt_bias_2,
        a_log_2, d_skip_2, ssm_norm_2, w_out_2, ffn2_norm_2, ffn2_w_gate_2, ffn2_w_up_2,
        ffn2_w_down_2, ple_norm_2, ple_w_gate_2, ple_b_gate_2, ple_w_proj_2, final_norm_2,
    )


_drawn_inputs = setup_inputs


def setup_inputs(seed=0):
    import zlib

    import numpy as np

    out = dict(_drawn_inputs(seed))
    spreads = {}
    factors = {'rw_w2': 8.0,
     'rw_lnx_b': 8.0,
     'ffn_conv_b': 6.462,
     'gm_ln_g_2': 5.082,
     'gm_ln_b_2': 35.112,
     'conv_b_2': 5.285,
     'ffn2_norm_2': 2.736,
     'ple_norm_2': 18.365,
     'ple_b_gate_2': 64.0}
    for name, (base, spread) in spreads.items():
        noise = np.random.default_rng([zlib.crc32(name.encode()), seed]).standard_normal(out[name].shape)
        drawn = base * np.exp(spread * noise) if base else spread * noise
        out[name] = jnp.asarray(drawn.astype(out[name].dtype))
    for name, factor in factors.items():
        out[name] = (out[name] * factor).astype(out[name].dtype)
    return out
```

```python
from contextlib import ExitStack

import numpy as np

import concourse.bass as bass
from concourse import mybir

F32 = mybir.dt.float32
F32R = mybir.dt.float32r
I32 = mybir.dt.int32
ACT = mybir.ActivationFunctionType
ALU = mybir.AluOpType
AX_X = mybir.AxisListType.X

P = 128
T = 256
D = 1024
KD = D // P
NHALF = T // P
RW = 512
RW_COLS = 1792
RET_COLS = 3072
FF = 2816
KF = FF // P
PAIRS = FF // 256
XBC = 1536
DT_COL = 4608
RING = 4
UNIT = 2048

STREAM = (
    ("rw", RW_COLS // 256), ("ret", RET_COLS // 256), ("gates", 2 * D // 256),
    ("branch_rw", 2), ("branch_ret", 4), ("mix_out", 4), ("conv_up", 2 * PAIRS), ("conv_down", PAIRS),
    ("ffn1_up", 2 * PAIRS), ("ffn1_down", PAIRS), ("uvz", 12), ("xbc", XBC // 256), ("mix2_out", 8),
    ("ffn2_up", 2 * PAIRS), ("ffn2_down", PAIRS), ("ple_gate", 4), ("ple_proj", 1),
)
FIRST = {}
UNITS = 0
for _name, _n in STREAM:
    FIRST[_name] = UNITS
    UNITS += _n

AGAIN = {
    "dt_adt": ("rw_sq", 1), "dt_cs": ("rw_kk0", 1), "dt_e": ("rw_norm", 1), "dt_ecs": ("rw_normrt", 1),
    "dt_mm": ("rw_rk", 1), "dt_na": ("rw_abkr", 1), "dt_used": ("rw_bonus", 1), "dt_whi": ("rw_gnv", 1),
    "dt_wlo": ("rw_gnrt", 1), "gm_mix": ("rw_yn", 1), "gm_ms": ("rw_yg", 1), "gm_rt": ("rw_yhi", 1),
    "gm_sq": ("rw_init", 1), "gm_v": ("rw_lora", 2), "gm_var": ("rw_css", 2), "gm_wt": ("rw_sums", 2),
    "gm_wtc": ("rw_z", 3), "gm_y": ("rw_e", 3), "gm_ya": ("rw_sw", 4), "ssm_att": ("rw_as", 4),
    "ssm_bmc": ("rw_g", 2), "ssm_cb": ("rw_rm_a", 4), "ssm_diff": ("rw_rm_d", 4), "ssm_exp": ("rw_tr", 8),
    "ssm_min": ("rw_l", 2), "ssm_ms": ("rw_lt", 4), "ssm_off": ("rw_xa", 2), "ssm_row": ("rw_xac", 2),
    "ssm_rt": ("rw_mv", 2), "ssm_sq": ("rw_mvc", 2), "ssm_state": ("rw_xmv", 2), "ssm_stc": ("rw_w", 2),
    "ssm_xds": ("rw_yt", 2),
}

COLS = (
    ("mix_pre", 8), ("ffn_pre", 8), ("mu", 14), ("w0", 4), ("a0", 4), ("k_k", 4), ("k_a", 4),
    ("r_k", 4), ("lnx_w", 4), ("lnx_b", 4), ("conv1_w", 3 * 44), ("conv1_b", 44), ("ffn1", 8),
    ("mix2", 8), ("gm_b", 8), ("gm_out", 8), ("conv2_w", 4 * 12), ("conv2_b", 12), ("ssm", 8),
    ("ffn2", 8), ("ple", 8),
)
COL = {}
NCOL = 0
for _name, _n in COLS:
    COL[_name] = NCOL
    NCOL += _n

ROWS = ("mix_post", "ffn_post", "gm_ln_g", "gm_ln_b", "ple_b", "final")

CHUNK = 64
LEVELS = 6
KIND = {"ident": 0, "strict": 1, "incl": 2, "tri": 3, "heads": 4, "level": 5, "decay": 5 + LEVELS,
        "qdecay": 5 + LEVELS + 8, "small": 5 + LEVELS + 8 + 4}
NKIND = KIND["small"] + 1
SMALL_KDECAY, SMALL_INV = 0, 8
DECAY_SCALE = float(np.exp(-0.5))
RMS_EPS = 1e-6
TWO_PI = 2 * np.pi
PI_A = 6.28125
PI_B = 2029 / 2 ** 20
PI_C = float(TWO_PI - PI_A - PI_B)
ROUND = 12582912.0
PI_F32 = 3.1415925


def shape_constants():
    s = np.arange(P)[:, None]
    t = np.arange(P)[None, :]
    same = (s // CHUNK) == (t // CHUNK)
    out = np.zeros((P, NKIND, P), np.float32)
    out[:, KIND["ident"]] = np.eye(P)
    out[:, KIND["strict"]] = same & (s < t)
    out[:, KIND["incl"]] = same & (s <= t)
    out[:, KIND["tri"]] = s <= t
    out[:, KIND["heads"]] = same
    for j in range(LEVELS):
        b = 1 << j
        out[:, KIND["level"] + j] = -1.0 * ((s // (2 * b) == t // (2 * b)) & (s // b % 2 == 0) & (t // b % 2 == 1))
    head = np.arange(8, dtype=np.float32)
    log_gamma = np.log1p(-np.exp2(np.float32(-5.0) - head)).astype(np.float32)
    rel = (t - s).astype(np.float32)
    for h in range(8):
        out[:, KIND["decay"] + h] = np.where(rel >= 0, np.exp(np.maximum(rel, 0) * log_gamma[h]), 0) * 0.125
    for tile in range(4):
        for q in range(2):
            row = np.exp((np.arange(P, dtype=np.float32) + 1) * log_gamma[2 * tile + q])
            out[64 * q:64 * q + 64, KIND["qdecay"] + tile] = row[None, :]
    small = out[:, KIND["small"]]
    small[:, SMALL_KDECAY:SMALL_KDECAY + 8] = np.exp((P - 1 - s).astype(np.float32) * log_gamma[None, :]) * 0.125
    small[:, SMALL_INV:SMALL_INV + 32] = np.float32(10000.0) ** (-np.arange(32, dtype=np.float32) / 32)
    return out.reshape(P, NKIND * P)


def two_layers(nc, io, out):
    x_d, pos_d = io["x"], io["positions"]
    w_in, w_in_2 = io["w_in"], io["w_in_2"]
    w_up = io["ffn_w_up"]

    def k_rows(w):
        return w.rearrange("(k p) n -> p k n", p=P)

    w_in_k, w_in2_k, w_up_k = k_rows(w_in), k_rows(w_in_2), k_rows(w_up)
    brw_k, bret_k = k_rows(io["w_branch_rw"]), k_rows(io["w_branch_ret"])
    pair_k = {
        "conv_up": (w_up_k, w_up_k[:, :, FF:]),
        "ffn1_up": (k_rows(io["ffn1_w_gate_2"]), k_rows(io["ffn1_w_up_2"])),
        "ffn2_up": (k_rows(io["ffn2_w_gate_2"]), k_rows(io["ffn2_w_up_2"])),
    }
    row_w = {
        "mix_out": io["w_out"], "conv_down": io["ffn_w_down"], "ffn1_down": io["ffn1_w_down_2"],
        "mix2_out": io["w_out_2"], "ffn2_down": io["ffn2_w_down_2"], "ple_gate": io["ple_w_gate_2"],
        "ple_proj": io["ple_w_proj_2"],
    }

    ctx = ExitStack()
    with ctx:
        def sb(name, shape, dt=F32, scope=ctx):
            return scope.enter_context(nc.sbuf_tensor(name, shape, dt))

        sems = {}

        def sem(name):
            name = AGAIN.get(name, (name, 0))[0]
            if name not in sems:
                sems[name] = ctx.enter_context(nc.semaphore(name))
            return sems[name]

        w_raw = sb("w_raw", [P, RING, UNIT])
        w_hi = sb("w_hi", [P, RING, UNIT], F32R)
        w_lo = sb("w_lo", [P, RING, UNIT], F32R)
        x_hi = sb("x_hi", [P, KD, T], F32R)
        x_lo = sb("x_lo", [P, KD, T], F32R)
        resid = sb("resid", [P, NHALF, D])
        cols = sb("cols", [P, NCOL])
        consts = sb("consts", [P, 5, P])
        norm_s = sb("norm_s", [P, 16])
        ident = consts[:, 0, :]

        nx = ExitStack()
        xn = sb("xn", [P, NHALF, D], F32, nx)
        nx.close()

        m1 = ExitStack()
        yrw_hi = sb("yrw_hi", [P, 4, T], F32R, m1)
        yrw_lo = sb("yrw_lo", [P, 4, T], F32R, m1)
        ra = ExitStack()
        pm = sb("pm", [P, 14, T], F32, ra)
        g_t = sb("g_t", [P, 4, T], F32, ra)
        bonus = sb("bonus", [P, 4, T], F32, ra)
        a_f = sb("a_f", [P, 4, T], F32, ra)
        b_f = sb("b_f", [P, 4, T], F32, ra)
        pc = sb("pc", [P, 4, 4], F32, ra)
        lvl = sb("lvl", [P, LEVELS, P], F32, ra)
        rb = ExitStack()
        e_pos = sb("e_pos", [P, 4, T], F32, rb)
        sw = sb("sw", [P, 4, T], F32, rb)
        a_s = sb("a_s", [P, 4, T], F32, rb)
        css = sb("css", [P, 4, T], F32, rb)
        kk = sb("kk", [P, 4, T], F32, rb)
        t1 = sb("t1", [P, 4, T], F32, rb)
        psh_flat = sb("psh", [P, 4 * (T + 1)], F32, rb)
        cmask = sb("cmask", [P, 4, T], F32, rb)
        act_w = sb("act_w", [P, 2, T], F32, rb)
        omka = sb("omka", [P, 4], F32, rb)
        small_w = sb("small_w", [P, 2, RW], F32, rb)
        psh = psh_flat[:, :].rearrange("p (b i n) -> p b i n", b=2, i=2)
        t2 = psh_flat[:, 0:4 * T].rearrange("p (i n) -> p i n", i=4)
        rb.close()
        rc = ExitStack()
        a_rm = sb("a_rm", [P, NHALF, RW], F32, rc)
        b_rm = sb("b_rm", [P, NHALF, RW], F32, rc)
        k_rm = sb("k_rm", [P, NHALF, RW], F32, rc)
        v_rm = sb("v_rm", [P, NHALF, RW], F32, rc)
        lm = sb("lm", [P, 8, P], F32, rc)
        xi = sb("xi", [P, 8, P], F32, rc)
        tp = sb("tp", [P, 8, P], F32, rc)
        xa = sb("xa", [P, 4, T], F32, rc)
        st = sb("st", [P, 4, 4, 64], F32, rc)
        stmp = sb("stmp", [P, 4, 64], F32, rc)
        xt = resid[:, :, :].rearrange("p h (g n) -> p h g n", g=8)
        wv = a_rm[:, :, :].rearrange("p h (g n) -> p h g n", g=8)
        lt = pm[:, 8:12, :].rearrange("p a (b n) -> p (a b) n", b=2)
        ys_v = pm[:, 8:12, :].rearrange("p (m a) n -> p m (a n)", m=2)
        rc.close()
        rd = ExitStack()
        yn = sb("yn", [P, NHALF, RW], F32, rd)
        yq = sb("yq", [P, NHALF, RW], F32, rd)
        gn = sb("gn", [P, 4, 16], F32, rd)
        ytmp = sb("ytmp", [P, 4, T], F32, rd)
        rd.close()
        ra.close()
        re = ExitStack()
        yret_hi = sb("yret_hi", [P, 8, T], F32R, re)
        yret_lo = sb("yret_lo", [P, 8, T], F32R, re)
        rf = ExitStack()
        q_rm = sb("q_rm", [P, NHALF, RW], F32, rf)
        kr_rm = sb("kr_rm", [P, NHALF, RW], F32, rf)
        vr_rm = sb("vr_rm", [P, NHALF, D], F32, rf)
        sg_rm = sb("sg_rm", [P, NHALF, D], F32, rf)
        rot = sb("rot", [P, 3, NHALF, RW // 2], F32, rf)
        q_f = resid[:, 0, :].rearrange("p (a n) -> p a n", a=4)
        k_f = resid[:, 1, :].rearrange("p (a n) -> p a n", a=4)
        qd_f = sb("qd_f", [P, 4, P], F32, rf)
        rstate = sb("rstate", [P, 4, P], F32, rf)
        decay = sb("decay", [P, 13, P], F32, rf)
        trig = sb("trig", [P, 6, NHALF, 32], F32, rf)
        posf = sb("posf", [P, 2, NHALF], F32, rf)
        posi = sb("posi", [P, NHALF], I32, rf)
        ret_s = sb("ret_s", [P, 12, 16], F32, rf)
        sco = sb("sco", [P, 2, 4, P], F32, rf)
        rf.close()
        rg = ExitStack()
        sig_rw = sb("sig_rw", [P, 8, T], F32, rg)
        sig_ret = sb("sig_ret", [P, 8, T], F32, rg)
        row_mix = sb("row_mix", [P, D], F32, rg)
        merged = sb("merged", [P, 8, T], F32, rg)
        mtmp = sb("mtmp", [P, 2, 2, T], F32, rg)
        rg.close()
        re.close()
        m1.close()

        ff = ExitStack()
        h_hi = sb("h_hi", [P, KF, T], F32R, ff)
        h_lo = sb("h_lo", [P, KF, T], F32R, ff)
        gate = sb("gate", [P, 2, 512], F32, ff)
        hid = sb("hid", [P, 2, 512], F32, ff)
        cgate = sb("cgate", [P, 2, 2, T], F32, ff)
        cval = sb("cval", [P, 2, 2, T], F32, ff)
        row_ffn = sb("row_ffn", [P, D], F32, ff)
        ff.close()

        m2 = ExitStack()
        y2_hi = sb("y2_hi", [P, 16, T], F32R, m2)
        y2_lo = sb("y2_lo", [P, 16, T], F32R, m2)
        z_s = sb("z_s", [P, NHALF, D], F32, m2)
        dt_s = sb("dt_s", [P, 12, NHALF, 16], F32, m2)
        rows16 = sb("rows16", [P, 3, 16], F32, m2)
        w_dt = sb("w_dt", [P, KD, 16], F32, m2)
        w_dt_hi = sb("w_dt_hi", [P, KD, 16], F32R, m2)
        w_dt_lo = sb("w_dt_lo", [P, KD, 16], F32R, m2)
        ga = ExitStack()
        u_rm = sb("u_rm", [P, NHALF, D], F32, ga)
        vg_rm = sb("vg_rm", [P, NHALF, D], F32, ga)
        ws_raw = sb("ws_raw", [P, 8, P], F32, ga)
        ws_t = sb("ws_t", [P, 8, P], F32, ga)
        gm_s = sb("gm_s", [P, 48], F32, ga)
        row_ln_g = sb("row_ln_g", [P, D], F32, ga)
        row_ln_b = sb("row_ln_b", [P, D], F32, ga)
        ga.close()
        gb = ExitStack()
        xbc_f = sb("xbc_f", [P, 12, T], F32, gb)
        xs_rm = sb("xs_rm", [P, NHALF, D], F32, gb)
        xd_rm = sb("xd_rm", [P, D], F32, gb)
        bm_rm = sb("bm_rm", [P, 256], F32, gb)
        cb = sb("cb", [P, 2, P], F32, gb)
        att = sb("att", [P, 8, P], F32, gb)
        sstate = sb("sstate", [P, 2, 512], F32, gb)
        y_rm = xbc_f[:, 0:8, :].rearrange("p (h a) n -> p h (a n)", h=2)
        gb.close()
        m2.close()
        pl = ExitStack()
        p_hi = sb("p_hi", [P, 2, T], F32R, pl)
        p_lo = sb("p_lo", [P, 2, T], F32R, pl)
        p_rm = sb("p_rm", [P, NHALF, 256], F32, pl)
        gsig = sb("gsig", [P, NHALF, D], F32, pl)
        row_ple = sb("row_ple", [P, D], F32, pl)
        row_fin = sb("row_fin", [P, D], F32, pl)
        pl.close()
        pb = [ctx.enter_context(nc.psum_tensor(f"bank{i}", [P, 512], F32)) for i in range(8)]

        def bank(i, a):
            return pb[i][:, :].rearrange("p (a n) -> p a n", a=a)

        def col(name, k, n=1):
            return cols[:, COL[name] + k:COL[name] + k + n]

        def at(n, it, per):
            return n if it is None else it * per + n

        def in_fours(eng, units, body):
            turns = units // 4 if units >= 8 else 0
            if turns:
                with eng.Fori(0, turns) as it:
                    for j in range(4):
                        body(j, it)
            for j in range(4 * turns, units):
                body(j, None)

        raw_landed = [sem(f"raw_landed{i}") for i in range(RING)]
        hi_split, lo_split, unit_used = sem("hi_split"), sem("lo_split"), sem("unit_used")
        S = sem
        block = ctx.enter_context(nc.Block())

        @block.sync
        def _(sp):
            for m in range(NHALF):
                sp.dma_start(resid[:, m, :], x_d[m * P:(m + 1) * P, :]).then_inc(S("x_landed"), 16)

            def load(u, it, nk, src):
                if u >= RING:
                    sp.wait_ge(lo_split, at(u - RING + 1, it, 4))
                dst = w_raw[:, u % RING, :].rearrange("p (k n) -> p k n", k=nk)
                sp.dma_start(dst, src).then_inc(raw_landed[u % RING], 16)

            def columns(name, w, first, nk, width):
                def body(j, it):
                    per_block = KD // nk
                    c = at(first + (j // per_block) * width, it, 4 // per_block * width)
                    k = j % per_block * nk
                    load(FIRST[name] + j, it, nk, w[:, k:k + nk, bass.ds(c, width)])
                in_fours(sp, dict(STREAM)[name], body)

            def pairs(name):
                def body(j, it):
                    load(FIRST[name] + j, it, 8, pair_k[name][j % 2][:, :, bass.ds(at(j // 2 * 256, it, 512), 256)])
                in_fours(sp, 2 * PAIRS, body)

            def rows(name):
                def body(j, it):
                    src = row_w[name][bass.ds(at(j * 256, it, 1024), 256), :]
                    load(FIRST[name] + j, it, 2, src.rearrange("(k p) n -> p k n", p=P))
                in_fours(sp, dict(STREAM)[name], body)

            columns("rw", w_in_k, 0, 8, 256)
            columns("ret", w_in_k, RW_COLS, 4, 512)
            columns("gates", w_in_k, RW_COLS + RET_COLS, 8, 256)
            for j in range(2):
                load(FIRST["branch_rw"] + j, None, 4, brw_k[:, :, j * 512:(j + 1) * 512])
            columns("branch_ret", bret_k, 0, 8, 256)
            rows("mix_out")
            pairs("conv_up")
            rows("conv_down")
            pairs("ffn1_up")
            rows("ffn1_down")
            columns("uvz", w_in2_k, 0, 4, 512)
            columns("xbc", w_in2_k, 3 * D, 8, 256)
            rows("mix2_out")
            pairs("ffn2_up")
            rows("ffn2_down")
            rows("ple_gate")
            rows("ple_proj")
            for m in range(NHALF):
                sp.wait_ge(S("out_ready"), m + 1)
                sp.dma_start(out[m * P:(m + 1) * P, :], xn[:, m, :]).then_inc(S("out_stored"), 16)
            sp.wait_ge(S("out_stored"), 32)

        @block.gpsimd
        def _(pool):
            kc = io["consts"].rearrange("p (k n) -> p k n", n=P)

            def row_of(name):
                return io["rows"][ROWS.index(name):ROWS.index(name) + 1, :].to_broadcast([P, D])

            pool.dma_start(cols[:, :], io["cols"]).then_inc(S("consts_landed"), 16)
            pool.dma_start(consts[:, :, :], kc[:, 0:5, :]).then_inc(S("consts_landed"), 16)
            pool.wait_ge(S("norm_tr"), 4)
            pool.dma_start(lvl[:, :, :], kc[:, KIND["level"]:KIND["level"] + LEVELS, :]).then_inc(S("rw_small"), 16)
            pool.dma_start(small_w[0:64, 0, :], io["rw_w2"]).then_inc(S("rw_small"), 16)
            pool.dma_start(small_w[64:128, 0, :], io["rw_a2"]).then_inc(S("rw_small"), 16)
            pool.dma_start(small_w[:, 1, :], io["rw_g2"]).then_inc(S("rw_small"), 16)
            pool.wait_ge(S("rw_small"), 64)
            for m in range(NHALF):
                pool.wait_ge(S("rw_lt"), 2 * m + 2)
                for j in range(LEVELS):
                    n = m * LEVELS + j
                    if n:
                        pool.wait_ge(S("rw_t"), n)
                    if j == 1:
                        pool.wait_ge(S("rw_xd"), n)
                    pool.tensor_tensor(lm[:, :, :], lt, lvl[:, j:j + 1, :].to_broadcast([P, 8, P]),
                                       ALU.mult).then_inc(S("rw_lm"), 1)
            pool.wait_ge(S("rw_done"), 1)
            pool.dma_start(decay[:, :, :], kc[:, KIND["decay"]:KIND["small"] + 1, :]).then_inc(S("ret_small"), 16)
            pool.dma_start(posi[:, :], pos_d).then_inc(S("ret_small"), 16)
            pool.wait_ge(S("ret_done"), 2)
            pool.dma_start(row_mix[:, :], row_of("mix_post")).then_inc(S("mix_row"), 16)
            for m in range(NHALF):
                pool.dma_start(resid[:, m, :], x_d[m * P:(m + 1) * P, :]).then_inc(S("mix_row"), 16)

            def split_hidden(name):
                def body(j, it):
                    p, b = at(j, it, 4), j % 2
                    pool.wait_ge(S(name + "_hid"), at(j + 3, it, 4))
                    pool.tensor_copy(h_hi[:, bass.ds(at(2 * j, it, 8), 2), :],
                                     hid[:, b, :].rearrange("p (i n) -> p i n", i=2)).then_inc(S(name + "_hhi"), 1)
                    pool.wait_ge(S(name + "_hhi"), at(j + 1, it, 4))
                    pool.tensor_tensor(h_lo[:, bass.ds(at(2 * j, it, 8), 2), :],
                                       hid[:, b, :].rearrange("p (i n) -> p i n", i=2),
                                       h_hi[:, bass.ds(at(2 * j, it, 8), 2), :],
                                       ALU.subtract).then_inc(S(name + "_hlo"), 1)
                pool.sem_inc(S(name + "_hlo"), 2)
                in_fours(pool, PAIRS, body)

            pool.wait_ge(S("norm_tr"), 8)
            pool.dma_start(row_ffn[:, :], row_of("ffn_post")).then_inc(S("ffn_row"), 16)
            split_hidden("conv")
            split_hidden("ffn1")
            pool.wait_ge(S("norm_tr"), 16)
            pool.dma_start(w_dt[:, :, :], w_in2_k[:, :, DT_COL:DT_COL + 16]).then_inc(S("dt_small"), 16)
            for i, name in enumerate(("dt_bias_2", "a_log_2", "d_skip_2")):
                pool.dma_start(rows16[:, i, :], io[name].to_broadcast([P, 16])).then_inc(S("dt_small"), 16)
            pool.dma_start(ws_raw[:, :, :], io["gm_w_s_2"].rearrange("h t s -> t h s")).then_inc(S("gm_small"), 16)
            pool.dma_start(row_ln_g[:, :], row_of("gm_ln_g")).then_inc(S("gm_small"), 16)
            pool.dma_start(row_ln_b[:, :], row_of("gm_ln_b")).then_inc(S("gm_small"), 16)
            split_hidden("ffn2")
            pool.wait_ge(S("norm_tr"), 24)
            for m in range(NHALF):
                pool.dma_start(p_rm[:, m, :], io["p_2"][m * P:(m + 1) * P, :]).then_inc(S("ple_small"), 16)
            pool.dma_start(row_ple[:, :], row_of("ple_b")).then_inc(S("ple_small"), 16)
            pool.dma_start(row_fin[:, :], row_of("final")).then_inc(S("ple_small"), 16)

        @block.tensor
        def _(pe):
            def mm3_t(dst, w_slot, c0, x_h, x_l, first, last):
                for n, (w, x) in enumerate(((w_hi, x_h), (w_hi, x_l), (w_lo, x_h))):
                    mm = pe.matmul(dst, w[:, w_slot, c0:c0 + P], x, start=(first and n == 0), stop=(last and n == 2))
                return mm

            def unit_t(u, it, nk, x_h, x_l, banks):
                pe.wait_ge(lo_split, at(u + 1, it, 4))
                width = UNIT // nk
                for c in range(width // P):
                    dst = pb[banks[c // 2]][:, c % 2 * T:c % 2 * T + T]
                    for k in range(nk):
                        mm = mm3_t(dst, u % RING, k * width + c * P, x_h[:, k, :], x_l[:, k, :], k == 0, k == nk - 1)
                mm.then_inc(unit_used, 1)

            def unit_r(u, it, nk, k0, ktotal, x_h, x_l, banks):
                pe.wait_ge(lo_split, at(u + 1, it, 4))
                width = UNIT // nk
                for k in range(nk):
                    for m in range(NHALF):
                        for c in range(width // 512):
                            for n, (x, w) in enumerate(((x_h, w_hi), (x_h, w_lo), (x_l, w_hi))):
                                o = k * width + c * 512
                                mm = pe.matmul(pb[banks[m][c]][:, :], x[:, k0 + k, m * P:(m + 1) * P],
                                               w[:, u % RING, o:o + 512], start=(k0 + k == 0 and n == 0),
                                               stop=(k0 + k == ktotal - 1 and n == 2))
                mm.then_inc(unit_used, 1)

            OUT = ((4, 5), (6, 7))

            def rows(name, ktotal, x_h, x_l, banks=OUT, ready=None):
                for j in range(dict(STREAM)[name]):
                    if ready:
                        ready(j)
                    unit_r(FIRST[name] + j, None, 2, 2 * j, ktotal, x_h, x_l, banks)

            def turn_normed(src, signal):
                for b in range(4):
                    for i in range(2):
                        for m in range(NHALF):
                            k = 2 * b + i
                            tr = pe.transpose(pb[b][:, i * T + m * P:i * T + (m + 1) * P],
                                              src[:, m, k * P:(k + 1) * P], ident)
                    tr.then_inc(S(signal), 1)

            def norm(n):
                pe.wait_ge(S("norm_xn"), 2 * n + 2)
                turn_normed(xn, "norm_tr")
                pe.wait_ge(S("norm_lo"), 8 * n + 8)

            pe.wait_ge(S("consts_landed"), 32)
            norm(0)
            for j in range(7):
                if j >= 4:
                    pe.wait_ge(S("rw_cp"), j - 3)
                unit_t(FIRST["rw"] + j, None, 8, x_hi, x_lo, (j % 4,))
            pe.wait_ge(S("rw_small"), 64)
            pe.wait_ge(S("rw_lora"), 2)
            pe.wait_ge(S("rw_pm"), 14)
            for t in range(4):
                mm = pe.matmul(pb[t // 2][:, t % 2 * T:t % 2 * T + T], small_w[0:64, 0, t * P:(t + 1) * P],
                               act_w[0:64, 0, :], start=True, stop=True)
            mm.then_inc(S("rw_z"), 1)
            for t in range(4):
                mm = pe.matmul(pb[2 + t // 2][:, t % 2 * T:t % 2 * T + T], small_w[64:128, 0, t * P:(t + 1) * P],
                               pm[64:128, 12, :], start=True, stop=True)
            mm.then_inc(S("rw_z"), 1)
            for t in range(4):
                mm = pe.matmul(pb[4 + t // 2][:, t % 2 * T:t % 2 * T + T], small_w[:, 1, t * P:(t + 1) * P],
                               act_w[:, 1, :], start=True, stop=True)
            mm.then_inc(S("rw_z"), 1)

            def head_sums(src):
                for t in range(4):
                    mm = pe.matmul(pb[6 + t // 2][:, t % 2 * T:t % 2 * T + T], consts[:, KIND["heads"], :],
                                   src[:, t, :], start=True, stop=True)
                mm.then_inc(S("rw_sums"), 1)

            pe.wait_ge(S("rw_sq"), 1)
            head_sums(t2)
            pe.wait_ge(S("rw_rk"), 1)
            head_sums(t1)
            pe.wait_ge(S("rw_g"), 2)
            pe.wait_ge(S("rw_abkr"), 1)
            for i, src in enumerate((a_f, b_f, pm[:, 4:8, :], pm[:, 8:12, :])):
                if i == 3:
                    pe.wait_ge(S("rw_bonus"), 1)
                for m in range(NHALF):
                    for t in range(4):
                        tr = pe.transpose(pb[2 * i + m][:, t * P:(t + 1) * P], src[:, t, m * P:(m + 1) * P], ident)
                    tr.then_inc(S("rw_tr"), 1)
            pe.wait_ge(S("rw_rm_a"), 4)
            pe.wait_ge(S("rw_rm_d"), 4)

            def against(first_bank, left, right, m):
                for t in range(4):
                    for q in range(2):
                        f = slice(64 * q, 64 * q + 64)
                        mm = pe.matmul(pb[first_bank + q][:, t * P:(t + 1) * P], left[f, t, m * P:(m + 1) * P],
                                       right[f, t, m * P:(m + 1) * P], start=True, stop=True)
                return mm

            HEADS = [(q, t) for q in range(2) for t in range(4)]
            for m in range(NHALF):
                against(0, b_f, a_f, m).then_inc(S("rw_l"), 1)
                for j in range(LEVELS):
                    n = m * LEVELS + j
                    pe.wait_ge(S("rw_lm"), n + 1)
                    if n:
                        pe.wait_ge(S("rw_xd"), n)
                    for q, t in HEADS:
                        mm = pe.matmul(pb[2 + q][:, t * P:(t + 1) * P], lm[:, 4 * q + t, :],
                                       ident if j == 0 else xi[:, 4 * q + t, :], start=True, stop=True)
                    mm.then_inc(S("rw_t"), 1)
                    if j == 0:
                        continue
                    pe.wait_ge(S("rw_tp"), 2 * (m * (LEVELS - 1) + j))
                    if j < LEVELS - 1:
                        for q, t in HEADS:
                            pe.matmul(pb[4 + q][:, t * P:(t + 1) * P], xt[:, m, 4 * q + t, :], tp[:, 4 * q + t, :],
                                      start=True, stop=True)
                    for q, t in HEADS:
                        mm = pe.matmul(pb[6 + q][:, t * P:(t + 1) * P], tp[:, 4 * q + t, :], xt[:, m, 4 * q + t, :],
                                       start=True, stop=True)
                    mm.then_inc(S("rw_x"), 1)
            pe.wait_ge(S("rw_xd"), 2 * LEVELS)
            for m in range(NHALF):
                for q, t in HEADS:
                    h = 2 * t + q
                    mm = pe.matmul(pb[m][64 * q:64 * q + 64, t * P:(t + 1) * P], a_rm[:, m, h * 64:h * 64 + 64],
                                   xt[:, m, 4 * q + t, :], start=True, stop=True)
                mm.then_inc(S("rw_xa"), 1)
            for m in range(NHALF):
                if m:
                    pe.wait_ge(S("rw_y"), 2)
                against(2, pm[:, 4:8, :], a_f, m).then_inc(S("rw_kr"), 1)
                against(4, b_f, pm[:, 0:4, :], m).then_inc(S("rw_kr"), 1)
                against(6, pm[:, 4:8, :], pm[:, 0:4, :], m).then_inc(S("rw_kr"), 1)
                pe.wait_ge(S("rw_xac"), 2)
                pe.wait_ge(S("rw_mt"), 6 * m + 2)
                for q, t in HEADS:
                    h = 2 * t + q
                    mm = pe.matmul(pb[0][:, (4 * q + t) * 64:(4 * q + t) * 64 + 64], lm[:, 4 * q + t, :],
                                   v_rm[:, m, h * 64:h * 64 + 64], start=True, stop=True)
                mm.then_inc(S("rw_mv"), 1)
                pe.wait_ge(S("rw_mvc"), m + 1)
                for q, t in HEADS:
                    mm = pe.matmul(pb[1][:, (4 * q + t) * 64:(4 * q + t) * 64 + 64], xt[:, m, 4 * q + t, :],
                                   wv[:, m, 4 * q + t, :], start=True, stop=True)
                mm.then_inc(S("rw_xmv"), 1)
                pe.wait_ge(S("rw_w"), m + 1)
                for e in range(2):
                    c, tok = 2 * m + e, slice(64 * e, 64 * e + 64)
                    if c:
                        pe.wait_ge(S("rw_st"), c)
                        for t in range(4):
                            for q in range(2):
                                f = slice(64 * q, 64 * q + 64)
                                mm = pe.matmul(pb[2 + q][tok, t * 64:t * 64 + 64], xa[f, t, c * 64:c * 64 + 64],
                                               st[f, c, t, :], start=True, stop=True)
                        mm.then_inc(S("rw_up"), 1)
                        pe.wait_ge(S("rw_u"), c)
                    if c < 3:
                        for q, t in HEADS:
                            h = 2 * t + q
                            dst = pb[0][64 * q:64 * q + 64, t * 64:t * 64 + 64]
                            pe.matmul(dst, b_rm[tok, m, h * 64:h * 64 + 64], wv[tok, m, 4 * q + t, :],
                                      start=True, stop=False)
                            mm = pe.matmul(dst, k_rm[tok, m, h * 64:h * 64 + 64], v_rm[tok, m, h * 64:h * 64 + 64],
                                           start=False, stop=True)
                        mm.then_inc(S("rw_s"), 1)
                pe.wait_ge(S("rw_mt"), 6 * m + 6)
                for q, t in HEADS:
                    h, f = 2 * t + q, slice(64 * q, 64 * q + 64)
                    dst = pb[4 + q][:, t * 64:t * 64 + 64]
                    pe.matmul(dst, tp[:, 4 * q + t, :], v_rm[:, m, h * 64:h * 64 + 64], start=True, stop=False,
                              skip_group_check=True)
                    mm = pe.matmul(dst, xi[:, 4 * q + t, :], wv[:, m, 4 * q + t, :], start=False, stop=True,
                                   skip_group_check=True)
                    for e in range(2):
                        c = 2 * m + e
                        if c:
                            mm = pe.matmul(pb[4 + q][64 * e:64 * e + 64, t * 64:t * 64 + 64],
                                           pm[f, t, c * 64:c * 64 + 64], st[f, c, t, :], start=False, stop=True,
                                           skip_group_check=True)
                mm.then_inc(S("rw_yp"), 1)
            pe.wait_ge(S("rw_yn"), 1)
            for b in range(2):
                for i in range(2):
                    for m in range(NHALF):
                        tr = pe.transpose(pb[b][:, i * T + m * P:i * T + (m + 1) * P],
                                          yn[:, m, (2 * b + i) * P:(2 * b + i + 1) * P], ident)
                tr.then_inc(S("rw_yt"), 1)

            def blocks(name, free):
                def body(j, it):
                    b = j // 2 % 2
                    if j % 2 == 0:
                        pe.wait_ge(S(free), at(j // 2 + 1, it, 2))
                    unit_r(FIRST[name] + j, it, 4, 4 * (j % 2), 8, x_hi, x_lo, ((4 + 2 * b,), (5 + 2 * b,)))
                in_fours(pe, 12, body)

            blocks("ret", "ret_free")
            pe.wait_ge(S("rw_done"), 1)
            for i, src in enumerate((q_rm, kr_rm)):
                pe.wait_ge(S("ret_rot"), i + 1)
                for b in range(2):
                    for t in (2 * b, 2 * b + 1):
                        for m in range(NHALF):
                            tr = pe.transpose(pb[2 * i + b][:, t % 2 * T + m * P:t % 2 * T + (m + 1) * P],
                                              src[:, m, t * P:(t + 1) * P], ident)
                    tr.then_inc(S("ret_tr"), 1)
            pe.wait_ge(S("ret_free"), 8)
            pe.wait_ge(S("ret_kd"), 1)
            for q, t in HEADS:
                h = 2 * t + q
                mm = pe.matmul(pb[4][64 * q:64 * q + 64, t * P:(t + 1) * P], kr_rm[:, 0, h * 64:h * 64 + 64],
                               vr_rm[:, 0, h * P:(h + 1) * P], start=True, stop=True)
            mm.then_inc(S("ret_r"), 1)
            pe.wait_ge(S("ret_qf"), 2)
            pe.wait_ge(S("ret_kf"), 2)
            for m in range(NHALF):
                if m:
                    pe.wait_ge(S("ret_sc"), 2)
                against(0, k_f, q_f, m).then_inc(S("ret_s"), 1)
                pe.wait_ge(S("ret_sc"), 2 * m + 2)
                if m:
                    pe.wait_ge(S("ret_rc"), 1)
                    pe.wait_ge(S("ret_qd"), 1)
                for h in range(8):
                    q, t = h % 2, h // 2
                    dst = pb[(2 if m else 6) + q][:, t * P:(t + 1) * P]
                    mm = pe.matmul(dst, sco[:, q, t, :], vr_rm[:, m, h * P:(h + 1) * P], start=True, stop=not m)
                    if m:
                        mm = pe.matmul(dst, qd_f[64 * q:64 * q + 64, t, :], rstate[64 * q:64 * q + 64, t, :],
                                       start=False, stop=True)
                mm.then_inc(S("ret_o"), 1)
            pe.wait_ge(S("ret_y"), 1)
            for b, dst in enumerate((0, 1, 4, 5)):
                for i in range(2):
                    for m in range(NHALF):
                        k = 2 * b + i
                        tr = pe.transpose(pb[dst][:, i * T + m * P:i * T + (m + 1) * P],
                                          sg_rm[:, m, k * P:(k + 1) * P], ident)
                tr.then_inc(S("ret_yt"), 1)
            pe.wait_ge(S("ret_done"), 2)
            for j in range(8):
                if j >= 4:
                    pe.wait_ge(S("gates_ev"), j - 3)
                unit_t(FIRST["gates"] + j, None, 8, x_hi, x_lo, (j % 4,))
            pe.wait_ge(S("gates_ev"), 8)
            for j in range(2):
                unit_t(FIRST["branch_rw"] + j, None, 4, yrw_hi, yrw_lo, (2 * j, 2 * j + 1))
            for j in range(4):
                unit_t(FIRST["branch_ret"] + j, None, 8, yret_hi, yret_lo, (4 + j,))
            pe.wait_ge(S("merged_lo"), 4)
            rows("mix_out", 8, x_hi, x_lo)

            def up_pairs(name, taken_gate, taken_val):
                def body(j, it):
                    pe.wait_ge(S(taken_val if j % 2 else taken_gate), at(j // 2 + 1, it, 2))
                    unit_t(FIRST[name] + j, it, 8, x_hi, x_lo, (j % 4,))
                in_fours(pe, 2 * PAIRS, body)

            def hidden_ready(name):
                return lambda j: pe.wait_ge(S(name + "_hlo"), j + 3)

            norm(1)
            up_pairs("conv_up", "conv_gfree", "conv_vfree")
            rows("conv_down", KF, h_hi, h_lo, ready=hidden_ready("conv"))
            norm(2)
            up_pairs("ffn1_up", "ffn1_gfree", "ffn1_hid")
            rows("ffn1_down", KF, h_hi, h_lo, ready=hidden_ready("ffn1"))
            norm(3)
            blocks("uvz", "uvz_free")
            pe.wait_ge(S("uvz_free"), 8)
            pe.wait_ge(S("dt_wlo"), AGAIN["dt_wlo"][1] + 1)
            for m in range(NHALF):
                for k in range(KD):
                    for n, (x, w) in enumerate(((x_hi, w_dt_hi), (x_hi, w_dt_lo), (x_lo, w_dt_hi))):
                        mm = pe.matmul(pb[4][:, 16 * m:16 * m + 16], x[:, k, m * P:(m + 1) * P], w[:, k, :],
                                       start=(k == 0 and n == 0), stop=(k == KD - 1 and n == 2))
            mm.then_inc(S("dt_mm"), 1)
            pe.wait_ge(S("gm_small"), 48)
            for h in range(8):
                tr = pe.transpose(pb[h // 4][:, h % 4 * P:(h % 4 + 1) * P], ws_raw[:, h, :], ident)
            tr.then_inc(S("gm_wt"), 1)
            pe.wait_ge(S("dt_adt"), AGAIN["dt_adt"][1] + 1)
            pe.matmul(pb[5][:, 0:32], consts[:, KIND["tri"], :], dt_s[:, 6, :, :], start=True, stop=True)
            pe.matmul(pb[5][:, 32:64], consts[:, KIND["tri"], P - 1:P].to_broadcast([P, P]), dt_s[:, 6, :, :],
                      start=True, stop=True).then_inc(S("dt_cs"), 1)
            pe.wait_ge(S("gm_v"), AGAIN["gm_v"][1] + 1)
            pe.wait_ge(S("gm_wtc"), AGAIN["gm_wtc"][1] + 2)
            for m, first in enumerate((2, 0)):
                for h in range(8):
                    mm = pe.matmul(pb[first + h // 4][:, h % 4 * P:(h % 4 + 1) * P], ws_t[:, h, :],
                                   vg_rm[:, m, h * P:(h + 1) * P], start=True, stop=True)
                mm.then_inc(S("gm_mix"), 1)
            pe.wait_ge(S("gm_y"), AGAIN["gm_y"][1] + 1)
            turn_normed(u_rm, "gm_tr")
            pe.wait_ge(S("gm_lo"), 8)
            for j in range(6):
                if j >= 4:
                    pe.wait_ge(S("xbc_taps"), 6 * (j - 3))
                unit_t(FIRST["xbc"] + j, None, 8, x_hi, x_lo, (j % 4,))
            pe.wait_ge(S("xbc_silu"), 6)
            for m in range(NHALF):
                for t in range(8):
                    tr = pe.transpose(pb[2 * m + t // 4][:, t % 4 * P:(t % 4 + 1) * P], xbc_f[:, t, m * P:(m + 1) * P],
                                      ident)
                tr.then_inc(S("ssm_tr"), 1)
            pe.wait_ge(S("dt_used"), AGAIN["dt_used"][1] + 1)
            for g in range(2):
                tr = pe.transpose(pb[4][:, g * P:(g + 1) * P], xbc_f[:, 8 + g, 0:P], ident)
            tr.then_inc(S("ssm_tr"), 1)
            pe.wait_ge(S("ssm_bmc"), AGAIN["ssm_bmc"][1] + 1)
            pe.wait_ge(S("ssm_xds"), AGAIN["ssm_xds"][1] + 1)
            for g in range(2):
                mm = pe.matmul(pb[6 + g][:, :], bm_rm[:, g * P:(g + 1) * P], y_rm[:, 1, g * 512:(g + 1) * 512],
                               start=True, stop=True)
            mm.then_inc(S("ssm_state"), 1)
            for m in range(NHALF):
                pe.wait_ge(S("ssm_bmc"), AGAIN["ssm_bmc"][1] + 1 + m)
                for g in range(2):
                    mm = pe.matmul(pb[4][:, g * P:(g + 1) * P], xbc_f[:, 8 + g, m * P:(m + 1) * P],
                                   xbc_f[:, 10 + g, m * P:(m + 1) * P], start=True, stop=True)
                mm.then_inc(S("ssm_cb"), 1)
                for g in range(2):
                    n = 2 * m + g
                    pe.wait_ge(S("ssm_xrm"), 2)
                    if n:
                        pe.wait_ge(S("ssm_diff"), AGAIN["ssm_diff"][1] + 2 * n)
                    for i in range(8):
                        mm = pe.matmul(pb[i // 4][:, i % 4 * P:(i % 4 + 1) * P],
                                       dt_s[:, 6, m, 8 * g + i:8 * g + i + 1].to_broadcast([P, P]),
                                       consts[:, KIND["tri"], :], start=True, stop=True)
                    mm.then_inc(S("ssm_row"), 1)
                    if n:
                        pe.wait_ge(S("ssm_yadd"), n)
                    if m:
                        pe.wait_ge(S("ssm_stc"), AGAIN["ssm_stc"][1] + 2)
                        pe.matmul(pb[3][:, :], xbc_f[:, 10 + g, P:T], sstate[:, g, :], start=True,
                                  stop=True).then_inc(S("ssm_off"), 1)
                    pe.wait_ge(S("ssm_att"), AGAIN["ssm_att"][1] + n + 1)
                    for i in range(8):
                        mm = pe.matmul(pb[2][:, i * 64:i * 64 + 64], att[:, i, :],
                                       xd_rm[:, (8 * g + i) * 64:(8 * g + i) * 64 + 64], start=True, stop=True)
                    mm.then_inc(S("ssm_y"), 1)
            pe.wait_ge(S("ssm_yn"), 4)
            turn_normed(y_rm, "ssm_ytr")
            pe.wait_ge(S("ssm_lo"), 8)
            rows("mix2_out", 16, y2_hi, y2_lo)
            norm(4)
            up_pairs("ffn2_up", "ffn2_gfree", "ffn2_hid")
            rows("ffn2_down", KF, h_hi, h_lo, ready=hidden_ready("ffn2"))
            norm(5)
            rows("ple_gate", 8, x_hi, x_lo)
            pe.wait_ge(S("ple_small"), 64)
            for k in range(2):
                for m in range(NHALF):
                    tr = pe.transpose(pb[0][:, k * T + m * P:k * T + (m + 1) * P], p_rm[:, m, k * P:(k + 1) * P], ident)
            tr.then_inc(S("ple_tr"), 1)
            pe.wait_ge(S("ple_lo"), 1)
            rows("ple_proj", 2, p_hi, p_lo, banks=((0, 1), (2, 3)))

        @block.scalar
        def _(act):
            nxt = [0]

            def split(u, it=None):
                act.wait_ge(raw_landed[u % RING], at(16 * (u // RING + 1), it, 16))
                if u >= RING:
                    act.wait_ge(unit_used, at(u - RING + 1, it, 4))
                act.activation(w_hi[:, u % RING, :], w_raw[:, u % RING, :], ACT.Copy).then_inc(hi_split, 1)

            def ahead(u):
                while nxt[0] < min(u + RING, UNITS):
                    split(nxt[0])
                    nxt[0] += 1

            def in_step(name, body):
                def step(j, it):
                    if it is None:
                        ahead(FIRST[name] + j)
                    else:
                        split(FIRST[name] + j + RING - 1, it)
                    body(j, it)
                    if it is not None and j == 3:
                        nxt[0] = FIRST[name] + units // 4 * 4 + RING - 1
                units = dict(STREAM)[name]
                ahead(FIRST[name] - 1)
                in_fours(act, units, step)

            def run_ahead(name):
                for j in range(dict(STREAM)[name]):
                    ahead(FIRST[name] + j)

            def norm(n, ready):
                ready()
                for m in range(NHALF):
                    act.activation(xn[:, m, :], resid[:, m, :], ACT.Square,
                                   accum_out=norm_s[:, m:m + 1]).then_inc(S("norm_ss"), 1)
                act.wait_ge(S("norm_ms"), n + 1)
                act.activation(norm_s[:, 4:6], norm_s[:, 2:4], ACT.Sqrt).then_inc(S("norm_rt"), 1)

            def turned_hi(base, turned, banks, name, dst, signal):
                for k in range(8):
                    act.wait_ge(S(turned), base + k // 2 + 1)
                    act.activation(dst[:, k, :], bank(banks[k // 2], 2)[:, k % 2, :], ACT.Copy,
                                   scale=col(name, k)).then_inc(S(signal), 1)

            def norm_split(n, name):
                turned_hi(4 * n, "norm_tr", (0, 1, 2, 3), name, x_hi, "norm_hi")

            ahead(-1)
            norm(0, lambda: act.wait_ge(S("x_landed"), 32))
            act.wait_ge(S("consts_landed"), 32)
            norm_split(0, "mix_pre")

            def rw_copy(j, it):
                act.wait_ge(unit_used, FIRST["rw"] + j + 1)
                if j >= 2:
                    act.wait_ge(S("rw_pm"), 2 * (j - 1))
                act.wait_ge(S("rw_init"), 1)
                act.activation(psh[:, j % 2, :, 1:T + 1], bank(j % 4, 2), ACT.Copy).then_inc(S("rw_cp"), 1)

            in_step("rw", rw_copy)
            ahead(FIRST["ret"] - 1)
            act.wait_ge(S("rw_pm"), 14)
            act.activation(act_w[0:64, 0, :], pm[0:64, 12, :], ACT.Tanh).then_inc(S("rw_lora"), 1)
            act.activation(act_w[:, 1, :], pm[:, 13, :], ACT.Sigmoid).then_inc(S("rw_lora"), 1)
            act.wait_ge(S("rw_kk0"), 1)
            act.activation(t2, t1[:, :, :], ACT.Square).then_inc(S("rw_sq"), 1)
            act.wait_ge(S("rw_z"), 1)
            for t in range(4):
                act.activation(sw[:, t, :], bank(t // 2, 2)[:, t % 2, :], ACT.Sigmoid,
                               bias=col("w0", t)).then_inc(S("rw_sw"), 1)
            act.wait_ge(S("rw_z"), 2)
            for t in range(4):
                act.activation(a_s[:, t, :], bank(2 + t // 2, 2)[:, t % 2, :], ACT.Sigmoid,
                               bias=col("a0", t)).then_inc(S("rw_as"), 1)
            act.wait_ge(S("rw_z"), 3)
            for b in range(2):
                act.activation(g_t[:, 2 * b:2 * b + 2, :], bank(4 + b, 2), ACT.Copy).then_inc(S("rw_g"), 1)
            act.wait_ge(S("rw_norm"), 1)
            act.activation(t2, t2, ACT.Sqrt).then_inc(S("rw_normrt"), 1)
            act.wait_ge(S("rw_css"), 2)
            act.activation(e_pos[:, :, :], css[:, :, :], ACT.Exp, scale=-DECAY_SCALE).then_inc(S("rw_e"), 1)
            act.wait_ge(S("rw_e"), 1)
            act.activation(css[:, :, :], css[:, :, :], ACT.Exp, scale=DECAY_SCALE).then_inc(S("rw_e"), 1)
            act.activation(b_f[:, :, :], b_f[:, :, :], ACT.Exp, scale=-DECAY_SCALE).then_inc(S("rw_e"), 1)
            for i, dst in enumerate((a_rm, b_rm)):
                for m in range(NHALF):
                    act.wait_ge(S("rw_tr"), 2 * i + m + 1)
                    act.activation(dst[:, m, :], pb[2 * i + m][:, :], ACT.Copy).then_inc(S("rw_rm_a"), 1)
            for m in range(NHALF):
                for j in range(1, LEVELS):
                    act.wait_ge(S("rw_t"), m * LEVELS + j + 1)
                    for q in range(2):
                        act.activation(tp[:, 4 * q:4 * q + 4, :], bank(2 + q, 4), ACT.Copy).then_inc(S("rw_tp"), 1)
            for m in range(NHALF):
                act.wait_ge(S("rw_xa"), m + 1)
                act.activation(xa[:, :, m * P:(m + 1) * P], bank(m, 4), ACT.Copy).then_inc(S("rw_xac"), 1)
            for m in range(NHALF):
                act.wait_ge(S("rw_mv"), m + 1)
                act.activation(wv[:, m, :, :], bank(0, 8), ACT.Copy).then_inc(S("rw_mvc"), 1)
                act.wait_ge(S("rw_yp"), m + 1)
                for q in range(2):
                    dst = ys_v[:, m, :].rearrange("p (t q d) -> p t q d", t=4, q=2)[:, :, q, :]
                    act.activation(dst, pb[4 + q][:, 0:256].rearrange("p (t d) -> p t d", t=4),
                                   ACT.Copy).then_inc(S("rw_y"), 1)
            act.wait_ge(S("rw_gnv"), 1)
            act.activation(gn[:, 2, :], gn[:, 1, :], ACT.Sqrt).then_inc(S("rw_gnrt"), 1)
            for t in range(4):
                act.wait_ge(S("rw_yt"), t // 2 + 1)
                act.activation(ytmp[:, t, :], bank(t // 2, 2)[:, t % 2, :], ACT.Identity, bias=col("lnx_b", t),
                               scale=col("lnx_w", t)).then_inc(S("rw_ln"), 1)
            act.wait_ge(S("rw_yg"), 1)
            act.activation(yrw_hi[:, :, :], ytmp[:, :, :], ACT.Copy).then_inc(S("rw_yhi"), 1)

            ret_dst = (q_rm, kr_rm, vr_rm, vr_rm, sg_rm, sg_rm)

            def block_copy(name, used, dsts, offs, funcs):
                act.sem_inc(S(used), 2)
                ahead(FIRST[name] - 1)
                for j in range(12):
                    ahead(FIRST[name] + j)
                    if j % 2 == 0:
                        continue
                    b = j // 2
                    act.wait_ge(unit_used, FIRST[name] + j + 1)
                    for m in range(NHALF):
                        ins = act.activation(dsts[b][:, m, offs[b]:offs[b] + 512], pb[4 + 2 * (b % 2) + m][:, :], funcs[b])
                    ins.then_inc(S(used), 1)

            act.wait_ge(S("rw_done"), 1)
            act.wait_ge(S("ret_trig"), 1)
            act.activation(trig[:, 4:6, :, :], trig[:, 2:4, :, :], ACT.Sin).then_inc(S("ret_sin"), 1)
            block_copy("ret", "ret_free", ret_dst, (0, 0, 0, 512, 0, 512),
                       (ACT.Copy,) * 4 + (ACT.Silu,) * 2)
            for b in range(2):
                act.wait_ge(S("ret_tr"), b + 1)
                act.activation(q_f[:, 2 * b:2 * b + 2, :], bank(b, 2), ACT.Copy).then_inc(S("ret_qf"), 1)
            act.wait_ge(S("ret_r"), 1)
            act.activation(rstate[:, :, :], bank(4, 4), ACT.Copy).then_inc(S("ret_rc"), 1)
            act.wait_ge(S("ret_var"), 1)
            act.activation(ret_s[:, 9, :], ret_s[:, 8, :], ACT.Sqrt).then_inc(S("ret_rt"), 1)
            for b, src in enumerate((0, 1, 4, 5)):
                act.wait_ge(S("ret_yt"), b + 1)
                act.activation(yret_hi[:, 2 * b:2 * b + 2, :], bank(src, 2), ACT.Copy).then_inc(S("ret_yhi"), 1)
            act.wait_ge(S("ret_lo"), 4)

            def gate_sigmoid(j, it):
                act.wait_ge(unit_used, FIRST["gates"] + j + 1)
                dst = sig_rw if j < 4 else sig_ret
                act.activation(dst[:, 2 * (j % 4):2 * (j % 4) + 2, :], bank(j % 4, 2),
                               ACT.Sigmoid).then_inc(S("gates_ev"), 1)

            ahead(FIRST["gates"] - 1)
            for j in range(8):
                ahead(FIRST["gates"] + j)
                gate_sigmoid(j, None)
            run_ahead("branch_rw")
            for j in range(4):
                ahead(FIRST["branch_ret"] + j)
                act.wait_ge(S("merged"), j + 1)
                act.activation(x_hi[:, 2 * j:2 * j + 2, :], merged[:, 2 * j:2 * j + 2, :],
                               ACT.Copy).then_inc(S("merged_hi"), 1)
            run_ahead("mix_out")

            def post(n, last):
                act.wait_ge(unit_used, last)
                for m in range(NHALF):
                    for c in range(2):
                        act.activation(xn[:, m, c * 512:(c + 1) * 512], pb[4 + 2 * m + c][:, :], ACT.Square,
                                       accum_out=norm_s[:, 8 + 2 * m + c:9 + 2 * m + c]).then_inc(S("post_sq"), 1)
                act.wait_ge(S("post_ms"), n + 1)
                act.activation(norm_s[:, 4:6], norm_s[:, 2:4], ACT.Sqrt).then_inc(S("post_rt"), 1)

            def resid_done(n):
                return lambda: act.wait_ge(S("resid_done"), n)

            post(0, FIRST["conv_up"])
            norm(1, resid_done(1))
            norm_split(1, "ffn_pre")
            def conv_first_tap(j, it):
                side, b = j % 2, j // 2 % 2
                act.wait_ge(unit_used, at(FIRST["conv_up"] + j + 1, it, 4))
                act.wait_ge(S("conv_hid"), at(j // 2 + 1, it, 2))
                for i in range(2):
                    tile = at(22 * side + j // 2 * 2 + i, it, 4)
                    act.activation((cval if side else cgate)[:, b, i, :], bank(j % 4, 2)[:, i, :], ACT.Identity,
                                   bias=cols[:, bass.ds(tile + COL["conv1_b"], 1)],
                                   scale=cols[:, bass.ds(tile + COL["conv1_w"] + 88, 1)]).then_inc(S("conv_tap2"), 1)
                if side:
                    act.wait_ge(S("conv_vfree"), at(j // 2 + 3, it, 2))
                    act.activation(gate[:, b, :].rearrange("p (i n) -> p i n", i=2), cgate[:, b, :, :],
                                   ACT.Gelu_apprx_tanh).then_inc(S("conv_gelu"), 1)

            in_step("conv_up", conv_first_tap)
            run_ahead("conv_down")
            post(1, FIRST["ffn1_up"])

            def swiglu_gate(name):
                act.sem_inc(S(name + "_gfree"), 2)

                def body(j, it):
                    if j % 2:
                        return
                    b = j // 2 % 2
                    act.wait_ge(unit_used, at(FIRST[name + "_up"] + j + 1, it, 4))
                    act.wait_ge(S(name + "_hid"), at(j // 2 + 1, it, 2))
                    act.activation(gate[:, b, :], pb[j % 4][:, :], ACT.Silu).then_inc(S(name + "_gfree"), 1)
                in_step(name + "_up", body)
                run_ahead(name + "_down")

            norm(2, resid_done(2))
            norm_split(2, "ffn1")
            swiglu_gate("ffn1")
            norm(3, resid_done(3))
            norm_split(3, "mix2")
            act.wait_ge(S("dt_small"), 64)
            act.activation(w_dt_hi[:, :, :], w_dt[:, :, :], ACT.Copy).then_inc(S("dt_whi"), 1)
            block_copy("uvz", "uvz_free", (u_rm, u_rm, vg_rm, vg_rm, z_s, z_s), (0, 512) * 3,
                       (ACT.Gelu,) * 4 + (ACT.Silu,) * 2)
            act.wait_ge(S("dt_na"), AGAIN["dt_na"][1] + 1)
            act.activation(dt_s[:, 2, :, :], dt_s[:, 1, :, :], ACT.Exp).then_inc(S("dt_e"), 1)
            act.activation(rows16[:, 1, :], rows16[:, 1, :], ACT.Exp).then_inc(S("dt_e"), 1)
            act.wait_ge(S("gm_var"), AGAIN["gm_var"][1] + 1)
            act.activation(gm_s[:, 20:22], gm_s[:, 18:20], ACT.Sqrt).then_inc(S("gm_rt"), 1)
            for m in range(NHALF):
                act.wait_ge(S("gm_ya"), AGAIN["gm_ya"][1] + m + 1)
                act.activation(vg_rm[:, m, :], u_rm[:, m, :], ACT.Square,
                               accum_out=gm_s[:, 24 + m:25 + m]).then_inc(S("gm_sq"), 1)
            act.wait_ge(S("gm_ms"), AGAIN["gm_ms"][1] + 1)
            act.activation(gm_s[:, 28:30], gm_s[:, 26:28], ACT.Sqrt).then_inc(S("gm_rt"), 1)
            turned_hi(0, "gm_tr", (0, 1, 2, 3), "gm_out", y2_hi, "gm_hi")
            act.wait_ge(S("gm_lo"), 8)

            def xbc_first_tap(j, it):
                act.wait_ge(unit_used, FIRST["xbc"] + j + 1)
                for i in range(2):
                    k = 2 * j + i
                    act.activation(xbc_f[:, k, :], bank(j % 4, 2)[:, i, :], ACT.Identity, bias=col("conv2_b", k),
                                   scale=col("conv2_w", 36 + k)).then_inc(S("xbc_tap3"), 1)
                if j:
                    xbc_silu(j - 1)

            def xbc_silu(j):
                act.wait_ge(S("xbc_taps"), 6 * j + 6)
                act.activation(xbc_f[:, 2 * j:2 * j + 2, :], xbc_f[:, 2 * j:2 * j + 2, :],
                               ACT.Silu).then_inc(S("xbc_silu"), 1)

            in_step("xbc", xbc_first_tap)
            xbc_silu(5)
            ahead(FIRST["mix2_out"] - 1)
            act.wait_ge(S("dt_csd"), 3)
            act.activation(dt_s[:, 9:11, :, :], dt_s[:, 7:9, :, :], ACT.Exp).then_inc(S("dt_ecs"), 1)
            for m in range(NHALF):
                act.wait_ge(S("ssm_tr"), m + 1)
                for b in range(2):
                    ins = act.activation(xs_rm[:, m, b * 512:(b + 1) * 512], pb[2 * m + b][:, :], ACT.Copy)
                ins.then_inc(S("ssm_xrm"), 1)
            act.wait_ge(S("ssm_tr"), 3)
            act.activation(bm_rm[:, :], pb[4][:, 0:256], ACT.Copy).then_inc(S("ssm_bmc"), 1)
            act.wait_ge(S("ssm_state"), AGAIN["ssm_state"][1] + 1)
            for g in range(2):
                act.activation(sstate[:, g, :], pb[6 + g][:, :], ACT.Copy).then_inc(S("ssm_stc"), 1)
            for n in range(4):
                act.wait_ge(S("ssm_min"), AGAIN["ssm_min"][1] + n + 1)
                act.activation(att[:, :, :], att[:, :, :], ACT.Exp).then_inc(S("ssm_exp"), 1)
            for m in range(NHALF):
                for g in range(2):
                    act.wait_ge(S("ssm_yz"), m + 1)
                    act.activation(xs_rm[:, m, g * 512:(g + 1) * 512], y_rm[:, m, g * 512:(g + 1) * 512], ACT.Square,
                                   accum_out=dt_s[:, 11, 0, 2 * m + g:2 * m + g + 1]).then_inc(S("ssm_sq"), 1)
            act.wait_ge(S("ssm_ms"), AGAIN["ssm_ms"][1] + 1)
            act.activation(dt_s[:, 11, 0, 8:12], dt_s[:, 11, 0, 4:8], ACT.Sqrt).then_inc(S("ssm_rt"), 1)
            turned_hi(0, "ssm_ytr", (0, 1, 2, 3), "ssm", y2_hi[:, 8:16, :], "ssm_hi")
            run_ahead("mix2_out")
            norm(4, resid_done(4))
            norm_split(4, "ffn2")
            swiglu_gate("ffn2")
            norm(5, resid_done(5))
            norm_split(5, "ple")
            run_ahead("ple_gate")
            act.wait_ge(S("ple_tr"), 1)
            act.activation(p_hi[:, :, :], bank(0, 2), ACT.Copy).then_inc(S("ple_hi"), 1)
            for m in range(NHALF):
                act.wait_ge(S("ple_g"), 2 * m + 2)
                act.activation(gsig[:, m, :], gsig[:, m, :], ACT.Sigmoid).then_inc(S("ple_sig"), 1)
            norm(6, resid_done(6))

        @block.vector
        def _(dve):
            nxt, steps = [0], [0]

            def link(ins):
                steps[0] += 1
                ins.then_inc(S("dve_step"), 1)
                dve.wait_ge(S("dve_step"), steps[0])

            def split(u, it=None):
                dve.wait_ge(hi_split, at(u + 1, it, 4))
                dve.tensor_tensor(w_lo[:, u % RING, :], w_raw[:, u % RING, :], w_hi[:, u % RING, :],
                                  ALU.subtract).then_inc(lo_split, 1)

            def ahead(u):
                while nxt[0] < min(u + RING, UNITS):
                    split(nxt[0])
                    nxt[0] += 1

            def in_step(name, body):
                def step(j, it):
                    if it is None:
                        ahead(FIRST[name] + j)
                    else:
                        split(FIRST[name] + j + RING - 1, it)
                    body(j, it)
                    if it is not None and j == 3:
                        nxt[0] = FIRST[name] + units // 4 * 4 + RING - 1
                units = dict(STREAM)[name]
                ahead(FIRST[name] - 1)
                in_fours(dve, units, step)

            def run_ahead(name):
                for j in range(dict(STREAM)[name]):
                    ahead(FIRST[name] + j)

            def norm_scale(n):
                dve.wait_ge(S("norm_ss"), 2 * n + 2)
                dve.tensor_scalar(norm_s[:, 2:4], norm_s[:, 0:2], 1.0 / D, RMS_EPS, ALU.mult,
                                  ALU.add).then_inc(S("norm_ms"), 1)
                dve.wait_ge(S("norm_rt"), n + 1)
                link(dve.reciprocal(norm_s[:, 6:8], norm_s[:, 4:6]))
                for m in range(NHALF):
                    dve.tensor_scalar(xn[:, m, :], resid[:, m, :], norm_s[:, 6 + m:7 + m], None,
                                      ALU.mult).then_inc(S("norm_xn"), 1)

            def turned_lo(base, hi, banks, name, dst_hi, dst, signal):
                for k in range(8):
                    dve.wait_ge(S(hi), base + k // 2 * 2 + 2)
                    dve.scalar_tensor_tensor(out=dst[:, k, :], in0=bank(banks[k // 2], 2)[:, k % 2, :],
                                             scalar=col(name, k), in1=dst_hi[:, k, :], op0=ALU.mult,
                                             op1=ALU.subtract).then_inc(S(signal), 1)

            def norm(n, name):
                norm_scale(n)
                turned_lo(8 * n, "norm_hi", (0, 1, 2, 3), name, x_hi, x_lo, "norm_lo")

            dve.wait_ge(S("consts_landed"), 32)
            ahead(-1)
            norm(0, "mix_pre")
            dve.wait_ge(S("norm_tr"), 4)
            link(dve.memset(cmask[:, :, :], 1.0))
            dve.memset(cmask[:, :, :].rearrange("p a (c n) -> p (a c) n", n=CHUNK)[:, :, 0:1], 0.0)
            dve.memset(psh_flat[:, :].rearrange("p (g n) -> p g n", g=4)[:, :, 0:1], 0.0).then_inc(S("rw_init"), 1)

            def shift_mix(j, it):
                dve.wait_ge(S("rw_cp"), j + 1)
                now, before = psh[:, j % 2, :, 1:T + 1], psh[:, j % 2, :, 0:T]
                if j >= 1:
                    dve.wait_ge(S("rw_pm"), 2 * j)
                link(dve.tensor_tensor(act_w[:, :, :], before, now, ALU.subtract))
                for i in range(2):
                    dve.scalar_tensor_tensor(out=pm[:, 2 * j + i, :], in0=act_w[:, i, :], scalar=col("mu", 2 * j + i),
                                             in1=now[:, i, :], op0=ALU.mult, op1=ALU.add).then_inc(S("rw_pm"), 1)

            in_step("rw", shift_mix)
            ahead(FIRST["ret"] - 1)
            link(dve.tensor_scalar(omka[:, :], col("k_a", 0, 4), -1.0, 1.0, ALU.mult, ALU.add))
            dve.wait_ge(S("rw_pm"), 14)
            for t in range(4):
                ins = dve.tensor_scalar(t1[:, t, :], pm[:, 4 + t, :], col("k_k", t), None, ALU.mult)
            ins.then_inc(S("rw_kk0"), 1)
            dve.wait_ge(S("rw_kk0"), 1)
            dve.wait_ge(S("rw_sw"), 4)
            dve.tensor_tensor_scan(css[:, :, :].rearrange("p a n -> p (a n)"), cmask[:, :, :].rearrange("p a n -> p (a n)"),
                                   sw[:, :, :].rearrange("p a n -> p (a n)"), 0.0, ALU.mult,
                                   ALU.add).then_inc(S("rw_css"), 1)
            dve.wait_ge(S("rw_css"), 1)
            dve.tensor_tensor(b_f[:, :, :], css[:, :, :], sw[:, :, :], ALU.subtract).then_inc(S("rw_css"), 1)
            dve.wait_ge(S("rw_sums"), 1)
            for b in range(2):
                ins = dve.tensor_scalar(t2[:, 2 * b:2 * b + 2, :], bank(6 + b, 2), 1e-24, None, ALU.max)
            ins.then_inc(S("rw_norm"), 1)
            dve.wait_ge(S("rw_normrt"), 1)
            link(dve.reciprocal(kk[:, :, :], t2))
            link(dve.tensor_tensor(kk[:, :, :], kk[:, :, :], t1[:, :, :], ALU.mult))
            dve.wait_ge(S("rw_as"), 4)
            for t in range(4):
                ins = dve.tensor_scalar(t1[:, t, :], a_s[:, t, :], col("k_a", t), omka[:, t:t + 1], ALU.mult, ALU.add)
            link(ins)
            link(dve.tensor_tensor(pm[:, 4:8, :], pm[:, 4:8, :], t1[:, :, :], ALU.mult))
            for t in range(4):
                ins = dve.scalar_tensor_tensor(out=t1[:, t, :], in0=pm[:, t, :], scalar=col("r_k", t),
                                               in1=pm[:, 4 + t, :], op0=ALU.mult, op1=ALU.mult)
            ins.then_inc(S("rw_rk"), 1)
            dve.wait_ge(S("rw_e"), 3)
            dve.tensor_copy(pc[:, :, :], e_pos[:, :, :].rearrange("p a (c n) -> p a c n", n=CHUNK)[:, :, :, CHUNK - 1])
            link(dve.tensor_tensor(a_f[:, :, :], kk[:, :, :], b_f[:, :, :], ALU.mult))
            link(dve.tensor_tensor(b_f[:, :, :], kk[:, :, :], a_s[:, :, :], ALU.mult))
            dve.tensor_tensor(b_f[:, :, :], b_f[:, :, :], css[:, :, :], ALU.mult)
            dve.wait_ge(S("rw_rk"), 1)
            dve.tensor_tensor(pm[:, 4:8, :], pm[:, 4:8, :], css[:, :, :], ALU.mult)
            dve.tensor_tensor(pm[:, 0:4, :], pm[:, 0:4, :], e_pos[:, :, :], ALU.mult).then_inc(S("rw_abkr"), 1)
            dve.wait_ge(S("rw_sums"), 2)
            for b in range(2):
                ins = dve.tensor_tensor(bonus[:, 2 * b:2 * b + 2, :], bank(6 + b, 2), pm[:, 8 + 2 * b:10 + 2 * b, :],
                                        ALU.mult)
            ins.then_inc(S("rw_bonus"), 1)
            dve.wait_ge(S("rw_abkr"), 1)
            for i, dst in enumerate((k_rm, v_rm)):
                for m in range(NHALF):
                    dve.wait_ge(S("rw_tr"), 5 + 2 * i + m)
                    dve.tensor_copy(dst[:, m, :], pb[4 + 2 * i + m][:, :]).then_inc(S("rw_rm_d"), 1)
            strict = consts[:, KIND["strict"]:KIND["strict"] + 1, :].to_broadcast([P, 4, P])
            incl = consts[:, KIND["incl"]:KIND["incl"] + 1, :].to_broadcast([P, 4, P])
            eye = consts[:, 0:1, :].to_broadcast([P, 4, P])
            for m in range(NHALF):
                dve.wait_ge(S("rw_l"), m + 1)
                if m:
                    dve.wait_ge(S("rw_lm"), LEVELS)
                for q in range(2):
                    dve.tensor_tensor(lt[:, 4 * q:4 * q + 4, :], bank(q, 4), strict, ALU.mult).then_inc(S("rw_lt"), 1)
                for j in range(LEVELS):
                    n = m * LEVELS + j
                    if j == 0:
                        dve.wait_ge(S("rw_t"), n + 1)
                        for q in range(2):
                            g = slice(4 * q, 4 * q + 4)
                            dve.tensor_tensor(xi[:, g, :], bank(2 + q, 4), eye, ALU.add)
                            ins = dve.tensor_tensor(xt[:, m, g, :], lm[:, g, :], eye, ALU.add)
                    else:
                        dve.wait_ge(S("rw_xd"), n)
                        dve.wait_ge(S("rw_x"), m * (LEVELS - 1) + j)
                        for q in range(2):
                            g = slice(4 * q, 4 * q + 4)
                            if j < LEVELS - 1:
                                dve.tensor_tensor(xi[:, g, :], bank(4 + q, 4), xi[:, g, :], ALU.add)
                            ins = dve.tensor_tensor(xt[:, m, g, :], bank(6 + q, 4), xt[:, m, g, :], ALU.add)
                    ins.then_inc(S("rw_xd"), 1)
            for m in range(NHALF):
                if m:
                    dve.wait_ge(S("rw_yp"), 1)
                for i, (dst, first, mask) in enumerate(((lm, 2, strict), (xi, 4, incl), (tp, 6, incl))):
                    dve.wait_ge(S("rw_kr"), 3 * m + i + 1)
                    for q in range(2):
                        dve.tensor_tensor(dst[:, 4 * q:4 * q + 4, :], bank(first + q, 4), mask,
                                          ALU.mult).then_inc(S("rw_mt"), 1)
                dve.wait_ge(S("rw_xmv"), m + 1)
                dve.tensor_scalar(wv[:, m, :, :], bank(1, 8), -1.0, None, ALU.mult).then_inc(S("rw_w"), 1)
                dve.wait_ge(S("rw_w"), m + 1)
                for e in range(2):
                    c, tok = 2 * m + e, slice(64 * e, 64 * e + 64)
                    if c:
                        dve.wait_ge(S("rw_up"), c)
                        for q in range(2):
                            u = wv[tok, m, 4 * q:4 * q + 4, :]
                            ins = dve.tensor_tensor(u, u, pb[2 + q][tok, 0:256].rearrange("p (t d) -> p t d", t=4),
                                                    ALU.subtract)
                        ins.then_inc(S("rw_u"), 1)
                    if c < 3:
                        dve.wait_ge(S("rw_s"), c + 1)
                        src = pb[0][:, 0:256].rearrange("p (t d) -> p t d", t=4)
                        if c:
                            link(dve.tensor_tensor(stmp[:, :, :], src, st[:, c, :, :], ALU.add))
                            src = stmp[:, :, :]
                        dve.tensor_tensor(st[:, c + 1, :, :], src,
                                          pc[:, :, c:c + 1].to_broadcast([P, 4, 64]), ALU.mult).then_inc(S("rw_st"), 1)
                        dve.wait_ge(S("rw_st"), c + 1)
            dve.wait_ge(S("rw_y"), 4)
            y16 = ys_v.rearrange("p m (h d) -> p (m h) d", h=8)
            n16 = yn[:, :, :].rearrange("p m (h d) -> p (m h) d", h=8)
            q16 = yq[:, :, :].rearrange("p m (h d) -> p (m h) d", h=8)

            def over_head(k):
                return gn[:, k, :].unsqueeze(2).to_broadcast([P, 16, 64])

            link(dve.tensor_reduce(gn[:, 0, :], y16, AX_X, ALU.add))
            link(dve.tensor_scalar(gn[:, 0, :], gn[:, 0, :], 1.0 / 64, None, ALU.mult))
            link(dve.tensor_tensor(n16, y16, over_head(0), ALU.subtract))
            link(dve.tensor_tensor(q16, n16, n16, ALU.mult))
            link(dve.tensor_reduce(gn[:, 1, :], q16, AX_X, ALU.add))
            dve.tensor_scalar(gn[:, 1, :], gn[:, 1, :], 1.0 / 64, 64e-5, ALU.mult, ALU.add).then_inc(S("rw_gnv"), 1)
            dve.wait_ge(S("rw_gnrt"), 1)
            link(dve.reciprocal(gn[:, 3, :], gn[:, 2, :]))
            dve.tensor_tensor(n16, n16, over_head(3), ALU.mult).then_inc(S("rw_yn"), 1)
            dve.wait_ge(S("rw_ln"), 4)
            link(dve.tensor_tensor(ytmp[:, :, :], ytmp[:, :, :], bonus[:, :, :], ALU.add))
            dve.tensor_tensor(ytmp[:, :, :], ytmp[:, :, :], g_t[:, :, :], ALU.mult).then_inc(S("rw_yg"), 1)
            dve.wait_ge(S("rw_yhi"), 1)
            dve.tensor_tensor(yrw_lo[:, :, :], ytmp[:, :, :], yrw_hi[:, :, :], ALU.subtract).then_inc(S("rw_done"), 1)

            dve.wait_ge(S("rw_done"), 1)
            dve.wait_ge(S("ret_small"), 32)
            link(dve.tensor_copy(posf[:, 0, :], posi[:, :]))
            inv = decay[:, 12, SMALL_INV:SMALL_INV + 32]
            for m in range(NHALF):
                ins = dve.tensor_scalar(trig[:, 0, m, :], inv, posf[:, 0, m:m + 1], None, ALU.mult)
            link(ins)
            for i, quarter in enumerate((0.0, 0.25)):
                turns, rest = trig[:, 1, :, :], trig[:, 2 + i, :, :]
                link(dve.tensor_scalar(turns, trig[:, 0, :, :], 1.0 / TWO_PI, quarter, ALU.mult, ALU.add))
                link(dve.tensor_scalar(turns, turns, ROUND, None, ALU.add))
                link(dve.tensor_scalar(turns, turns, ROUND, None, ALU.subtract))
                src = trig[:, 0, :, :]
                for part in (PI_A, PI_B, PI_C):
                    link(dve.scalar_tensor_tensor(out=rest, in0=turns, scalar=-part, in1=src, op0=ALU.mult, op1=ALU.add))
                    src = rest
                link(dve.tensor_scalar(rest, rest, quarter * TWO_PI, PI_F32, ALU.add, ALU.min))
                ins = dve.tensor_scalar(rest, rest, -PI_F32, None, ALU.max)
                link(ins)
            dve.tensor_scalar(trig[:, 0, :, :], trig[:, 0, :, :], 0.0, None, ALU.add).then_inc(S("ret_trig"), 1)

            run_ahead_at = ahead

            def rotate(src, i):
                z = src[:, :, :].rearrange("p m (h two d) -> p m h two d", two=2, d=32)
                z1, z2 = z[:, :, :, 0, :], z[:, :, :, 1, :]
                sin, cos = (trig[:, k, :, :].unsqueeze(2).to_broadcast([P, NHALF, 8, 32]) for k in (4, 5))
                a, b, c = (rot[:, k, :, :].rearrange("p m (h d) -> p m h d", h=8) for k in range(3))
                dve.tensor_tensor(a, z1, cos, ALU.mult)
                dve.tensor_tensor(b, z2, sin, ALU.mult)
                link(dve.tensor_tensor(c, z1, sin, ALU.mult))
                link(dve.tensor_tensor(z1, a, b, ALU.subtract))
                link(dve.tensor_tensor(a, z2, cos, ALU.mult))
                dve.tensor_tensor(z2, c, a, ALU.add).then_inc(S("ret_rot"), 1)

            ahead(FIRST["ret"] - 1)
            for j in range(12):
                ahead(FIRST["ret"] + j)
                if j == 3:
                    dve.wait_ge(S("ret_sin"), 1)
                    dve.wait_ge(S("ret_free"), 3)
                    rotate(q_rm, 0)
                if j == 5:
                    dve.wait_ge(S("ret_free"), 4)
                    dve.wait_ge(S("ret_rot"), 1)
                    rotate(kr_rm, 1)
            for b in range(2):
                dve.wait_ge(S("ret_tr"), 3 + b)
                dve.tensor_copy(k_f[:, 2 * b:2 * b + 2, :], bank(2 + b, 2)).then_inc(S("ret_kf"), 1)
            kd = decay[:, 12, SMALL_KDECAY:SMALL_KDECAY + 8].unsqueeze(2).to_broadcast([P, 8, 64])
            k0 = kr_rm[:, 0, :].rearrange("p (h d) -> p h d", h=8)
            dve.wait_ge(S("ret_rot"), 2)
            dve.tensor_tensor(k0, k0, kd, ALU.mult).then_inc(S("ret_kd"), 1)
            dve.wait_ge(S("ret_qf"), 2)
            dve.tensor_tensor(qd_f[:, :, :], q_f[:, :, P:T], decay[:, 8:12, :], ALU.mult).then_inc(S("ret_qd"), 1)
            for m in range(NHALF):
                dve.wait_ge(S("ret_s"), m + 1)
                if m:
                    dve.wait_ge(S("ret_o"), 1)
                masks = decay[:, 0:8, :].rearrange("p (t q) n -> p q t n", q=2)
                for q in range(2):
                    dve.tensor_tensor(sco[:, q, :, :], bank(q, 4), masks[:, q, :, :], ALU.mult).then_inc(S("ret_sc"), 1)
            stats = ret_s[:, 0:6, :].rearrange("p a b -> p (a b)").rearrange("p (h s) -> p h s", s=6)
            mv = ret_s[:, 6:8, :].rearrange("p a b -> p (a b)").rearrange("p (h s) -> p h s", s=2)

            def o_of(m, h):
                return pb[(2 if m else 6) + h % 2][:, h // 2 * P:(h // 2 + 1) * P]

            for m in range(NHALF):
                dve.wait_ge(S("ret_o"), m + 1)
                for h in range(8):
                    ins = dve.bn_stats(stats[:, 8 * m + h, :], o_of(m, h))
            link(ins)
            for n in range(16):
                ins = dve.bn_aggr(mv[:, n, :], stats[:, n, :])
            link(ins)
            dve.tensor_scalar(ret_s[:, 8, :], mv[:, :, 1], 1e-5, None, ALU.add).then_inc(S("ret_var"), 1)
            dve.wait_ge(S("ret_rt"), 1)
            link(dve.reciprocal(ret_s[:, 10, :], ret_s[:, 9, :]))
            sg16 = sg_rm[:, :, :].rearrange("p m (h e) -> p (m h) e", h=8)
            dve.wait_ge(S("ret_free"), 8)
            link(dve.tensor_tensor(sg16, sg16, ret_s[:, 10, :].unsqueeze(2).to_broadcast([P, 16, P]), ALU.mult))
            for m in range(NHALF):
                for h in range(8):
                    n = 8 * m + h
                    ins = dve.scalar_tensor_tensor(out=sg16[:, n, :], in0=o_of(m, h), scalar=mv[:, n, 0:1],
                                                   in1=sg16[:, n, :], op0=ALU.subtract, op1=ALU.mult)
            ins.then_inc(S("ret_y"), 1)
            for b, src in enumerate((0, 1, 4, 5)):
                dve.wait_ge(S("ret_yhi"), b + 1)
                dve.tensor_tensor(yret_lo[:, 2 * b:2 * b + 2, :], bank(src, 2), yret_hi[:, 2 * b:2 * b + 2, :],
                                  ALU.subtract).then_inc(S("ret_lo"), 1)
            dve.wait_ge(S("ret_lo"), 4)
            dve.sem_inc(S("ret_done"), 2)
            for j in range(8):
                ahead(FIRST["gates"] + j)
            for j in range(2):
                ahead(FIRST["branch_rw"] + j)
                dve.wait_ge(unit_used, FIRST["branch_rw"] + j + 1)
                dve.wait_ge(S("gates_ev"), 8)
                for b in range(2):
                    k = 4 * j + 2 * b
                    dve.tensor_tensor(merged[:, k:k + 2, :], bank(2 * j + b, 2), sig_rw[:, k:k + 2, :],
                                      ALU.mult).then_inc(S("merged_rw"), 1)
            for j in range(4):
                ahead(FIRST["branch_ret"] + j)
                dve.wait_ge(unit_used, FIRST["branch_ret"] + j + 1)
                k = slice(2 * j, 2 * j + 2)
                if j >= 2:
                    dve.wait_ge(S("merged"), j - 1)
                dve.wait_ge(S("merged_rw"), 4)
                link(dve.tensor_tensor(mtmp[:, j % 2, :, :], bank(4 + j, 2), sig_ret[:, k, :], ALU.mult))
                dve.tensor_tensor(merged[:, k, :], merged[:, k, :], mtmp[:, j % 2, :, :], ALU.add).then_inc(S("merged"), 1)
                dve.wait_ge(S("merged_hi"), j + 1)
                dve.tensor_tensor(x_lo[:, k, :], merged[:, k, :], x_hi[:, k, :], ALU.subtract).then_inc(S("merged_lo"), 1)
            run_ahead("mix_out")

            def post(n, row, row_sem, landed):
                dve.wait_ge(S("post_sq"), 4 * n + 4)
                four = norm_s[:, 8:12].rearrange("p (m c) -> p m c", c=2)
                link(dve.tensor_tensor(norm_s[:, 0:2], four[:, :, 0], four[:, :, 1], ALU.add))
                dve.tensor_scalar(norm_s[:, 2:4], norm_s[:, 0:2], 1.0 / D, RMS_EPS, ALU.mult,
                                  ALU.add).then_inc(S("post_ms"), 1)
                dve.wait_ge(S("post_rt"), n + 1)
                link(dve.reciprocal(norm_s[:, 6:8], norm_s[:, 4:6]))
                dve.wait_ge(S(row_sem), landed)
                for m in range(NHALF):
                    for c in range(2):
                        cc = slice(c * 512, (c + 1) * 512)
                        ins = dve.scalar_tensor_tensor(out=xn[:, m, cc], in0=pb[4 + 2 * m + c][:, :],
                                                       scalar=norm_s[:, 6 + m:7 + m], in1=row[:, cc],
                                                       op0=ALU.mult, op1=ALU.mult)
                    link(ins)
                    ins = dve.tensor_tensor(resid[:, m, :], resid[:, m, :], xn[:, m, :], ALU.add)
                ins.then_inc(S("resid_done"), 1)

            post(0, row_mix, "mix_row", 48)
            norm(1, "ffn_pre")
            dve.sem_inc(S("conv_gfree"), 2)
            dve.sem_inc(S("conv_vfree"), 2)
            dve.sem_inc(S("conv_hid"), 2)

            def conv_taps(j, it):
                side, b = j % 2, j // 2 % 2
                c = cval if side else cgate
                free = S("conv_vfree" if side else "conv_gfree")
                dve.wait_ge(S("conv_tap2"), at(2 * j + 2, it, 8))
                for i in range(2):
                    tile = at(22 * side + j // 2 * 2 + i + COL["conv1_w"] + 44, it, 4)
                    dve.scalar_tensor_tensor(out=c[:, b, i, 1:T], in0=bank(j % 4, 2)[:, i, 0:T - 1],
                                             scalar=cols[:, bass.ds(tile, 1)], in1=c[:, b, i, 1:T],
                                             op0=ALU.mult, op1=ALU.add).then_inc(S("conv_tap1"), 1)
                for i in range(2):
                    tile = at(22 * side + j // 2 * 2 + i + COL["conv1_w"], it, 4)
                    dve.wait_ge(S("conv_tap1"), at(2 * j + i + 1, it, 8))
                    ins = dve.scalar_tensor_tensor(out=c[:, b, i, 2:T], in0=bank(j % 4, 2)[:, i, 0:T - 2],
                                                   scalar=cols[:, bass.ds(tile, 1)], in1=c[:, b, i, 2:T],
                                                   op0=ALU.mult, op1=ALU.add)
                ins.then_inc(free, 1)
                if side:
                    dve.wait_ge(S("conv_gelu"), at(j // 2 + 1, it, 2))
                    dve.wait_ge(S("conv_vfree"), at(j // 2 + 3, it, 2))
                    dve.wait_ge(S("conv_hlo"), at(j // 2 + 1, it, 2))
                    dve.tensor_tensor(hid[:, b, :], gate[:, b, :], cval[:, b, :, :].rearrange("p i n -> p (i n)"),
                                      ALU.mult).then_inc(S("conv_hid"), 1)

            in_step("conv_up", conv_taps)
            run_ahead("conv_down")
            post(1, row_ffn, "ffn_row", 16)

            def swiglu_mul(name):
                dve.sem_inc(S(name + "_hid"), 2)

                def body(j, it):
                    if j % 2 == 0:
                        return
                    b = j // 2 % 2
                    dve.wait_ge(unit_used, at(FIRST[name + "_up"] + j + 1, it, 4))
                    dve.wait_ge(S(name + "_gfree"), at(j // 2 + 3, it, 2))
                    dve.wait_ge(S(name + "_hlo"), at(j // 2 + 1, it, 2))
                    dve.tensor_tensor(hid[:, b, :], pb[j % 4][:, :], gate[:, b, :],
                                      ALU.mult).then_inc(S(name + "_hid"), 1)
                in_step(name + "_up", body)
                run_ahead(name + "_down")

            def add_out(scale, last):
                dve.wait_ge(unit_used, last)
                for m in range(NHALF):
                    for c in range(2):
                        r = resid[:, m, c * 512:(c + 1) * 512]
                        ins = dve.scalar_tensor_tensor(out=r, in0=pb[4 + 2 * m + c][:, :], scalar=scale, in1=r,
                                                       op0=ALU.mult, op1=ALU.add)
                ins.then_inc(S("resid_done"), 1)

            norm(2, "ffn1")
            swiglu_mul("ffn1")
            add_out(0.5, FIRST["uvz"])
            norm(3, "mix2")
            dve.wait_ge(S("dt_whi"), AGAIN["dt_whi"][1] + 1)
            dve.tensor_tensor(w_dt_lo[:, :, :], w_dt[:, :, :], w_dt_hi[:, :, :], ALU.subtract).then_inc(S("dt_wlo"), 1)
            run_ahead("uvz")
            ahead(FIRST["xbc"] - 1)
            dve.wait_ge(S("uvz_free"), 6)
            gstat = gm_s[:, 32:44]
            for m in range(NHALF):
                for c in range(2):
                    link(dve.bn_stats(gstat[:, 6 * c:6 * c + 6], vg_rm[:, m, c * 512:(c + 1) * 512]))
                link(dve.bn_aggr(gm_s[:, 2 * m:2 * m + 2], gstat))
            mvar = gm_s[:, 0:4].rearrange("p (m s) -> p m s", s=2)
            dve.tensor_scalar(gm_s[:, 18:20], mvar[:, :, 1], RMS_EPS, None, ALU.add).then_inc(S("gm_var"), 1)
            dve.wait_ge(S("dt_mm"), AGAIN["dt_mm"][1] + 1)
            bias = rows16[:, 0:1, :].to_broadcast([P, NHALF, 16])
            link(dve.tensor_tensor(dt_s[:, 0, :, :], pb[4][:, 0:32].rearrange("p (m h) -> p m h", m=2), bias, ALU.add))
            dve.scalar_tensor_tensor(out=dt_s[:, 1, :, :], in0=dt_s[:, 0, :, :], scalar=-1.0, in1=dt_s[:, 0, :, :],
                                     op0=ALU.mult, op1=ALU.min).then_inc(S("dt_na"), 1)
            dve.wait_ge(S("dt_e"), AGAIN["dt_e"][1] + 2)
            e, s_, z_, acc = (dt_s[:, k, :, :] for k in (2, 3, 4, 5))
            link(dve.tensor_scalar(s_, e, 2.0, None, ALU.add))
            link(dve.reciprocal(z_, s_))
            link(dve.tensor_tensor(s_, e, z_, ALU.mult))
            link(dve.tensor_tensor(z_, s_, s_, ALU.mult))
            link(dve.tensor_scalar(acc, z_, 2.0 / 17, 2.0 / 15, ALU.mult, ALU.add))
            for k in (13, 11, 9, 7, 5, 3, 1):
                link(dve.tensor_tensor(acc, acc, z_, ALU.mult))
                link(dve.tensor_scalar(acc, acc, 2.0 / k, None, ALU.add))
            link(dve.tensor_tensor(acc, acc, s_, ALU.mult))
            link(dve.scalar_tensor_tensor(out=acc, in0=dt_s[:, 0, :, :], scalar=0.0, in1=acc, op0=ALU.max, op1=ALU.add))
            dve.scalar_tensor_tensor(out=dt_s[:, 6, :, :], in0=acc, scalar=-1.0,
                                     in1=rows16[:, 1:2, :].to_broadcast([P, NHALF, 16]),
                                     op0=ALU.mult, op1=ALU.mult).then_inc(S("dt_adt"), 1)
            tri4 = consts[:, KIND["tri"]:KIND["tri"] + 1, :].to_broadcast([P, 4, P])
            dve.wait_ge(S("gm_wt"), AGAIN["gm_wt"][1] + 1)
            for b in range(2):
                dve.tensor_tensor(ws_t[:, 4 * b:4 * b + 4, :], bank(b, 4), tri4, ALU.mult).then_inc(S("gm_wtc"), 1)
            dve.wait_ge(S("gm_rt"), AGAIN["gm_rt"][1] + 1)
            link(dve.reciprocal(gm_s[:, 22:24], gm_s[:, 20:22]))
            dve.wait_ge(S("gm_small"), 48)
            for m in range(NHALF):
                ins = dve.tensor_scalar(vg_rm[:, m, :], vg_rm[:, m, :], gm_s[:, 2 * m:2 * m + 1], gm_s[:, 22 + m:23 + m],
                                        ALU.subtract, ALU.mult)
            link(ins)
            for m in range(NHALF):
                ins = dve.tensor_tensor(vg_rm[:, m, :], vg_rm[:, m, :], row_ln_g[:, :], ALU.mult)
            link(ins)
            for m in range(NHALF):
                ins = dve.tensor_tensor(vg_rm[:, m, :], vg_rm[:, m, :], row_ln_b[:, :], ALU.add)
            ins.then_inc(S("gm_v"), 1)
            for m, first in enumerate((2, 0)):
                dve.wait_ge(S("gm_mix"), AGAIN["gm_mix"][1] + m + 1)
                for h in range(8):
                    u = u_rm[:, m, h * P:(h + 1) * P]
                    ins = dve.scalar_tensor_tensor(out=u, in0=pb[first + h // 4][:, h % 4 * P:(h % 4 + 1) * P],
                                                   scalar=col("gm_b", h), in1=u, op0=ALU.add, op1=ALU.mult)
                ins.then_inc(S("gm_ya"), 1)
            dve.wait_ge(S("dt_cs"), AGAIN["dt_cs"][1] + 1)
            cs_p = pb[5][:, 0:32].rearrange("p (m h) -> p m h", m=2)
            dve.tensor_copy(dt_s[:, 7, :, :], cs_p).then_inc(S("dt_csd"), 1)
            dve.wait_ge(S("dt_csd"), 1)
            dve.tensor_tensor(dt_s[:, 8, :, :], pb[5][:, 32:64].rearrange("p (m h) -> p m h", m=2), dt_s[:, 7, :, :],
                              ALU.subtract).then_inc(S("dt_csd"), 1)
            dve.wait_ge(S("dt_csd"), 2)
            dve.sem_inc(S("dt_csd"), 1)
            dve.sem_inc(S("dt_used"), 1)
            dve.wait_ge(S("gm_sq"), AGAIN["gm_sq"][1] + 2)
            dve.tensor_scalar(gm_s[:, 26:28], gm_s[:, 24:26], 1.0 / D, RMS_EPS, ALU.mult, ALU.add).then_inc(S("gm_ms"), 1)
            dve.wait_ge(S("gm_rt"), AGAIN["gm_rt"][1] + 2)
            link(dve.reciprocal(gm_s[:, 30:32], gm_s[:, 28:30]))
            for m in range(NHALF):
                ins = dve.tensor_scalar(u_rm[:, m, :], u_rm[:, m, :], gm_s[:, 30 + m:31 + m], None, ALU.mult)
            ins.then_inc(S("gm_y"), 1)
            turned_lo(0, "gm_hi", (0, 1, 2, 3), "gm_out", y2_hi, y2_lo, "gm_lo")

            def xbc_taps(j, it):
                for i in range(2):
                    k = 2 * j + i
                    dve.wait_ge(S("xbc_tap3"), 2 * j + 2)
                    for back in (1, 2, 3):
                        n = 6 * j + 3 * i + back
                        if back > 1:
                            dve.wait_ge(S("xbc_taps"), n - 1)
                        dve.scalar_tensor_tensor(out=xbc_f[:, k, back:T], in0=bank(j % 4, 2)[:, i, 0:T - back],
                                                 scalar=col("conv2_w", 12 * (3 - back) + k), in1=xbc_f[:, k, back:T],
                                                 op0=ALU.mult, op1=ALU.add).then_inc(S("xbc_taps"), 1)

            in_step("xbc", xbc_taps)
            ahead(FIRST["mix2_out"] - 1)

            def heads16(ap):
                return ap.unsqueeze(2).to_broadcast([P, 16, 64])

            def by_head(ap):
                return ap.rearrange("p (h d) -> p h d", d=64)

            dve.wait_ge(S("ssm_xrm"), 1)
            link(dve.tensor_tensor(by_head(xd_rm[:, :]), by_head(xs_rm[:, 0, :]), heads16(dt_s[:, 5, 0, :]), ALU.mult))
            dve.wait_ge(S("dt_ecs"), AGAIN["dt_ecs"][1] + 1)
            dve.wait_ge(S("ssm_xrm"), 2)
            dve.wait_ge(S("ssm_tr"), 2)
            dve.tensor_tensor(by_head(y_rm[:, 1, :]), by_head(xd_rm[:, :]), heads16(dt_s[:, 10, 0, :]),
                              ALU.mult).then_inc(S("ssm_xds"), 1)
            tri2 = consts[:, KIND["tri"]:KIND["tri"] + 1, :].to_broadcast([P, 2, P])
            for m in range(NHALF):
                if m:
                    dve.wait_ge(S("ssm_y"), 2)
                    link(dve.tensor_tensor(by_head(xd_rm[:, :]), by_head(xs_rm[:, 1, :]), heads16(dt_s[:, 5, 1, :]),
                                           ALU.mult))
                dve.wait_ge(S("ssm_cb"), AGAIN["ssm_cb"][1] + m + 1)
                dve.tensor_tensor(cb[:, :, :], pb[4][:, 0:256].rearrange("p (g n) -> p g n", g=2), tri2,
                                  ALU.mult).then_inc(S("ssm_bmc"), 1)
                dve.wait_ge(S("ssm_bmc"), AGAIN["ssm_bmc"][1] + m + 2)
                if m:
                    dve.wait_ge(S("ssm_state"), AGAIN["ssm_state"][1] + 1)
                link(dve.tensor_tensor(by_head(y_rm[:, m, :]), by_head(xs_rm[:, m, :]), heads16(rows16[:, 2, :]),
                                       ALU.mult))
                for g in range(2):
                    n = 2 * m + g
                    dve.wait_ge(S("ssm_row"), AGAIN["ssm_row"][1] + n + 1)
                    if n:
                        dve.wait_ge(S("ssm_y"), n)
                    for b in range(2):
                        h = 8 * g + 4 * b
                        dve.tensor_tensor(att[:, 4 * b:4 * b + 4, :], bank(b, 4),
                                          dt_s[:, 7, m, h:h + 4].unsqueeze(2).to_broadcast([P, 4, P]),
                                          ALU.subtract).then_inc(S("ssm_diff"), 1)
                    dve.wait_ge(S("ssm_diff"), AGAIN["ssm_diff"][1] + 2 * n + 2)
                    dve.tensor_scalar(att[:, :, :], att[:, :, :], 0.0, None, ALU.min).then_inc(S("ssm_min"), 1)
                    dve.wait_ge(S("ssm_exp"), AGAIN["ssm_exp"][1] + n + 1)
                    dve.tensor_tensor(att[:, :, :], att[:, :, :], cb[:, g:g + 1, :].to_broadcast([P, 8, P]),
                                      ALU.mult).then_inc(S("ssm_att"), 1)
                    y = y_rm[:, m, g * 512:(g + 1) * 512]
                    dve.wait_ge(S("ssm_y"), n + 1)
                    ins = dve.tensor_tensor(y, y, pb[2][:, :], ALU.add)
                    if m:
                        link(ins)
                        dve.wait_ge(S("ssm_off"), AGAIN["ssm_off"][1] + g + 1)
                        tmp = xs_rm[:, 0, g * 512:(g + 1) * 512]
                        link(dve.tensor_tensor(by_head(tmp), by_head(pb[3][:, :]),
                                               dt_s[:, 9, 1, 8 * g:8 * g + 8].unsqueeze(2).to_broadcast([P, 8, 64]),
                                               ALU.mult))
                        ins = dve.tensor_tensor(y, y, tmp, ALU.add)
                    ins.then_inc(S("ssm_yadd"), 1)
            for m in range(NHALF):
                dve.wait_ge(S("ssm_yadd"), 4)
                dve.tensor_tensor(y_rm[:, m, :], y_rm[:, m, :], z_s[:, m, :], ALU.mult).then_inc(S("ssm_yz"), 1)
            dve.wait_ge(S("ssm_sq"), AGAIN["ssm_sq"][1] + 4)
            dve.tensor_scalar(dt_s[:, 11, 0, 4:8], dt_s[:, 11, 0, 0:4], 1.0 / 512, RMS_EPS, ALU.mult,
                              ALU.add).then_inc(S("ssm_ms"), 1)
            dve.wait_ge(S("ssm_rt"), AGAIN["ssm_rt"][1] + 1)
            link(dve.reciprocal(dt_s[:, 11, 0, 12:16], dt_s[:, 11, 0, 8:12]))
            for n in range(4):
                y = y_rm[:, n // 2, n % 2 * 512:(n % 2 + 1) * 512]
                dve.tensor_scalar(y, y, dt_s[:, 11, 0, 12 + n:13 + n], None, ALU.mult).then_inc(S("ssm_yn"), 1)
            turned_lo(0, "ssm_hi", (0, 1, 2, 3), "ssm", y2_hi[:, 8:16, :], y2_lo[:, 8:16, :], "ssm_lo")
            run_ahead("mix2_out")
            add_out(1.0, FIRST["ffn2_up"])
            norm(4, "ffn2")
            swiglu_mul("ffn2")
            add_out(0.5, FIRST["ple_gate"])
            norm(5, "ple")
            run_ahead("ple_gate")
            dve.wait_ge(S("ple_hi"), 1)
            dve.tensor_tensor(p_lo[:, :, :], bank(0, 2), p_hi[:, :, :], ALU.subtract).then_inc(S("ple_lo"), 1)
            dve.wait_ge(S("ple_small"), 64)
            dve.wait_ge(unit_used, FIRST["ple_proj"])
            for m in range(NHALF):
                for c in range(2):
                    cc = slice(c * 512, (c + 1) * 512)
                    dve.tensor_tensor(gsig[:, m, cc], pb[4 + 2 * m + c][:, :], row_ple[:, cc],
                                      ALU.add).then_inc(S("ple_g"), 1)
            dve.wait_ge(unit_used, UNITS)
            for m in range(NHALF):
                dve.wait_ge(S("ple_sig"), m + 1)
                for c in range(2):
                    cc = slice(c * 512, (c + 1) * 512)
                    ins = dve.tensor_tensor(gsig[:, m, cc], pb[2 * m + c][:, :], gsig[:, m, cc], ALU.mult)
                link(ins)
                ins = dve.tensor_tensor(resid[:, m, :], resid[:, m, :], gsig[:, m, :], ALU.add)
            ins.then_inc(S("resid_done"), 1)
            norm_scale(6)
            for m in range(NHALF):
                dve.wait_ge(S("norm_xn"), 2 * 6 + m + 1)
                dve.tensor_tensor(xn[:, m, :], xn[:, m, :], row_fin[:, :], ALU.mult).then_inc(S("out_ready"), 1)


_NAMES = ("x", "positions", "w_in", "rw_w2", "rw_a2", "rw_g2", "w_branch_rw", "w_branch_ret", "w_out", "ffn_w_up",
          "ffn_w_down", "p_2", "ffn1_w_gate_2", "ffn1_w_up_2", "ffn1_w_down_2", "w_in_2", "gm_w_s_2", "dt_bias_2",
          "a_log_2", "d_skip_2", "w_out_2", "ffn2_w_gate_2", "ffn2_w_up_2", "ffn2_w_down_2", "ple_w_gate_2",
          "ple_w_proj_2")


def laid_out(inputs):
    arrays = {}
    for name in _NAMES:
        a = np.asarray(inputs[name])
        keep = 1 if name in ("dt_bias_2", "a_log_2", "d_skip_2") else None
        if name == "positions":
            a = np.ascontiguousarray(a.reshape(NHALF, P).T)
        elif name == "p_2":
            a = a.reshape(T, -1)
        elif keep is None:
            a = a.reshape(a.shape[1:])
        arrays[name] = np.ascontiguousarray(a)
    packed = {
        "mix_pre": "norm_mix_pre", "ffn_pre": "norm_ffn_pre", "mu": "rw_mu", "w0": "rw_w0", "a0": "rw_a0",
        "k_k": "rw_k_k", "k_a": "rw_k_a", "r_k": "rw_r_k", "lnx_w": "rw_lnx_w", "lnx_b": "rw_lnx_b",
        "conv1_w": "ffn_conv_w", "conv1_b": "ffn_conv_b", "ffn1": "ffn1_norm_2", "mix2": "mix_norm_2",
        "gm_b": "gm_b_s_2", "gm_out": "gm_out_norm_2", "conv2_w": "conv_w_2", "conv2_b": "conv_b_2",
        "ssm": "ssm_norm_2", "ffn2": "ffn2_norm_2", "ple": "ple_norm_2",
    }
    arrays["cols"] = np.ascontiguousarray(
        np.concatenate([np.asarray(inputs[packed[name]]).reshape(n, P) for name, n in COLS]).T)
    rows = {"mix_post": "norm_mix_post", "ffn_post": "norm_ffn_post", "gm_ln_g": "gm_ln_g_2", "gm_ln_b": "gm_ln_b_2",
            "ple_b": "ple_b_gate_2", "final": "final_norm_2"}
    arrays["rows"] = np.ascontiguousarray(np.stack([np.asarray(inputs[rows[name]]).reshape(D) for name in ROWS]))
    arrays["consts"] = shape_constants()
    return arrays


def kernel(**inputs):
    import concourse.bacc as bacc
    from concourse.bass_utils import run_bass_kernel_spmd

    arrays = laid_out(inputs)
    nc = bacc.Bacc("TRN2", target_bir_lowering=False, num_devices=1)
    io = {name: nc.dram_tensor(f"in_{name}", a.shape, mybir.dt.from_np(a.dtype), kind="ExternalInput").ap()
          for name, a in arrays.items()}
    out = nc.dram_tensor("out", (T, D), F32, kind="ExternalOutput").ap()
    two_layers(nc, io, out)
    r = run_bass_kernel_spmd(nc, [{f"in_{n}": a for n, a in arrays.items()}], core_ids=[0])
    return r.results[0]["out"].reshape(1, T, D)
```

```python
from contextlib import ExitStack

import numpy as np

import concourse.bass as bass
from concourse import mybir

F32 = mybir.dt.float32
F32R = mybir.dt.float32r
I32 = mybir.dt.int32
ACT = mybir.ActivationFunctionType
ALU = mybir.AluOpType
AX_X = mybir.AxisListType.X

P = 128
T = 256
D = 1024
KD = D // P
NHALF = T // P
RW = 512
RW_COLS = 1792
RET_COLS = 3072
FF = 2816
KF = FF // P
PAIRS = FF // 256
XBC = 1536
DT_COL = 4608
RING = 4
UNIT = 2048

STREAM = (
    ("rw", RW_COLS // 256), ("ret", RET_COLS // 256), ("gates", 2 * D // 256),
    ("branch_rw", 2), ("branch_ret", 4), ("mix_out", 4), ("conv_up", 2 * PAIRS), ("conv_down", PAIRS),
    ("ffn1_up", 2 * PAIRS), ("ffn1_down", PAIRS), ("uvz", 12), ("xbc", XBC // 256), ("mix2_out", 8),
    ("ffn2_up", 2 * PAIRS), ("ffn2_down", PAIRS), ("ple_gate", 4), ("ple_proj", 1),
)
FIRST = {}
UNITS = 0
for _name, _n in STREAM:
    FIRST[_name] = UNITS
    UNITS += _n

AGAIN = {
    "dt_adt": ("rw_sq", 1), "dt_cs": ("rw_kk0", 1), "dt_e": ("rw_norm", 1), "dt_ecs": ("rw_normrt", 1),
    "dt_mm": ("rw_rk", 1), "dt_na": ("rw_abkr", 1), "dt_used": ("rw_bonus", 1), "dt_whi": ("rw_gnv", 1),
    "dt_wlo": ("rw_gnrt", 1), "gm_mix": ("rw_yn", 1), "gm_ms": ("rw_yg", 1), "gm_rt": ("rw_yhi", 1),
    "gm_sq": ("rw_init", 1), "gm_v": ("rw_lora", 2), "gm_var": ("rw_css", 2), "gm_wt": ("rw_sums", 2),
    "gm_wtc": ("rw_z", 3), "gm_y": ("rw_e", 3), "gm_ya": ("rw_sw", 4), "ssm_att": ("rw_as", 4),
    "ssm_bmc": ("rw_g", 2), "ssm_cb": ("rw_v", 2), "ssm_diff": ("rw_fd", 14), "ssm_exp": ("rw_tr", 2),
    "ssm_min": ("rw_l", 1), "ssm_ms": ("rw_lt", 2), "ssm_off": ("rw_xa", 1), "ssm_row": ("rw_xac", 2),
    "ssm_rt": ("rw_f", 7), "ssm_sq": ("rw_up", 3), "ssm_state": ("rw_xmv", 1), "ssm_stc": ("rw_w", 2),
    "ssm_xds": ("rw_yt", 2),
}

WEAVE = {
    "low_rank": 4, "norms": 5, "keys": 8, "l": 2,
    "t0": 1, "t1": 1, "x1": 1, "t2": 1, "x2": 1, "t3": 1, "x3": 1, "t4": 1, "x4": 1, "t5": 1, "x5": 1,
    "xa": 1, "xmv": 1, "s0": 1, "u1": 1, "s1": 1, "u2": 1, "s2": 1, "u3": 1,
    "y": 8, "y2": 8, "yt": 8, "qk": 4, "sc0": 3, "o0": 3, "o1": 4, "stats": 4, "rest0": 4, "rest1": 4,
}
BEFORE = {}
_n = 0
for _step in WEAVE:
    BEFORE[_step] = _n
    _n += WEAVE[_step]
assert _n == 4 * (12 + 8 + 2), _n

COLS = (
    ("mix_pre", 8), ("ffn_pre", 8), ("mu", 14), ("w0", 4), ("a0", 4), ("k_k", 4), ("k_a", 4),
    ("r_k", 4), ("lnx_w", 4), ("lnx_b", 4), ("conv1_w", 3 * 44), ("conv1_b", 44), ("ffn1", 8),
    ("mix2", 8), ("gm_b", 8), ("gm_out", 8), ("conv2_w", 4 * 12), ("conv2_b", 12), ("ssm", 8),
    ("ffn2", 8), ("ple", 8),
)
COL = {}
NCOL = 0
for _name, _n in COLS:
    COL[_name] = NCOL
    NCOL += _n

ROWS = ("mix_post", "ffn_post", "gm_ln_g", "gm_ln_b", "ple_b", "final")

CHUNK = 64
LEVELS = 6
KIND = {"ident": 0, "causal": 1, "eye": 2, "tri": 3, "heads": 4, "level": 5, "decay": 5 + LEVELS // 2,
        "qdecay": 5 + LEVELS // 2 + 8, "small": 5 + LEVELS // 2 + 8 + 4}
NKIND = KIND["small"] + 1
SMALL_KDECAY, SMALL_INV = 0, 8
DECAY_SCALE = float(np.exp(-0.5))
RMS_EPS = 1e-6
TWO_PI = 2 * np.pi
PI_A = 6.28125
PI_B = 2029 / 2 ** 20
PI_C = float(TWO_PI - PI_A - PI_B)
ROUND = 12582912.0
PI_F32 = 3.1415925


TURN = RING


def shape_constants():
    s = np.arange(P)[:, None]
    t = np.arange(P)[None, :]
    sc, tc = s % CHUNK, np.arange(CHUNK)[None, :]
    out = np.zeros((P, NKIND, P), np.float32)
    out[:, KIND["ident"]] = np.eye(P)
    out[:, KIND["causal"], :CHUNK] = sc < tc
    out[:, KIND["causal"], CHUNK:] = sc <= tc
    out[:, KIND["eye"], :CHUNK] = sc == tc
    out[:, KIND["tri"]] = s <= t
    out[:, KIND["heads"]] = (s // CHUNK) == (t // CHUNK)
    for j in range(LEVELS):
        b = 1 << j
        out[:, KIND["level"] + j // 2, j % 2 * CHUNK:(j % 2 + 1) * CHUNK] = -1.0 * (
            (sc // (2 * b) == tc // (2 * b)) & (sc // b % 2 == 0) & (tc // b % 2 == 1))
    head = np.arange(8, dtype=np.float32)
    log_gamma = np.log1p(-np.exp2(np.float32(-5.0) - head)).astype(np.float32)
    rel = (t - s).astype(np.float32)
    for h in range(8):
        out[:, KIND["decay"] + h] = np.where(rel >= 0, np.exp(np.maximum(rel, 0) * log_gamma[h]), 0) * 0.125
    for tile in range(4):
        for q in range(2):
            row = np.exp((np.arange(P, dtype=np.float32) + 1) * log_gamma[2 * tile + q])
            out[64 * q:64 * q + 64, KIND["qdecay"] + tile] = row[None, :]
    small = out[:, KIND["small"]]
    small[:, SMALL_KDECAY:SMALL_KDECAY + 8] = np.exp((P - 1 - s).astype(np.float32) * log_gamma[None, :]) * 0.125
    small[:, SMALL_INV:SMALL_INV + 32] = np.float32(10000.0) ** (-np.arange(32, dtype=np.float32) / 32)
    return out.reshape(P, NKIND * P)


def two_layers(nc, io, out):
    x_d = io["x"]
    w_in, w_in_2 = io["w_in"], io["w_in_2"]
    w_up = io["ffn_w_up"]

    def k_rows(w):
        return w.rearrange("(k p) n -> p k n", p=P)

    w_in_k, w_in2_k, w_up_k = k_rows(w_in), k_rows(w_in_2), k_rows(w_up)
    brw_k, bret_k = k_rows(io["w_branch_rw"]), k_rows(io["w_branch_ret"])
    pair_k = {
        "conv_up": (w_up_k, w_up_k[:, :, FF:]),
        "ffn1_up": (k_rows(io["ffn1_w_gate_2"]), k_rows(io["ffn1_w_up_2"])),
        "ffn2_up": (k_rows(io["ffn2_w_gate_2"]), k_rows(io["ffn2_w_up_2"])),
    }
    row_w = {
        "mix_out": io["w_out"], "conv_down": io["ffn_w_down"], "ffn1_down": io["ffn1_w_down_2"],
        "mix2_out": io["w_out_2"], "ffn2_down": io["ffn2_w_down_2"], "ple_gate": io["ple_w_gate_2"],
        "ple_proj": io["ple_w_proj_2"],
    }

    ctx = ExitStack()
    with ctx:
        def sb(name, shape, dt=F32, scope=ctx):
            return scope.enter_context(nc.sbuf_tensor(name, shape, dt))

        sems = {}

        def sem(name):
            name = AGAIN.get(name, (name, 0))[0]
            if name not in sems:
                sems[name] = ctx.enter_context(nc.semaphore(name))
            return sems[name]

        w_hi = sb("w_hi", [P, RING, UNIT], F32R)
        x_hi = sb("x_hi", [P, KD, T], F32R)
        x_lo = sb("x_lo", [P, KD, T], F32R)
        resid = sb("resid", [P, NHALF, D])
        cols = sb("cols", [P, NCOL])
        consts = sb("consts", [P, 5, P])
        norm_s = sb("norm_s", [P, 32])
        ident = consts[:, 0, :]
        wr = ExitStack()
        w_raw = sb("w_raw", [P, RING, UNIT], F32, wr)
        wr.close()
        w_lo = sb("w_lo", [P, RING, UNIT], F32R)

        nx = ExitStack()
        xn = sb("xn", [P, NHALF, D], F32, nx)
        nx.close()

        m1 = ExitStack()
        yrw_hi = sb("yrw_hi", [P, 4, T], F32R, m1)
        yrw_lo = sb("yrw_lo", [P, 4, T], F32R, m1)
        q_rm = sb("q_rm", [P, NHALF, RW], F32, m1)
        kr_rm = sb("kr_rm", [P, NHALF, RW], F32, m1)
        vr_rm = sb("vr_rm", [P, NHALF, D], F32, m1)
        sg_rm = sb("sg_rm", [P, NHALF, D], F32, m1)
        sig_rw = sb("sig_rw", [P, 8, T], F32, m1)
        trig = sb("trig", [P, 6, NHALF, 32], F32, m1)
        posf = sb("posf", [P, 2, NHALF], F32, m1)
        posi = sb("posi", [P, NHALF], I32, m1)
        small = sb("small", [P, P], F32, m1)
        ra = ExitStack()
        pm = sb("pm", [P, 14, T], F32, ra)
        g_t = sb("g_t", [P, 4, T], F32, ra)
        bonus = sb("bonus", [P, 4, T], F32, ra)
        a_f = sb("a_f", [P, 4, T], F32, ra)
        b_f = sb("b_f", [P, 4, T], F32, ra)
        pc = sb("pc", [P, 4, 4], F32, ra)
        lvl = sb("lvl", [P, LEVELS, CHUNK], F32, ra)
        rb = ExitStack()
        e_pos = sb("e_pos", [P, 4, T], F32, rb)
        css = sb("css", [P, 4, T], F32, rb)
        kk = sb("kk", [P, 4, T], F32, rb)
        a_s = sb("a_s", [P, 4, T], F32, rb)
        t1 = sb("t1", [P, 4, T], F32, rb)
        sw = sb("sw", [P, 4, T], F32, rb)
        psh_flat = sb("psh", [P, 4 * (T + 1)], F32, rb)
        cmask = sb("cmask", [P, 4, T], F32, rb)
        act_w = sb("act_w", [P, 2, T], F32, rb)
        omka = sb("omka", [P, 4], F32, rb)
        small_w = sb("small_w", [P, 2, RW], F32, rb)
        psh = psh_flat[:, :].rearrange("p (b i n) -> p b i n", b=2, i=2)
        t2 = psh_flat[:, 0:4 * T].rearrange("p (i n) -> p i n", i=4)
        rb.close()
        rc = ExitStack()
        a_rm = sb("a_rm", [P, NHALF, RW], F32, rc)
        b_rm = sb("b_rm", [P, NHALF, RW], F32, rc)
        k_rm = sb("k_rm", [P, NHALF, RW], F32, rc)
        lm = sb("lm", [P, 16, CHUNK], F32, rc)
        xi = sb("xi", [P, 16, CHUNK], F32, rc)
        tp = sb("tp", [P, 16, CHUNK], F32, rc)
        xa = sb("xa", [P, 4, T], F32, rc)
        v_rm = sb("v_rm", [P, NHALF, RW], F32, rc)
        gm = sb("gm", [P, 16, CHUNK], F32, rc)
        st = sb("st", [P, 4, 4, 64], F32, rc)
        stmp = sb("stmp", [P, 4, 64], F32, rc)
        xt = resid[:, 0, :].rearrange("p (g n) -> p g n", g=16)
        g1 = xn[:, 0, :].rearrange("p (g n) -> p g n", g=16)
        g2 = xn[:, 1, :].rearrange("p (g n) -> p g n", g=16)
        wv = a_rm[:, :, :].rearrange("p h (g n) -> p (h g) n", g=8)
        lt = pm[:, 8:12, :].rearrange("p a (b n) -> p (a b) n", n=CHUNK)
        ys_v = pm[:, 8:12, :].rearrange("p (m a) n -> p m (a n)", m=2)
        rc.close()
        rd = ExitStack()
        yn = sb("yn", [P, NHALF, RW], F32, rd)
        yq = sb("yq", [P, NHALF, RW], F32, rd)
        gn = sb("gn", [P, 4, 16], F32, rd)
        ytmp = sb("ytmp", [P, 4, T], F32, rd)
        rd.close()
        ra.close()
        yret_hi = sb("yret_hi", [P, 8, T], F32R, m1)
        yret_lo = sb("yret_lo", [P, 8, T], F32R, m1)
        rot = resid[:, 1, 0:768].rearrange("p (k n) -> p k n", k=3)
        q_f = resid[:, 0, :].rearrange("p (a n) -> p a n", a=4)
        k_f = resid[:, 1, :].rearrange("p (a n) -> p a n", a=4)
        qd_f = sb("qd_f", [P, 4, P], F32, m1)
        rstate = sb("rstate", [P, 4, P], F32, m1)
        decay = sb("decay", [P, 12, P], F32, m1)
        ret_s = sb("ret_s", [P, 12, 16], F32, m1)
        sco = sb("sco", [P, 2, 4, P], F32, m1)
        sig_ret = sb("sig_ret", [P, 8, T], F32, m1)
        row_mix = sb("row_mix", [P, D], F32, m1)
        merged = sb("merged", [P, 8, T], F32, m1)
        mtmp = sb("mtmp", [P, 2, 2, T], F32, m1)
        m1.close()

        ff = ExitStack()
        h_hi = sb("h_hi", [P, KF, T], F32R, ff)
        h_lo = sb("h_lo", [P, KF, T], F32R, ff)
        gate = sb("gate", [P, 2, 512], F32, ff)
        hid = sb("hid", [P, 2, 512], F32, ff)
        cgate = sb("cgate", [P, 2, 2, T], F32, ff)
        cval = sb("cval", [P, 2, 2, T], F32, ff)
        row_ffn = sb("row_ffn", [P, D], F32, ff)
        ff.close()

        m2 = ExitStack()
        y2_hi = sb("y2_hi", [P, 16, T], F32R, m2)
        y2_lo = sb("y2_lo", [P, 16, T], F32R, m2)
        z_s = sb("z_s", [P, NHALF, D], F32, m2)
        dt_s = sb("dt_s", [P, 12, NHALF, 16], F32, m2)
        rows16 = sb("rows16", [P, 3, 16], F32, m2)
        w_dt = sb("w_dt", [P, KD, 16], F32, m2)
        w_dt_hi = sb("w_dt_hi", [P, KD, 16], F32R, m2)
        w_dt_lo = sb("w_dt_lo", [P, KD, 16], F32R, m2)
        ga = ExitStack()
        u_rm = sb("u_rm", [P, NHALF, D], F32, ga)
        vg_rm = sb("vg_rm", [P, NHALF, D], F32, ga)
        ws_raw = sb("ws_raw", [P, 8, P], F32, ga)
        ws_t = sb("ws_t", [P, 8, P], F32, ga)
        gm_s = sb("gm_s", [P, 48], F32, ga)
        row_ln_g = sb("row_ln_g", [P, D], F32, ga)
        row_ln_b = sb("row_ln_b", [P, D], F32, ga)
        ga.close()
        gb = ExitStack()
        xbc_f = sb("xbc_f", [P, 12, T], F32, gb)
        xs_rm = sb("xs_rm", [P, NHALF, D], F32, gb)
        xd_rm = sb("xd_rm", [P, D], F32, gb)
        bm_rm = sb("bm_rm", [P, 256], F32, gb)
        cb = sb("cb", [P, 2, P], F32, gb)
        att = sb("att", [P, 8, P], F32, gb)
        sstate = sb("sstate", [P, 2, 512], F32, gb)
        y_rm = xbc_f[:, 0:8, :].rearrange("p (h a) n -> p h (a n)", h=2)
        gb.close()
        m2.close()
        pl = ExitStack()
        p_hi = sb("p_hi", [P, 2, T], F32R, pl)
        p_lo = sb("p_lo", [P, 2, T], F32R, pl)
        p_rm = sb("p_rm", [P, NHALF, 256], F32, pl)
        gsig = sb("gsig", [P, NHALF, D], F32, pl)
        row_ple = sb("row_ple", [P, D], F32, pl)
        row_fin = sb("row_fin", [P, D], F32, pl)
        pl.close()
        pb = [ctx.enter_context(nc.psum_tensor(f"bank{i}", [P, 512], F32)) for i in range(8)]

        def bank(i, a):
            return pb[i][:, :].rearrange("p (a n) -> p a n", a=a)

        def col(name, k, n=1):
            return cols[:, COL[name] + k:COL[name] + k + n]

        def at(n, it, per):
            return n if it is None else it * per + n

        def in_turns(eng, units, body):
            turns = units // TURN if units >= 2 * TURN else 0
            if turns:
                with eng.Fori(0, turns) as it:
                    for j in range(TURN):
                        body(j, it)
            for j in range(TURN * turns, units):
                body(j, None)

        raw_landed = [sem(f"raw_landed{i}") for i in range(RING)]
        hi_split, lo_split, unit_used = sem("hi_split"), sem("lo_split"), sem("unit_used")
        S = sem
        block = ctx.enter_context(nc.Block())

        @block.sync
        def _(sp):
            for m in range(NHALF):
                sp.dma_start(resid[:, m, :], x_d[m * P:(m + 1) * P, :]).then_inc(S(f"x_landed{m}"), 16)

            def load(u, it, nk, src):
                if u >= RING:
                    sp.wait_ge(unit_used, at(u - RING + 1, it, 4))
                dst = w_raw[:, u % RING, :].rearrange("p (k n) -> p k n", k=nk)
                sp.dma_start(dst, src).then_inc(raw_landed[u % RING], 16)

            def columns(name, w, first, nk, width):
                def body(j, it):
                    per_block = KD // nk
                    c = at(first + (j // per_block) * width, it, 4 // per_block * width)
                    k = j % per_block * nk
                    load(FIRST[name] + j, it, nk, w[:, k:k + nk, bass.ds(c, width)])
                in_turns(sp, dict(STREAM)[name], body)

            def pairs(name):
                def body(j, it):
                    load(FIRST[name] + j, it, 8, pair_k[name][j % 2][:, :, bass.ds(at(j // 2 * 256, it, 512), 256)])
                in_turns(sp, 2 * PAIRS, body)

            def rows(name):
                def body(j, it):
                    src = row_w[name][bass.ds(at(j * 256, it, 1024), 256), :]
                    load(FIRST[name] + j, it, 2, src.rearrange("(k p) n -> p k n", p=P))
                in_turns(sp, dict(STREAM)[name], body)

            columns("rw", w_in_k, 0, 8, 256)
            columns("ret", w_in_k, RW_COLS, 4, 512)
            columns("gates", w_in_k, RW_COLS + RET_COLS, 8, 256)
            for j in range(2):
                load(FIRST["branch_rw"] + j, None, 4, brw_k[:, :, j * 512:(j + 1) * 512])
            columns("branch_ret", bret_k, 0, 8, 256)
            rows("mix_out")
            pairs("conv_up")
            rows("conv_down")
            pairs("ffn1_up")
            rows("ffn1_down")
            columns("uvz", w_in2_k, 0, 4, 512)
            columns("xbc", w_in2_k, 3 * D, 8, 256)
            rows("mix2_out")
            pairs("ffn2_up")
            rows("ffn2_down")
            rows("ple_gate")
            rows("ple_proj")
            for m in range(NHALF):
                sp.wait_ge(S("out_ready"), m + 1)
                sp.dma_start(out[m * P:(m + 1) * P, :], xn[:, m, :]).then_inc(S("out_stored"), 16)
            sp.wait_ge(S("out_stored"), 32)

        @block.gpsimd
        def _(pool):
            kc = io["consts"].rearrange("p (k n) -> p k n", n=P)

            def row_of(name):
                return io["rows"][ROWS.index(name):ROWS.index(name) + 1, :].to_broadcast([P, D])

            steps = [0]

            def link(ins):
                steps[0] += 1
                ins.then_inc(S("pool_step"), 1)
                pool.wait_ge(S("pool_step"), steps[0])

            def rsqrt(dst, src, ready, count, signal):
                pool.wait_ge(S(ready), count)
                pool.tensor_tensor(dst, src, norm_s[:, 12:12 + src.shape[-1]], ALU.pow).then_inc(S(signal), 1)

            def norm(n, post=None):
                for m in range(NHALF):
                    if post is not None:
                        rsqrt(norm_s[:, 24 + m:25 + m], norm_s[:, 22 + m:23 + m], "post_ms", 2 * post + m + 1, "post_rt")
                    rsqrt(norm_s[:, 6 + m:7 + m], norm_s[:, 2 + m:3 + m], "norm_ms", 2 * n + m + 1, "norm_rt")

            link(pool.memset(norm_s[:, 12:16], -0.5))
            pool.dma_start(cols[:, :], io["cols"]).then_inc(S("consts_landed"), 16)
            pool.dma_start(consts[:, :, :], kc[:, 0:5, :]).then_inc(S("consts_landed"), 16)
            norm(0)
            pool.dma_start(small[:, :], kc[:, KIND["small"], :]).then_inc(S("trig_small"), 16)
            pool.dma_start(posi[:, :], io["positions"]).then_inc(S("trig_small"), 16)
            pool.dma_start(lvl[:, :, :], kc[:, KIND["level"]:KIND["level"] + LEVELS // 2, :].rearrange(
                "p a (b n) -> p (a b) n", n=CHUNK)).then_inc(S("rw_small"), 16)
            pool.dma_start(small_w[0:64, 0, :], io["rw_w2"]).then_inc(S("rw_small"), 16)
            pool.dma_start(small_w[64:128, 0, :], io["rw_a2"]).then_inc(S("rw_small"), 16)
            pool.dma_start(small_w[:, 1, :], io["rw_g2"]).then_inc(S("rw_small"), 16)
            pool.wait_ge(S("rw_small"), 64)
            pool.wait_ge(S("rw_lt"), 2)
            for j in range(LEVELS):
                if j:
                    pool.wait_ge(S("rw_t"), j)
                if j == 1:
                    pool.wait_ge(S("rw_xd"), 1)
                pool.tensor_tensor(lm[:, :, :], lt, lvl[:, j:j + 1, :].to_broadcast([P, 16, CHUNK]),
                                   ALU.mult).then_inc(S("rw_lm"), 1)
            pool.wait_ge(S("ret_sin"), 1)
            for i, src in enumerate((q_rm, kr_rm)):
                pool.wait_ge(S("ret_free"), i + 1)
                for m in range(NHALF):
                    z = src[:, m, :].rearrange("p (h two d) -> p h two d", two=2, d=32)
                    z1, z2 = z[:, :, 0, :], z[:, :, 1, :]
                    sin, cos = (trig[:, k, m:m + 1, :].to_broadcast([P, 8, 32]) for k in (4, 5))
                    a, b, c = (rot[:, k, :].rearrange("p (h d) -> p h d", h=8) for k in range(3))
                    pool.tensor_tensor(a, z1, cos, ALU.mult)
                    pool.tensor_tensor(b, z2, sin, ALU.mult)
                    link(pool.tensor_tensor(c, z1, sin, ALU.mult))
                    link(pool.tensor_tensor(z1, a, b, ALU.subtract))
                    link(pool.tensor_tensor(a, z2, cos, ALU.mult))
                    link(pool.tensor_tensor(z2, c, a, ALU.add))
                pool.sem_inc(S("ret_rot"), 1)
            pool.wait_ge(S("rw_done"), 1)
            pool.dma_start(decay[:, :, :], kc[:, KIND["decay"]:KIND["small"], :]).then_inc(S("ret_small"), 16)
            pool.dma_start(row_mix[:, :], row_of("mix_post")).then_inc(S("mix_row"), 16)
            pool.wait_ge(S("ret_tr"), 4)
            k0 = kr_rm[:, 0, :].rearrange("p (h d) -> p h d", h=8)
            pool.tensor_tensor(k0, k0, small[:, SMALL_KDECAY:SMALL_KDECAY + 8].unsqueeze(2).to_broadcast([P, 8, 64]),
                               ALU.mult).then_inc(S("ret_kd"), 1)
            pool.wait_ge(S("ret_done"), 2)
            for m in range(NHALF):
                pool.dma_start(resid[:, m, :], x_d[m * P:(m + 1) * P, :]).then_inc(S("mix_row"), 16)

            def split_hidden(name):
                def body(j, it):
                    p, b = at(j, it, 4), j % 2
                    pool.wait_ge(S(name + "_hid"), at(j + 3, it, 4))
                    pool.tensor_copy(h_hi[:, bass.ds(at(2 * j, it, 8), 2), :],
                                     hid[:, b, :].rearrange("p (i n) -> p i n", i=2)).then_inc(S(name + "_hhi"), 1)
                    pool.wait_ge(S(name + "_hhi"), at(j + 1, it, 4))
                    pool.tensor_tensor(h_lo[:, bass.ds(at(2 * j, it, 8), 2), :],
                                       hid[:, b, :].rearrange("p (i n) -> p i n", i=2),
                                       h_hi[:, bass.ds(at(2 * j, it, 8), 2), :],
                                       ALU.subtract).then_inc(S(name + "_hlo"), 1)
                pool.sem_inc(S(name + "_hlo"), 2)
                in_turns(pool, PAIRS, body)

            norm(1, post=0)
            pool.wait_ge(S("norm_tr"), 8)
            pool.dma_start(row_ffn[:, :], row_of("ffn_post")).then_inc(S("ffn_row"), 16)
            split_hidden("conv")
            norm(2, post=1)
            split_hidden("ffn1")
            norm(3)
            pool.wait_ge(S("norm_tr"), 16)
            pool.dma_start(w_dt[:, :, :], w_in2_k[:, :, DT_COL:DT_COL + 16]).then_inc(S("dt_small"), 16)
            for i, name in enumerate(("dt_bias_2", "a_log_2", "d_skip_2")):
                pool.dma_start(rows16[:, i, :], io[name].to_broadcast([P, 16])).then_inc(S("dt_small"), 16)
            pool.dma_start(ws_raw[:, :, :], io["gm_w_s_2"].rearrange("h t s -> t h s")).then_inc(S("gm_small"), 16)
            pool.dma_start(row_ln_g[:, :], row_of("gm_ln_g")).then_inc(S("gm_small"), 16)
            pool.dma_start(row_ln_b[:, :], row_of("gm_ln_b")).then_inc(S("gm_small"), 16)
            rsqrt(gm_s[:, 22:24], gm_s[:, 18:20], "gm_var", AGAIN["gm_var"][1] + 1, "gm_rt")
            rsqrt(gm_s[:, 30:32], gm_s[:, 26:28], "gm_ms", AGAIN["gm_ms"][1] + 1, "gm_rt")
            rsqrt(dt_s[:, 11, 0, 12:16], dt_s[:, 11, 0, 4:8], "ssm_ms", AGAIN["ssm_ms"][1] + 1, "ssm_rt")
            norm(4)
            split_hidden("ffn2")
            norm(5)
            pool.wait_ge(S("norm_tr"), 24)
            for m in range(NHALF):
                pool.dma_start(p_rm[:, m, :], io["p_2"][m * P:(m + 1) * P, :]).then_inc(S("ple_small"), 16)
            pool.dma_start(row_ple[:, :], row_of("ple_b")).then_inc(S("ple_small"), 16)
            pool.dma_start(row_fin[:, :], row_of("final")).then_inc(S("ple_small"), 16)
            norm(6)

        @block.tensor
        def _(pe):
            def mm3_t(dst, w_slot, c0, x_h, x_l, first, last):
                for n, (w, x) in enumerate(((w_hi, x_h), (w_hi, x_l), (w_lo, x_h))):
                    mm = pe.matmul(dst, w[:, w_slot, c0:c0 + P], x, start=(first and n == 0), stop=(last and n == 2))
                return mm

            def unit_t(u, it, nk, x_h, x_l, banks, part=None, ready=None):
                if not part:
                    pe.wait_ge(lo_split, at(u + 1, it, 4))
                tiles = [(c, k) for c in range(UNIT // nk // P) for k in range(nk)]
                for c, k in tiles if part is None else tiles[4 * part:4 * part + 4]:
                    if ready and c == 0:
                        ready(k)
                    mm = mm3_t(pb[banks[c // 2]][:, c % 2 * T:c % 2 * T + T], u % RING, k * (UNIT // nk) + c * P,
                               x_h[:, k, :], x_l[:, k, :], k == 0, k == nk - 1)
                if part in (None, 3):
                    mm.then_inc(unit_used, 1)

            def unit_r(u, it, nk, k0, ktotal, x_h, x_l, banks, part=None):
                if not part:
                    pe.wait_ge(lo_split, at(u + 1, it, 4))
                width = UNIT // nk
                for k in range(nk) if part is None else (part,):
                    for m in range(NHALF):
                        for c in range(width // 512):
                            for n, (x, w) in enumerate(((x_h, w_hi), (x_h, w_lo), (x_l, w_hi))):
                                o = k * width + c * 512
                                mm = pe.matmul(pb[banks[m][c]][:, :], x[:, k0 + k, m * P:(m + 1) * P],
                                               w[:, u % RING, o:o + 512], start=(k0 + k == 0 and n == 0),
                                               stop=(k0 + k == ktotal - 1 and n == 2))
                if part in (None, 3):
                    mm.then_inc(unit_used, 1)

            def fill(step):
                for n in range(BEFORE[step], BEFORE[step] + WEAVE[step]):
                    j, part = divmod(n, 4)
                    u = FIRST["ret"] + j
                    if part == 0:
                        def read(signal, count, unit):
                            assert 4 * (unit + 1) <= BEFORE[step], (step, j)
                            pe.wait_ge(S(signal), count)
                        if j < 12 and j % 2 == 0 and j >= 4:
                            read("ret_free", j // 2 - 1, j - 3)
                        elif 12 <= j < 16:
                            read("ret_free", 5 + (j - 12) // 2, 9 + (j - 12) // 2 * 2)
                        elif 16 <= j < 20:
                            read("gates_ev", j - 15, j - 4)
                        elif j >= 20:
                            pe.wait_ge(S("rw_done"), 1)
                            read("gates_ev", 6 + 2 * (j - 20), 17 + 2 * (j - 20))
                    if j < 12:
                        b = j // 2 % 2
                        unit_r(u, None, 4, 4 * (j % 2), 8, x_hi, x_lo, ((4 + 2 * b,), (5 + 2 * b,)), part)
                    elif j < 20:
                        unit_t(u, None, 8, x_hi, x_lo, (4 + j % 4,), part)
                    else:
                        unit_t(u, None, 4, yrw_hi, yrw_lo, (4 + 2 * (j - 20), 5 + 2 * (j - 20)), part)

            OUT = ((4, 5), (6, 7))

            def rows(name, ktotal, x_h, x_l, banks=OUT, ready=None):
                for j in range(dict(STREAM)[name]):
                    if ready:
                        ready(j)
                    unit_r(FIRST[name] + j, None, 2, 2 * j, ktotal, x_h, x_l, banks)

            def out_rows(name, ktotal, x_h, x_l, ready=None):
                units = dict(STREAM)[name]
                u = FIRST[name] + units - 2
                for j in range(units - 2):
                    if ready:
                        ready(j)
                    unit_r(FIRST[name] + j, None, 2, 2 * j, ktotal, x_h, x_l, OUT)
                if ready:
                    ready(units - 1)
                pe.wait_ge(lo_split, u + 2)
                for m in range(NHALF):
                    for k in range(4):
                        k_all = 2 * units - 4 + k
                        for c in range(2):
                            for n, (x, w) in enumerate(((x_h, w_hi), (x_h, w_lo), (x_l, w_hi))):
                                o = k % 2 * D + c * 512
                                mm = pe.matmul(pb[OUT[m][c]][:, :], x[:, k_all, m * P:(m + 1) * P],
                                               w[:, (u + k // 2) % RING, o:o + 512], start=False,
                                               stop=(k == 3 and n == 2))
                    if m == 0:
                        mm.then_inc(S("half_out"), 1)
                mm.then_inc(unit_used, 2)

            def turn_normed(src, signal):
                for b in range(4):
                    for i in range(2):
                        for m in range(NHALF):
                            k = 2 * b + i
                            tr = pe.transpose(pb[b][:, i * T + m * P:i * T + (m + 1) * P],
                                              src[:, m, k * P:(k + 1) * P], ident)
                    tr.then_inc(S(signal), 1)

            def norm(n):
                for m in range(NHALF):
                    pe.wait_ge(S("norm_xn"), 2 * n + m + 1)
                    for k in range(KD):
                        tr = pe.transpose(pb[k // 2][:, k % 2 * T + m * P:k % 2 * T + (m + 1) * P],
                                          xn[:, m, k * P:(k + 1) * P], ident)
                        if m and k % 2:
                            tr.then_inc(S("norm_tr"), 1)

            def normed(n):
                return lambda k: pe.wait_ge(S("norm_lo"), 8 * n + max(k + 1, 2))

            pe.wait_ge(S("consts_landed"), 32)
            norm(0)
            for j in range(7):
                if j >= 4:
                    pe.wait_ge(S("rw_cp"), j - 3)
                unit_t(FIRST["rw"] + j, None, 8, x_hi, x_lo, (j % 4,), ready=None if j else normed(0))
            pe.wait_ge(S("rw_small"), 64)
            pe.wait_ge(S("rw_lora"), 2)
            pe.wait_ge(S("rw_pm"), 14)

            def low_rank(first_bank, left, right):
                for t in range(4):
                    mm = pe.matmul(pb[first_bank + t // 2][:, t % 2 * T:t % 2 * T + T], left[:, t * P:(t + 1) * P],
                                   right, start=True, stop=True)
                mm.then_inc(S("rw_z"), 1)

            def head_sums(first_bank, src):
                for t in range(4):
                    mm = pe.matmul(pb[first_bank + t // 2][:, t % 2 * T:t % 2 * T + T], consts[:, KIND["heads"], :],
                                   src[:, t, :], start=True, stop=True)
                mm.then_inc(S("rw_sums"), 1)

            low_rank(0, small_w[0:64, 0, :], act_w[0:64, 0, :])
            pe.wait_ge(S("rw_sq"), 1)
            head_sums(2, t2)
            fill("low_rank")
            pe.wait_ge(S("rw_sw"), 4)
            low_rank(0, small_w[64:128, 0, :], pm[64:128, 12, :])
            pe.wait_ge(S("rw_norm"), 1)
            low_rank(2, small_w[:, 1, :], act_w[:, 1, :])
            fill("norms")

            def by_token(src, first_bank):
                for m in range(NHALF):
                    for t in range(4):
                        tr = pe.transpose(pb[first_bank + m][:, t * P:(t + 1) * P], src[:, t, m * P:(m + 1) * P],
                                          ident)
                return tr

            pe.wait_ge(S("rw_g"), 2)
            by_token(pm[:, 8:12, :], 2).then_inc(S("rw_tr"), 2)
            pe.wait_ge(S("rw_as"), 4)
            pe.wait_ge(S("rw_rk"), 1)
            head_sums(0, t1)
            fill("keys")

            HEADS = [(q, t) for q in range(2) for t in range(4)]
            BLOCKS = [(q, m, t) for q in range(2) for m in range(NHALF) for t in range(4)]

            def against(first_bank, left, right):
                for q, m, t in BLOCKS:
                    f = slice(64 * q, 64 * q + 64)
                    for e in range(2):
                        tok = slice(m * P + 64 * e, m * P + 64 * e + 64)
                        o = (4 * m + t) * 64
                        mm = pe.matmul(pb[first_bank + q][64 * e:64 * e + 64, o:o + 64], left[f, t, tok],
                                       right[f, t, tok], start=True, stop=True)
                return mm

            def of_block(x, q, m, t, e):
                return x[64 * e:64 * e + 64, 8 * q + 4 * m + t, :]

            def of_token(x, q, m, t, e):
                h = 2 * t + q
                return x[64 * e:64 * e + 64, m, h * 64:h * 64 + 64]

            def in_blocks(first_bank, left, right, start=True, stop=True):
                for q, m, t in BLOCKS:
                    for e in range(2):
                        o = (4 * m + t) * 64
                        mm = pe.matmul(pb[first_bank + q][64 * e:64 * e + 64, o:o + 64], left(q, m, t, e),
                                       right(q, m, t, e), start=start, stop=stop)
                return mm

            def block(x):
                return lambda *a: of_block(x, *a)

            def token(x):
                return lambda *a: of_token(x, *a)

            def eye(q, m, t, e):
                return consts[64 * e:64 * e + 64, KIND["eye"], 0:CHUNK]

            pe.wait_ge(S("rw_bonus"), 1)
            pe.wait_ge(S("rw_abkr"), 1)
            against(0, b_f, a_f).then_inc(S("rw_l"), 1)
            fill("l")
            for j in range(LEVELS):
                pe.wait_ge(S("rw_lm"), j + 1)
                if j:
                    pe.wait_ge(S("rw_xd"), j)
                in_blocks(0, block(lm), block(xi) if j else eye).then_inc(S("rw_t"), 1)
                if j == 0:
                    pe.wait_ge(S("rw_v"), 2)
                    mm = against(2, pm[:, 4:8, :], a_f)
                elif j == 1:
                    pe.wait_ge(S("rw_fd"), 2)
                    mm = by_token(pm[:, 4:8, :], 2)
                elif j == 2:
                    mm = by_token(a_f, 2)
                elif j == 3:
                    mm = by_token(b_f, 2)
                elif j == 4:
                    mm = in_blocks(2, block(gm), token(v_rm))
                else:
                    mm = against(2, b_f, pm[:, 0:4, :])
                mm.then_inc(S("rw_f"), 1)
                fill(f"t{j}")
                if j == 0:
                    continue
                pe.wait_ge(S("rw_tp"), 2 * j)
                pe.wait_ge(S("rw_fd"), 2 * j + 2)
                if j < LEVELS - 1:
                    in_blocks(2, block(xt), block(tp))
                in_blocks(0, block(tp), block(xt)).then_inc(S("rw_x"), 1)
                if j == LEVELS - 1:
                    against(2, pm[:, 4:8, :], pm[:, 0:4, :]).then_inc(S("rw_f"), 1)
                fill(f"x{j}")
            pe.wait_ge(S("rw_xd"), LEVELS)
            for q, m, t in BLOCKS:
                for e in range(2):
                    mm = pe.matmul(pb[e][64 * q:64 * q + 64, (4 * m + t) * 64:(4 * m + t) * 64 + 64],
                                   of_token(a_rm, q, m, t, e), of_block(xt, q, m, t, e), start=True, stop=True)
            mm.then_inc(S("rw_xa"), 1)
            fill("xa")
            pe.wait_ge(S("rw_fd"), 14)
            in_blocks(2, block(xt), block(gm)).then_inc(S("rw_xmv"), 1)
            fill("xmv")
            pe.wait_ge(S("rw_w"), 2)
            pe.wait_ge(S("rw_xac"), 2)
            for c in range(4):
                m, e = divmod(c, 2)
                tok = slice(64 * e, 64 * e + 64)
                if c:
                    pe.wait_ge(S("rw_st"), c)
                    for t in range(4):
                        for q in range(2):
                            f = slice(64 * q, 64 * q + 64)
                            mm = pe.matmul(pb[2 + q][tok, t * 64:t * 64 + 64], xa[f, t, c * 64:c * 64 + 64],
                                           st[f, c, t, :], start=True, stop=True)
                    mm.then_inc(S("rw_up"), 1)
                    fill(f"u{c}")
                    pe.wait_ge(S("rw_u"), c)
                if c < 3:
                    for q, t in HEADS:
                        dst = pb[0][64 * q:64 * q + 64, t * 64:t * 64 + 64]
                        pe.matmul(dst, of_token(b_rm, q, m, t, e), of_block(wv, q, m, t, e), start=True, stop=False)
                        mm = pe.matmul(dst, of_token(k_rm, q, m, t, e), of_token(v_rm, q, m, t, e), start=False,
                                       stop=True)
                    mm.then_inc(S("rw_s"), 1)
                    fill(f"s{c}")
            for q, m, t in BLOCKS:
                for e in range(2):
                    dst = pb[q][64 * e:64 * e + 64, (4 * m + t) * 64:(4 * m + t) * 64 + 64]
                    pe.matmul(dst, of_block(g2, q, m, t, e), of_token(v_rm, q, m, t, e), start=True, stop=False)
                    mm = pe.matmul(dst, of_block(g1, q, m, t, e), of_block(wv, q, m, t, e), start=False, stop=True)
            mm.then_inc(S("rw_yp"), 1)
            for q, t in HEADS:
                f = slice(64 * q, 64 * q + 64)
                for c in range(1, 4):
                    m, e = divmod(c, 2)
                    mm = pe.matmul(pb[2 + q][64 * e:64 * e + 64, (4 * m + t) * 64:(4 * m + t) * 64 + 64],
                                   pm[f, t, c * 64:c * 64 + 64], st[f, c, t, :], start=True, stop=True)
            mm.then_inc(S("rw_yp"), 1)
            fill("y")
            fill("y2")
            pe.wait_ge(S("rw_yn"), 1)
            for b in range(2):
                for i in range(2):
                    for m in range(NHALF):
                        tr = pe.transpose(pb[b][:, i * T + m * P:i * T + (m + 1) * P],
                                          yn[:, m, (2 * b + i) * P:(2 * b + i + 1) * P], ident)
                tr.then_inc(S("rw_yt"), 1)
            fill("yt")

            pe.wait_ge(S("rw_ln"), 4)
            for i, src in enumerate((q_rm, kr_rm)):
                pe.wait_ge(S("ret_rot"), i + 1)
                for b in range(2):
                    for t in (2 * b, 2 * b + 1):
                        for m in range(NHALF):
                            tr = pe.transpose(pb[2 * i + b][:, t % 2 * T + m * P:t % 2 * T + (m + 1) * P],
                                              src[:, m, t * P:(t + 1) * P], ident)
                    tr.then_inc(S("ret_tr"), 1)
            fill("qk")

            def scores(m):
                for t in range(4):
                    for q in range(2):
                        f = slice(64 * q, 64 * q + 64)
                        mm = pe.matmul(pb[2 + q][:, t * P:(t + 1) * P], k_f[f, t, m * P:(m + 1) * P],
                                       q_f[f, t, m * P:(m + 1) * P], start=True, stop=True)
                mm.then_inc(S("ret_s"), 1)

            pe.wait_ge(S("ret_qf"), 2)
            pe.wait_ge(S("ret_kf"), 2)
            scores(0)
            pe.wait_ge(S("ret_free"), 4)
            pe.wait_ge(S("ret_kd"), 1)
            for q, t in HEADS:
                h = 2 * t + q
                mm = pe.matmul(pb[0][64 * q:64 * q + 64, t * P:(t + 1) * P], kr_rm[:, 0, h * 64:h * 64 + 64],
                               vr_rm[:, 0, h * P:(h + 1) * P], start=True, stop=True)
            mm.then_inc(S("ret_r"), 1)
            fill("sc0")
            pe.wait_ge(S("ret_rc"), 1)
            for m in range(NHALF):
                pe.wait_ge(S("ret_sc"), 2 * m + 2)
                if m:
                    pe.wait_ge(S("ret_qd"), 1)
                for h in range(8):
                    q, t = h % 2, h // 2
                    dst = pb[2 * m + q][:, t * P:(t + 1) * P]
                    mm = pe.matmul(dst, sco[:, q, t, :], vr_rm[:, m, h * P:(h + 1) * P], start=True, stop=not m)
                    if m:
                        mm = pe.matmul(dst, qd_f[64 * q:64 * q + 64, t, :], rstate[64 * q:64 * q + 64, t, :],
                                       start=False, stop=True)
                mm.then_inc(S("ret_o"), 1)
                if m == 0:
                    scores(1)
                fill(f"o{m}")
            fill("stats")
            pe.wait_ge(S("ret_y"), 1)
            for b in range(4):
                for i in range(2):
                    for m in range(NHALF):
                        k = 2 * b + i
                        tr = pe.transpose(pb[b][:, i * T + m * P:i * T + (m + 1) * P],
                                          sg_rm[:, m, k * P:(k + 1) * P], ident)
                tr.then_inc(S("ret_yt"), 1)
            fill("rest0")
            fill("rest1")
            pe.wait_ge(S("ret_done"), 2)
            for j in range(4):
                unit_t(FIRST["branch_ret"] + j, None, 8, yret_hi, yret_lo, (j,))
            pe.wait_ge(S("merged_lo"), 4)
            out_rows("mix_out", 8, x_hi, x_lo)

            def blocks(name, free):
                def body(j, it):
                    b = j // 2 % 2
                    if j % 2 == 0:
                        pe.wait_ge(S(free), at(j // 2 + 1, it, 2))
                    unit_r(FIRST[name] + j, it, 4, 4 * (j % 2), 8, x_hi, x_lo, ((4 + 2 * b,), (5 + 2 * b,)))
                pe.wait_ge(S("norm_lo"), 32)
                in_turns(pe, 12, body)

            def up_pairs(name, taken_gate, taken_val, n):
                def body(j, it):
                    pe.wait_ge(S(taken_val if j % 2 else taken_gate), at(j // 2 + 1, it, 2))
                    unit_t(FIRST[name] + j, it, 8, x_hi, x_lo, (j % 4,), ready=None if j else normed(n))
                in_turns(pe, 2 * PAIRS, body)

            def hidden_ready(name):
                return lambda j: pe.wait_ge(S(name + "_hlo"), j + 3)

            norm(1)
            up_pairs("conv_up", "conv_gfree", "conv_vfree", 1)
            out_rows("conv_down", KF, h_hi, h_lo, ready=hidden_ready("conv"))
            norm(2)
            up_pairs("ffn1_up", "ffn1_gfree", "ffn1_hid", 2)
            out_rows("ffn1_down", KF, h_hi, h_lo, ready=hidden_ready("ffn1"))
            norm(3)
            blocks("uvz", "uvz_free")
            pe.wait_ge(S("uvz_free"), 8)
            pe.wait_ge(S("dt_wlo"), AGAIN["dt_wlo"][1] + 1)
            for m in range(NHALF):
                for k in range(KD):
                    for n, (x, w) in enumerate(((x_hi, w_dt_hi), (x_hi, w_dt_lo), (x_lo, w_dt_hi))):
                        mm = pe.matmul(pb[4][:, 16 * m:16 * m + 16], x[:, k, m * P:(m + 1) * P], w[:, k, :],
                                       start=(k == 0 and n == 0), stop=(k == KD - 1 and n == 2))
            mm.then_inc(S("dt_mm"), 1)
            pe.wait_ge(S("gm_small"), 48)
            for h in range(8):
                tr = pe.transpose(pb[h // 4][:, h % 4 * P:(h % 4 + 1) * P], ws_raw[:, h, :], ident)
            tr.then_inc(S("gm_wt"), 1)
            pe.wait_ge(S("dt_adt"), AGAIN["dt_adt"][1] + 1)
            pe.matmul(pb[5][:, 0:32], consts[:, KIND["tri"], :], dt_s[:, 6, :, :], start=True, stop=True)
            pe.matmul(pb[5][:, 32:64], consts[:, KIND["tri"], P - 1:P].to_broadcast([P, P]), dt_s[:, 6, :, :],
                      start=True, stop=True).then_inc(S("dt_cs"), 1)
            pe.wait_ge(S("gm_v"), AGAIN["gm_v"][1] + 1)
            pe.wait_ge(S("gm_wtc"), AGAIN["gm_wtc"][1] + 2)
            for m, first in enumerate((2, 0)):
                for h in range(8):
                    mm = pe.matmul(pb[first + h // 4][:, h % 4 * P:(h % 4 + 1) * P], ws_t[:, h, :],
                                   vg_rm[:, m, h * P:(h + 1) * P], start=True, stop=True)
                mm.then_inc(S("gm_mix"), 1)
            pe.wait_ge(S("gm_y"), AGAIN["gm_y"][1] + 1)
            turn_normed(u_rm, "gm_tr")
            pe.wait_ge(S("gm_lo"), 8)
            for j in range(6):
                if j >= 4:
                    pe.wait_ge(S("xbc_taps"), 6 * (j - 3))
                unit_t(FIRST["xbc"] + j, None, 8, x_hi, x_lo, (j % 4,))
            pe.wait_ge(S("xbc_silu"), 6)
            for m in range(NHALF):
                for t in range(8):
                    tr = pe.transpose(pb[2 * m + t // 4][:, t % 4 * P:(t % 4 + 1) * P], xbc_f[:, t, m * P:(m + 1) * P],
                                      ident)
                tr.then_inc(S("ssm_tr"), 1)
            pe.wait_ge(S("dt_used"), AGAIN["dt_used"][1] + 1)
            for g in range(2):
                tr = pe.transpose(pb[4][:, g * P:(g + 1) * P], xbc_f[:, 8 + g, 0:P], ident)
            tr.then_inc(S("ssm_tr"), 1)
            pe.wait_ge(S("ssm_bmc"), AGAIN["ssm_bmc"][1] + 1)
            pe.wait_ge(S("ssm_xds"), AGAIN["ssm_xds"][1] + 1)
            for g in range(2):
                mm = pe.matmul(pb[6 + g][:, :], bm_rm[:, g * P:(g + 1) * P], y_rm[:, 1, g * 512:(g + 1) * 512],
                               start=True, stop=True)
            mm.then_inc(S("ssm_state"), 1)
            for m in range(NHALF):
                pe.wait_ge(S("ssm_bmc"), AGAIN["ssm_bmc"][1] + 1 + m)
                for g in range(2):
                    mm = pe.matmul(pb[4][:, g * P:(g + 1) * P], xbc_f[:, 8 + g, m * P:(m + 1) * P],
                                   xbc_f[:, 10 + g, m * P:(m + 1) * P], start=True, stop=True)
                mm.then_inc(S("ssm_cb"), 1)
                for g in range(2):
                    n = 2 * m + g
                    pe.wait_ge(S("ssm_xrm"), 2)
                    if n:
                        pe.wait_ge(S("ssm_diff"), AGAIN["ssm_diff"][1] + 2 * n)
                    for i in range(8):
                        mm = pe.matmul(pb[i // 4][:, i % 4 * P:(i % 4 + 1) * P],
                                       dt_s[:, 6, m, 8 * g + i:8 * g + i + 1].to_broadcast([P, P]),
                                       consts[:, KIND["tri"], :], start=True, stop=True)
                    mm.then_inc(S("ssm_row"), 1)
                    if n:
                        pe.wait_ge(S("ssm_yadd"), n)
                    if m:
                        pe.wait_ge(S("ssm_stc"), AGAIN["ssm_stc"][1] + 2)
                        pe.matmul(pb[3][:, :], xbc_f[:, 10 + g, P:T], sstate[:, g, :], start=True,
                                  stop=True).then_inc(S("ssm_off"), 1)
                    pe.wait_ge(S("ssm_att"), AGAIN["ssm_att"][1] + n + 1)
                    for i in range(8):
                        mm = pe.matmul(pb[2][:, i * 64:i * 64 + 64], att[:, i, :],
                                       xd_rm[:, (8 * g + i) * 64:(8 * g + i) * 64 + 64], start=True, stop=True)
                    mm.then_inc(S("ssm_y"), 1)
            pe.wait_ge(S("ssm_yn"), 4)
            turn_normed(y_rm, "ssm_ytr")
            pe.wait_ge(S("ssm_lo"), 8)
            out_rows("mix2_out", 16, y2_hi, y2_lo)
            norm(4)
            up_pairs("ffn2_up", "ffn2_gfree", "ffn2_hid", 4)
            out_rows("ffn2_down", KF, h_hi, h_lo, ready=hidden_ready("ffn2"))
            norm(5)
            pe.wait_ge(S("norm_lo"), 48)
            rows("ple_gate", 8, x_hi, x_lo)
            pe.wait_ge(S("ple_small"), 64)
            for k in range(2):
                for m in range(NHALF):
                    tr = pe.transpose(pb[0][:, k * T + m * P:k * T + (m + 1) * P], p_rm[:, m, k * P:(k + 1) * P], ident)
            tr.then_inc(S("ple_tr"), 1)
            pe.wait_ge(S("ple_lo"), 1)
            rows("ple_proj", 2, p_hi, p_lo, banks=((0, 1), (2, 3)))

        @block.scalar
        def _(act):
            nxt = [0]

            def split(u, it=None):
                act.wait_ge(raw_landed[u % RING], at(16 * (u // RING + 1), it, 16))
                if u >= RING:
                    act.wait_ge(unit_used, at(u - RING + 1, it, 4))
                act.activation(w_hi[:, u % RING, :], w_raw[:, u % RING, :], ACT.Copy).then_inc(hi_split, 1)

            def ahead(u):
                while nxt[0] < min(u + RING, UNITS):
                    split(nxt[0])
                    nxt[0] += 1

            def in_step(name, body):
                def step(j, it):
                    if it is None:
                        ahead(FIRST[name] + j)
                    else:
                        split(FIRST[name] + j + RING - 1, it)
                    body(j, it)
                    if it is not None and j == 3:
                        nxt[0] = FIRST[name] + units // 4 * 4 + RING - 1
                units = dict(STREAM)[name]
                ahead(FIRST[name] - 1)
                in_turns(act, units, step)

            def run_ahead(name, but=0):
                for j in range(dict(STREAM)[name] - but):
                    ahead(FIRST[name] + j)

            def norm(n):
                for m in range(NHALF):
                    out_squares(n, m)
                    for c in range(2):
                        if n:
                            act.wait_ge(S("resid_done"), 4 * (n - 1) + 2 * m + c + 1)
                        else:
                            act.wait_ge(S(f"x_landed{m}"), 16)
                        act.activation(xn[:, m, c * 512:(c + 1) * 512], resid[:, m, c * 512:(c + 1) * 512], ACT.Square,
                                       scale=1.0 / 32, accum_out=norm_s[:, 16 + 2 * m + c:17 + 2 * m + c]
                                       ).then_inc(S("norm_ss"), 1)

            OUT_LAST = (FIRST["conv_up"], FIRST["ffn1_up"])

            def out_squares(n, m):
                if n not in (1, 2):
                    return
                act.wait_ge(S("half_out"), n) if m == 0 else act.wait_ge(unit_used, OUT_LAST[n - 1])
                for c in range(2):
                    act.activation(xn[:, m, c * 512:(c + 1) * 512], pb[4 + 2 * m + c][:, :], ACT.Square,
                                   scale=1.0 / 32, accum_out=norm_s[:, 8 + 2 * m + c:9 + 2 * m + c]
                                   ).then_inc(S("post_sq"), 1)

            def turned_hi(base, turned, banks, name, dst, signal):
                for k in range(8):
                    act.wait_ge(S(turned), base + k // 2 + 1)
                    act.activation(dst[:, k, :], bank(banks[k // 2], 2)[:, k % 2, :], ACT.Copy,
                                   scale=col(name, k)).then_inc(S(signal), 1)

            def norm_split(n, name):
                turned_hi(4 * n, "norm_tr", (0, 1, 2, 3), name, x_hi, "norm_hi")

            norm(0)
            split(0)
            nxt[0] = 1
            act.wait_ge(S("consts_landed"), 32)
            norm_split(0, "mix_pre")
            ahead(-1)

            def rw_copy(j, it):
                act.wait_ge(unit_used, FIRST["rw"] + j + 1)
                if j >= 2:
                    act.wait_ge(S("rw_pm"), 2 * (j - 1))
                act.wait_ge(S("rw_init"), 1)
                act.activation(psh[:, j % 2, :, 1:T + 1], bank(j % 4, 2), ACT.Copy).then_inc(S("rw_cp"), 1)

            in_step("rw", rw_copy)
            ahead(FIRST["ret"] - 1)
            act.wait_ge(S("ret_trig"), 1)
            act.activation(trig[:, 4:6, :, :], trig[:, 2:4, :, :], ACT.Sin).then_inc(S("ret_sin"), 1)

            def block_copy(b, used, dst, func):
                for m in range(NHALF):
                    ins = act.activation(dst[:, m, :], pb[4 + 2 * (b % 2) + m][:, :], func)
                ins.then_inc(S(used), 1)

            ret_dst = (q_rm, kr_rm, vr_rm[:, :, 0:512], vr_rm[:, :, 512:1024], sg_rm[:, :, 0:512],
                       sg_rm[:, :, 512:1024])
            evacuated = [0]

            def behind(step):
                done = BEFORE[step] // 4
                while evacuated[0] < done:
                    j = evacuated[0]
                    if j >= 12 or j % 2:
                        act.wait_ge(unit_used, FIRST["ret"] + j + 1)
                    if j < 12 and j % 2:
                        block_copy(j // 2, "ret_free", ret_dst[j // 2], ACT.Copy if j < 8 else ACT.Silu)
                    elif 12 <= j < 20:
                        if j == 16:
                            act.wait_ge(S("rw_done"), 1)
                        dst = sig_rw if j < 16 else sig_ret
                        act.activation(dst[:, 2 * (j % 4):2 * (j % 4) + 2, :], bank(4 + j % 4, 2),
                                       ACT.Sigmoid).then_inc(S("gates_ev"), 1)
                    evacuated[0] += 1
                ahead(FIRST["ret"] + done)

            act.wait_ge(S("rw_pm"), 14)
            act.activation(act_w[0:64, 0, :], pm[0:64, 12, :], ACT.Tanh).then_inc(S("rw_lora"), 1)
            act.activation(act_w[:, 1, :], pm[:, 13, :], ACT.Sigmoid).then_inc(S("rw_lora"), 1)
            act.wait_ge(S("rw_kk0"), 1)
            act.activation(t2, t1[:, :, :], ACT.Square).then_inc(S("rw_sq"), 1)
            act.wait_ge(S("rw_z"), 1)
            for t in range(4):
                act.activation(sw[:, t, :], bank(t // 2, 2)[:, t % 2, :], ACT.Sigmoid,
                               bias=col("w0", t)).then_inc(S("rw_sw"), 1)
            act.wait_ge(S("rw_z"), 2)
            for t in range(4):
                act.activation(a_s[:, t, :], bank(t // 2, 2)[:, t % 2, :], ACT.Sigmoid,
                               bias=col("a0", t)).then_inc(S("rw_as"), 1)
            act.wait_ge(S("rw_norm"), 1)
            act.activation(t2, t2, ACT.Sqrt).then_inc(S("rw_normrt"), 1)
            behind("low_rank")
            act.wait_ge(S("rw_z"), 3)
            for b in range(2):
                act.activation(g_t[:, 2 * b:2 * b + 2, :], bank(2 + b, 2), ACT.Copy).then_inc(S("rw_g"), 1)
            act.wait_ge(S("rw_css"), 2)
            act.activation(e_pos[:, :, :], css[:, :, :], ACT.Exp, scale=-DECAY_SCALE).then_inc(S("rw_e"), 1)
            act.wait_ge(S("rw_e"), 1)
            act.activation(css[:, :, :], css[:, :, :], ACT.Exp, scale=DECAY_SCALE).then_inc(S("rw_e"), 1)
            act.activation(b_f[:, :, :], b_f[:, :, :], ACT.Exp, scale=-DECAY_SCALE).then_inc(S("rw_e"), 1)
            act.wait_ge(S("rw_tr"), 2)
            for m in range(NHALF):
                act.activation(v_rm[:, m, :], pb[2 + m][:, :], ACT.Copy).then_inc(S("rw_v"), 1)
            behind("norms")
            behind("keys")
            behind("l")
            behind("t0")
            for j in range(1, LEVELS):
                act.wait_ge(S("rw_t"), j + 1)
                for q in range(2):
                    act.activation(tp[:, 8 * q:8 * q + 8, :], bank(q, 8), ACT.Copy).then_inc(S("rw_tp"), 1)
                behind(f"t{j}")
                behind(f"x{j}")
            act.wait_ge(S("rw_xa"), 1)
            for e in range(2):
                dst = xa[:, :, :].rearrange("p t (m e n) -> p m t e n", m=2, e=2)[:, :, :, e, :]
                act.activation(dst, pb[e][:, :].rearrange("p (m t n) -> p m t n", m=2, t=4),
                               ACT.Copy).then_inc(S("rw_xac"), 1)
            for step in ("xa", "xmv", "s0", "u1", "s1", "u2", "s2", "u3"):
                behind(step)
            act.wait_ge(S("rw_yp"), 1)
            for q in range(2):
                dst = ys_v.rearrange("p m (t q d) -> p m t q d", t=4, q=2)[:, :, :, q, :]
                act.activation(dst, pb[q][:, :].rearrange("p (m t d) -> p m t d", m=2, t=4),
                               ACT.Copy).then_inc(S("rw_y"), 1)
            behind("y")
            act.wait_ge(S("rw_gnv"), 1)
            act.activation(gn[:, 2, :], gn[:, 1, :], ACT.Sqrt).then_inc(S("rw_gnrt"), 1)
            behind("y2")
            for t in range(4):
                act.wait_ge(S("rw_yt"), t // 2 + 1)
                act.activation(ytmp[:, t, :], bank(t // 2, 2)[:, t % 2, :], ACT.Identity, bias=col("lnx_b", t),
                               scale=col("lnx_w", t)).then_inc(S("rw_ln"), 1)
            act.wait_ge(S("rw_yg"), 1)
            act.activation(yrw_hi[:, :, :], ytmp[:, :, :], ACT.Copy).then_inc(S("rw_yhi"), 1)
            behind("yt")

            for b in range(2):
                act.wait_ge(S("ret_tr"), b + 1)
                act.activation(q_f[:, 2 * b:2 * b + 2, :], bank(b, 2), ACT.Copy).then_inc(S("ret_qf"), 1)
            behind("qk")
            act.wait_ge(S("ret_r"), 1)
            act.activation(rstate[:, :, :], bank(0, 4), ACT.Copy).then_inc(S("ret_rc"), 1)
            behind("sc0")
            behind("o0")
            behind("o1")
            act.wait_ge(S("ret_var"), 1)
            act.activation(ret_s[:, 9, :], ret_s[:, 8, :], ACT.Sqrt).then_inc(S("ret_rt"), 1)
            behind("stats")
            for b in range(4):
                act.wait_ge(S("ret_yt"), b + 1)
                act.activation(yret_hi[:, 2 * b:2 * b + 2, :], bank(b, 2), ACT.Copy).then_inc(S("ret_yhi"), 1)
            behind("rest0")
            behind("rest1")
            for j in range(4):
                ahead(FIRST["branch_ret"] + j)
                act.wait_ge(S("merged"), j + 1)
                act.activation(x_hi[:, 2 * j:2 * j + 2, :], merged[:, 2 * j:2 * j + 2, :],
                               ACT.Copy).then_inc(S("merged_hi"), 1)
            run_ahead("mix_out", 2)

            norm(1)
            norm_split(1, "ffn_pre")
            def conv_first_tap(j, it):
                side, b = j % 2, j // 2 % 2
                act.wait_ge(unit_used, at(FIRST["conv_up"] + j + 1, it, 4))
                act.wait_ge(S("conv_hid"), at(j // 2 + 1, it, 2))
                for i in range(2):
                    tile = at(22 * side + j // 2 * 2 + i, it, 4)
                    act.activation((cval if side else cgate)[:, b, i, :], bank(j % 4, 2)[:, i, :], ACT.Identity,
                                   bias=cols[:, bass.ds(tile + COL["conv1_b"], 1)],
                                   scale=cols[:, bass.ds(tile + COL["conv1_w"] + 88, 1)]).then_inc(S("conv_tap2"), 1)
                if side:
                    act.wait_ge(S("conv_vfree"), at(j // 2 + 3, it, 2))
                    act.activation(gate[:, b, :].rearrange("p (i n) -> p i n", i=2), cgate[:, b, :, :],
                                   ACT.Gelu_apprx_tanh).then_inc(S("conv_gelu"), 1)

            in_step("conv_up", conv_first_tap)
            run_ahead("conv_down", 2)

            def swiglu_gate(name):
                act.sem_inc(S(name + "_gfree"), 2)

                def body(j, it):
                    if j % 2:
                        return
                    b = j // 2 % 2
                    act.wait_ge(unit_used, at(FIRST[name + "_up"] + j + 1, it, 4))
                    act.wait_ge(S(name + "_hid"), at(j // 2 + 1, it, 2))
                    act.activation(gate[:, b, :], pb[j % 4][:, :], ACT.Silu).then_inc(S(name + "_gfree"), 1)
                in_step(name + "_up", body)
                run_ahead(name + "_down", 2)

            norm(2)
            norm_split(2, "ffn1")
            swiglu_gate("ffn1")
            norm(3)
            norm_split(3, "mix2")
            act.wait_ge(S("dt_small"), 64)
            act.activation(w_dt_hi[:, :, :], w_dt[:, :, :], ACT.Copy).then_inc(S("dt_whi"), 1)
            act.sem_inc(S("uvz_free"), 2)
            ahead(FIRST["uvz"] - 1)
            for j in range(12):
                ahead(FIRST["uvz"] + j)
                if j % 2:
                    act.wait_ge(unit_used, FIRST["uvz"] + j + 1)
                    block_copy(j // 2, "uvz_free", (u_rm, vg_rm, z_s)[j // 4][:, :, j // 2 % 2 * 512:][:, :, 0:512],
                               ACT.Gelu if j < 8 else ACT.Silu)
            act.wait_ge(S("dt_na"), AGAIN["dt_na"][1] + 1)
            act.activation(dt_s[:, 2, :, :], dt_s[:, 1, :, :], ACT.Exp).then_inc(S("dt_e"), 1)
            act.activation(rows16[:, 1, :], rows16[:, 1, :], ACT.Exp).then_inc(S("dt_e"), 1)
            for m in range(NHALF):
                act.wait_ge(S("gm_ya"), AGAIN["gm_ya"][1] + m + 1)
                act.activation(vg_rm[:, m, :], u_rm[:, m, :], ACT.Square,
                               accum_out=gm_s[:, 24 + m:25 + m]).then_inc(S("gm_sq"), 1)
            turned_hi(0, "gm_tr", (0, 1, 2, 3), "gm_out", y2_hi, "gm_hi")
            act.wait_ge(S("gm_lo"), 8)

            def xbc_first_tap(j, it):
                act.wait_ge(unit_used, FIRST["xbc"] + j + 1)
                for i in range(2):
                    k = 2 * j + i
                    act.activation(xbc_f[:, k, :], bank(j % 4, 2)[:, i, :], ACT.Identity, bias=col("conv2_b", k),
                                   scale=col("conv2_w", 36 + k)).then_inc(S("xbc_tap3"), 1)
                if j:
                    xbc_silu(j - 1)

            def xbc_silu(j):
                act.wait_ge(S("xbc_taps"), 6 * j + 6)
                act.activation(xbc_f[:, 2 * j:2 * j + 2, :], xbc_f[:, 2 * j:2 * j + 2, :],
                               ACT.Silu).then_inc(S("xbc_silu"), 1)

            in_step("xbc", xbc_first_tap)
            xbc_silu(5)
            ahead(FIRST["mix2_out"] - 1)
            act.wait_ge(S("dt_csd"), 3)
            act.activation(dt_s[:, 9:11, :, :], dt_s[:, 7:9, :, :], ACT.Exp).then_inc(S("dt_ecs"), 1)
            for m in range(NHALF):
                act.wait_ge(S("ssm_tr"), m + 1)
                for b in range(2):
                    ins = act.activation(xs_rm[:, m, b * 512:(b + 1) * 512], pb[2 * m + b][:, :], ACT.Copy)
                ins.then_inc(S("ssm_xrm"), 1)
            act.wait_ge(S("ssm_tr"), 3)
            act.activation(bm_rm[:, :], pb[4][:, 0:256], ACT.Copy).then_inc(S("ssm_bmc"), 1)
            act.wait_ge(S("ssm_state"), AGAIN["ssm_state"][1] + 1)
            for g in range(2):
                act.activation(sstate[:, g, :], pb[6 + g][:, :], ACT.Copy).then_inc(S("ssm_stc"), 1)
            for n in range(4):
                act.wait_ge(S("ssm_min"), AGAIN["ssm_min"][1] + n + 1)
                act.activation(att[:, :, :], att[:, :, :], ACT.Exp).then_inc(S("ssm_exp"), 1)
            for m in range(NHALF):
                for g in range(2):
                    act.wait_ge(S("ssm_yz"), m + 1)
                    act.activation(xs_rm[:, m, g * 512:(g + 1) * 512], y_rm[:, m, g * 512:(g + 1) * 512], ACT.Square,
                                   accum_out=dt_s[:, 11, 0, 2 * m + g:2 * m + g + 1]).then_inc(S("ssm_sq"), 1)
            turned_hi(0, "ssm_ytr", (0, 1, 2, 3), "ssm", y2_hi[:, 8:16, :], "ssm_hi")
            run_ahead("mix2_out", 2)
            norm(4)
            norm_split(4, "ffn2")
            swiglu_gate("ffn2")
            norm(5)
            norm_split(5, "ple")
            run_ahead("ple_gate")
            act.wait_ge(S("ple_tr"), 1)
            act.activation(p_hi[:, :, :], bank(0, 2), ACT.Copy).then_inc(S("ple_hi"), 1)
            for m in range(NHALF):
                act.wait_ge(S("ple_g"), 2 * m + 2)
                act.activation(gsig[:, m, :], gsig[:, m, :], ACT.Sigmoid).then_inc(S("ple_sig"), 1)
            norm(6)

        @block.vector
        def _(dve):
            nxt, steps = [0], [0]

            def link(ins):
                steps[0] += 1
                ins.then_inc(S("dve_step"), 1)
                dve.wait_ge(S("dve_step"), steps[0])

            def split(u, it=None):
                dve.wait_ge(hi_split, at(u + 1, it, 4))
                dve.tensor_tensor(w_lo[:, u % RING, :], w_raw[:, u % RING, :], w_hi[:, u % RING, :],
                                  ALU.subtract).then_inc(lo_split, 1)

            def ahead(u):
                while nxt[0] < min(u + RING, UNITS):
                    split(nxt[0])
                    nxt[0] += 1

            def in_step(name, body):
                def step(j, it):
                    if it is None:
                        ahead(FIRST[name] + j)
                    else:
                        split(FIRST[name] + j + RING - 1, it)
                    body(j, it)
                    if it is not None and j == 3:
                        nxt[0] = FIRST[name] + units // 4 * 4 + RING - 1
                units = dict(STREAM)[name]
                ahead(FIRST[name] - 1)
                in_turns(dve, units, step)

            def run_ahead(name, but=0):
                for j in range(dict(STREAM)[name] - but):
                    ahead(FIRST[name] + j)

            def norm_scale(n, m):
                dve.wait_ge(S("norm_ss"), 4 * n + 2 * m + 2)
                dve.scalar_tensor_tensor(out=norm_s[:, 2 + m:3 + m], in0=norm_s[:, 16 + 2 * m:17 + 2 * m], scalar=RMS_EPS,
                                         in1=norm_s[:, 17 + 2 * m:18 + 2 * m], op0=ALU.add,
                                         op1=ALU.add).then_inc(S("norm_ms"), 1)
                dve.wait_ge(S("norm_rt"), 2 * n + m + 1)
                dve.tensor_scalar(xn[:, m, :], resid[:, m, :], norm_s[:, 6 + m:7 + m], None,
                                  ALU.mult).then_inc(S("norm_xn"), 1)

            def turned_lo(base, hi, banks, name, dst_hi, dst, signal):
                for k in range(8):
                    dve.wait_ge(S(hi), base + k // 2 * 2 + 2)
                    dve.scalar_tensor_tensor(out=dst[:, k, :], in0=bank(banks[k // 2], 2)[:, k % 2, :],
                                             scalar=col(name, k), in1=dst_hi[:, k, :], op0=ALU.mult,
                                             op1=ALU.subtract).then_inc(S(signal), 1)

            def norm(n, name, out):
                for m in range(NHALF):
                    out(m)
                    norm_scale(n, m)
                if n == 0:
                    split(0)
                    nxt[0] = 1
                turned_lo(8 * n, "norm_hi", (0, 1, 2, 3), name, x_hi, x_lo, "norm_lo")

            dve.wait_ge(S("consts_landed"), 32)
            norm(0, "mix_pre", lambda m: None)
            ahead(-1)
            dve.wait_ge(S("trig_small"), 32)
            link(dve.tensor_copy(posf[:, 0, :], posi[:, :]))
            inv = small[:, SMALL_INV:SMALL_INV + 32]
            for m in range(NHALF):
                ins = dve.tensor_scalar(trig[:, 0, m, :], inv, posf[:, 0, m:m + 1], None, ALU.mult)
            link(ins)
            for i, quarter in enumerate((0.0, 0.25)):
                turns, rest = trig[:, 1, :, :], trig[:, 2 + i, :, :]
                link(dve.tensor_scalar(turns, trig[:, 0, :, :], 1.0 / TWO_PI, quarter, ALU.mult, ALU.add))
                link(dve.tensor_scalar(turns, turns, ROUND, None, ALU.add))
                link(dve.tensor_scalar(turns, turns, ROUND, None, ALU.subtract))
                src = trig[:, 0, :, :]
                for part in (PI_A, PI_B, PI_C):
                    link(dve.scalar_tensor_tensor(out=rest, in0=turns, scalar=-part, in1=src, op0=ALU.mult, op1=ALU.add))
                    src = rest
                link(dve.tensor_scalar(rest, rest, quarter * TWO_PI, PI_F32, ALU.add, ALU.min))
                ins = dve.tensor_scalar(rest, rest, -PI_F32, None, ALU.max)
                link(ins)
            dve.tensor_scalar(trig[:, 0, :, :], trig[:, 0, :, :], 0.0, None, ALU.add).then_inc(S("ret_trig"), 1)

            link(dve.memset(cmask[:, :, :], 1.0))
            dve.memset(cmask[:, :, :].rearrange("p a (c n) -> p (a c) n", n=CHUNK)[:, :, 0:1], 0.0)
            dve.memset(psh_flat[:, :].rearrange("p (g n) -> p g n", g=4)[:, :, 0:1], 0.0).then_inc(S("rw_init"), 1)

            def shift_mix(j, it):
                dve.wait_ge(S("rw_cp"), j + 1)
                now, before = psh[:, j % 2, :, 1:T + 1], psh[:, j % 2, :, 0:T]
                if j >= 1:
                    dve.wait_ge(S("rw_pm"), 2 * j)
                link(dve.tensor_tensor(act_w[:, :, :], before, now, ALU.subtract))
                for i in range(2):
                    dve.scalar_tensor_tensor(out=pm[:, 2 * j + i, :], in0=act_w[:, i, :], scalar=col("mu", 2 * j + i),
                                             in1=now[:, i, :], op0=ALU.mult, op1=ALU.add).then_inc(S("rw_pm"), 1)

            in_step("rw", shift_mix)
            ahead(FIRST["ret"] - 1)
            link(dve.tensor_scalar(omka[:, :], col("k_a", 0, 4), -1.0, 1.0, ALU.mult, ALU.add))
            dve.wait_ge(S("rw_pm"), 14)
            for t in range(4):
                ins = dve.tensor_scalar(t1[:, t, :], pm[:, 4 + t, :], col("k_k", t), None, ALU.mult)
            ins.then_inc(S("rw_kk0"), 1)
            dve.wait_ge(S("rw_kk0"), 1)
            merged_rw = [0]

            def behind(step):
                done = BEFORE[step] // 4
                while 20 + merged_rw[0] < done:
                    j = merged_rw[0]
                    dve.wait_ge(unit_used, FIRST["branch_rw"] + j + 1)
                    dve.wait_ge(S("gates_ev"), 4)
                    for b in range(2):
                        k = 4 * j + 2 * b
                        dve.tensor_tensor(merged[:, k:k + 2, :], bank(4 + 2 * j + b, 2), sig_rw[:, k:k + 2, :],
                                          ALU.mult).then_inc(S("merged_rw"), 1)
                    merged_rw[0] += 1
                ahead(FIRST["ret"] + done)

            dve.wait_ge(S("rw_sw"), 4)
            dve.tensor_tensor_scan(css[:, :, :].rearrange("p a n -> p (a n)"), cmask[:, :, :].rearrange("p a n -> p (a n)"),
                                   sw[:, :, :].rearrange("p a n -> p (a n)"), 0.0, ALU.mult,
                                   ALU.add).then_inc(S("rw_css"), 1)
            dve.wait_ge(S("rw_sums"), 1)
            for b in range(2):
                ins = dve.tensor_scalar(t2[:, 2 * b:2 * b + 2, :], bank(2 + b, 2), 1e-24, None, ALU.max)
            ins.then_inc(S("rw_norm"), 1)
            dve.wait_ge(S("rw_css"), 1)
            dve.tensor_tensor(b_f[:, :, :], css[:, :, :], sw[:, :, :], ALU.subtract).then_inc(S("rw_css"), 1)
            behind("low_rank")
            dve.wait_ge(S("rw_as"), 4)
            dve.wait_ge(S("rw_normrt"), 1)
            link(dve.reciprocal(kk[:, :, :], t2))
            link(dve.tensor_tensor(kk[:, :, :], kk[:, :, :], t1[:, :, :], ALU.mult))
            for t in range(4):
                ins = dve.tensor_scalar(t1[:, t, :], a_s[:, t, :], col("k_a", t), omka[:, t:t + 1], ALU.mult, ALU.add)
            link(ins)
            link(dve.tensor_tensor(pm[:, 4:8, :], pm[:, 4:8, :], t1[:, :, :], ALU.mult))
            for t in range(4):
                ins = dve.scalar_tensor_tensor(out=t1[:, t, :], in0=pm[:, t, :], scalar=col("r_k", t),
                                               in1=pm[:, 4 + t, :], op0=ALU.mult, op1=ALU.mult)
            ins.then_inc(S("rw_rk"), 1)
            behind("norms")
            dve.wait_ge(S("rw_e"), 3)
            dve.tensor_copy(pc[:, :, :], e_pos[:, :, :].rearrange("p a (c n) -> p a c n", n=CHUNK)[:, :, :, CHUNK - 1])
            link(dve.tensor_tensor(a_f[:, :, :], kk[:, :, :], b_f[:, :, :], ALU.mult))
            link(dve.tensor_tensor(b_f[:, :, :], kk[:, :, :], a_s[:, :, :], ALU.mult))
            dve.tensor_tensor(b_f[:, :, :], b_f[:, :, :], css[:, :, :], ALU.mult)
            dve.wait_ge(S("rw_rk"), 1)
            dve.tensor_tensor(pm[:, 4:8, :], pm[:, 4:8, :], css[:, :, :], ALU.mult)
            dve.tensor_tensor(pm[:, 0:4, :], pm[:, 0:4, :], e_pos[:, :, :], ALU.mult).then_inc(S("rw_abkr"), 1)
            dve.wait_ge(S("rw_sums"), 2)
            for b in range(2):
                ins = dve.tensor_tensor(bonus[:, 2 * b:2 * b + 2, :], bank(b, 2), pm[:, 8 + 2 * b:10 + 2 * b, :],
                                        ALU.mult)
            ins.then_inc(S("rw_bonus"), 1)
            behind("keys")

            def causal(k):
                return consts[:, KIND["causal"]:KIND["causal"] + 1, k * CHUNK:(k + 1) * CHUNK].to_broadcast([P, 8, CHUNK])

            strict, incl = causal(0), causal(1)
            eye = consts[:, KIND["eye"]:KIND["eye"] + 1, 0:CHUNK].to_broadcast([P, 8, CHUNK])

            def masked(dst, first_bank, mask, signal):
                for q in range(2):
                    dve.tensor_tensor(dst[:, 8 * q:8 * q + 8, :], bank(first_bank + q, 8), mask,
                                      ALU.mult).then_inc(S(signal), 1)

            def copied(dst, first_bank, signal):
                for i in range(2):
                    dve.tensor_copy(dst[i], pb[first_bank + i][:, :]).then_inc(S(signal), 1)

            dve.wait_ge(S("rw_l"), 1)
            dve.wait_ge(S("rw_bonus"), 1)
            dve.wait_ge(S("rw_tr"), 2)
            masked(lt, 0, strict, "rw_lt")
            behind("l")
            for j in range(LEVELS):
                if j == 0:
                    dve.wait_ge(S("rw_t"), 1)
                    for q in range(2):
                        g = slice(8 * q, 8 * q + 8)
                        dve.tensor_tensor(xi[:, g, :], bank(q, 8), eye, ALU.add)
                        ins = dve.tensor_tensor(xt[:, g, :], lm[:, g, :], eye, ALU.add)
                    ins.then_inc(S("rw_xd"), 1)
                dve.wait_ge(S("rw_f"), j + 1)
                if j in (0, 5):
                    masked(gm if j == 0 else g1, 2, strict if j == 0 else incl, "rw_fd")
                elif j == 4:
                    copied([gm[:, 8 * i:8 * i + 8, :].rearrange("p g n -> p (g n)") for i in range(2)], 2, "rw_fd")
                else:
                    dst = (k_rm, a_rm, b_rm)[j - 1]
                    copied([dst[:, i, :] for i in range(2)], 2, "rw_fd")
                behind(f"t{j}")
                if j == 0:
                    continue
                dve.wait_ge(S("rw_xd"), j)
                dve.wait_ge(S("rw_x"), j)
                for q in range(2):
                    g = slice(8 * q, 8 * q + 8)
                    if j < LEVELS - 1:
                        dve.tensor_tensor(xi[:, g, :], bank(2 + q, 8), xi[:, g, :], ALU.add)
                    ins = dve.tensor_tensor(xt[:, g, :], bank(q, 8), xt[:, g, :], ALU.add)
                ins.then_inc(S("rw_xd"), 1)
                if j == LEVELS - 1:
                    dve.wait_ge(S("rw_f"), 7)
                    masked(g2, 2, incl, "rw_fd")
                behind(f"x{j}")
            behind("xa")
            dve.wait_ge(S("rw_xmv"), 1)
            for q in range(2):
                dve.tensor_scalar(wv[:, 8 * q:8 * q + 8, :], bank(2 + q, 8), -1.0, None, ALU.mult).then_inc(S("rw_w"), 1)
            behind("xmv")
            dve.wait_ge(S("rw_w"), 2)
            for c in range(4):
                m, e = divmod(c, 2)
                tok = slice(64 * e, 64 * e + 64)
                if c:
                    dve.wait_ge(S("rw_up"), c)
                    for q in range(2):
                        u = wv[tok, 8 * q + 4 * m:8 * q + 4 * m + 4, :]
                        ins = dve.tensor_tensor(u, u, pb[2 + q][tok, 0:256].rearrange("p (t d) -> p t d", t=4),
                                                ALU.subtract)
                    ins.then_inc(S("rw_u"), 1)
                    behind(f"u{c}")
                if c < 3:
                    dve.wait_ge(S("rw_s"), c + 1)
                    src = pb[0][:, 0:256].rearrange("p (t d) -> p t d", t=4)
                    if c:
                        link(dve.tensor_tensor(stmp[:, :, :], src, st[:, c, :, :], ALU.add))
                        src = stmp[:, :, :]
                    dve.tensor_tensor(st[:, c + 1, :, :], src,
                                      pc[:, :, c:c + 1].to_broadcast([P, 4, 64]), ALU.mult).then_inc(S("rw_st"), 1)
                    dve.wait_ge(S("rw_st"), c + 1)
                    behind(f"s{c}")
            dve.wait_ge(S("rw_y"), 2)
            dve.wait_ge(S("rw_yp"), 2)
            for m, e0 in ((0, 1), (1, 0)):
                for q in range(2):
                    rows_ = slice(64 * e0, P)
                    y = ys_v[rows_, m, :].rearrange("p (t q d) -> p t q d", t=4, q=2)[:, :, q, :]
                    ins = dve.tensor_tensor(y, y, pb[2 + q][rows_, m * 256:m * 256 + 256].rearrange(
                        "p (t d) -> p t d", t=4), ALU.add)
            link(ins)
            y16 = ys_v.rearrange("p m (h d) -> p (m h) d", h=8)
            n16 = yn[:, :, :].rearrange("p m (h d) -> p (m h) d", h=8)
            q16 = yq[:, :, :].rearrange("p m (h d) -> p (m h) d", h=8)

            def over_head(k):
                return gn[:, k, :].unsqueeze(2).to_broadcast([P, 16, 64])

            link(dve.tensor_reduce(gn[:, 0, :], y16, AX_X, ALU.add))
            link(dve.tensor_scalar(gn[:, 0, :], gn[:, 0, :], 1.0 / 64, None, ALU.mult))
            link(dve.tensor_tensor(n16, y16, over_head(0), ALU.subtract))
            link(dve.tensor_tensor(q16, n16, n16, ALU.mult))
            link(dve.tensor_reduce(gn[:, 1, :], q16, AX_X, ALU.add))
            dve.tensor_scalar(gn[:, 1, :], gn[:, 1, :], 1.0 / 64, 64e-5, ALU.mult, ALU.add).then_inc(S("rw_gnv"), 1)
            behind("y")
            dve.wait_ge(S("rw_gnrt"), 1)
            link(dve.reciprocal(gn[:, 3, :], gn[:, 2, :]))
            dve.tensor_tensor(n16, n16, over_head(3), ALU.mult).then_inc(S("rw_yn"), 1)
            behind("y2")
            dve.wait_ge(S("rw_ln"), 4)
            link(dve.tensor_tensor(ytmp[:, :, :], ytmp[:, :, :], bonus[:, :, :], ALU.add))
            dve.tensor_tensor(ytmp[:, :, :], ytmp[:, :, :], g_t[:, :, :], ALU.mult).then_inc(S("rw_yg"), 1)
            dve.wait_ge(S("rw_yhi"), 1)
            dve.tensor_tensor(yrw_lo[:, :, :], ytmp[:, :, :], yrw_hi[:, :, :], ALU.subtract).then_inc(S("rw_done"), 1)
            behind("yt")

            for b in range(2):
                dve.wait_ge(S("ret_tr"), 3 + b)
                dve.tensor_copy(k_f[:, 2 * b:2 * b + 2, :], bank(2 + b, 2)).then_inc(S("ret_kf"), 1)
            behind("qk")
            dve.wait_ge(S("ret_qf"), 2)
            dve.wait_ge(S("ret_small"), 16)
            dve.tensor_tensor(qd_f[:, :, :], q_f[:, :, P:T], decay[:, 8:12, :], ALU.mult).then_inc(S("ret_qd"), 1)
            masks = decay[:, 0:8, :].rearrange("p (t q) n -> p q t n", q=2)
            for m in range(NHALF):
                dve.wait_ge(S("ret_s"), m + 1)
                if m:
                    dve.wait_ge(S("ret_o"), 1)
                for q in range(2):
                    dve.tensor_tensor(sco[:, q, :, :], bank(2 + q, 4), masks[:, q, :, :], ALU.mult).then_inc(S("ret_sc"), 1)
                behind(("sc0", "o0")[m])
            stats = ret_s[:, 0:6, :].rearrange("p a b -> p (a b)").rearrange("p (h s) -> p h s", s=6)
            mv = ret_s[:, 6:8, :].rearrange("p a b -> p (a b)").rearrange("p (h s) -> p h s", s=2)

            def o_of(m, h):
                return pb[2 * m + h % 2][:, h // 2 * P:(h // 2 + 1) * P]

            for m in range(NHALF):
                dve.wait_ge(S("ret_o"), m + 1)
                for h in range(8):
                    ins = dve.bn_stats(stats[:, 8 * m + h, :], o_of(m, h))
            link(ins)
            for n in range(16):
                ins = dve.bn_aggr(mv[:, n, :], stats[:, n, :])
            link(ins)
            dve.tensor_scalar(ret_s[:, 8, :], mv[:, :, 1], 1e-5, None, ALU.add).then_inc(S("ret_var"), 1)
            behind("o1")
            dve.wait_ge(S("ret_rt"), 1)
            link(dve.reciprocal(ret_s[:, 10, :], ret_s[:, 9, :]))
            sg16 = sg_rm[:, :, :].rearrange("p m (h e) -> p (m h) e", h=8)
            dve.wait_ge(S("ret_free"), 6)
            link(dve.tensor_tensor(sg16, sg16, ret_s[:, 10, :].unsqueeze(2).to_broadcast([P, 16, P]), ALU.mult))
            for m in range(NHALF):
                for h in range(8):
                    n = 8 * m + h
                    ins = dve.scalar_tensor_tensor(out=sg16[:, n, :], in0=o_of(m, h), scalar=mv[:, n, 0:1],
                                                   in1=sg16[:, n, :], op0=ALU.subtract, op1=ALU.mult)
            ins.then_inc(S("ret_y"), 1)
            behind("stats")
            for b in range(4):
                dve.wait_ge(S("ret_yhi"), b + 1)
                dve.tensor_tensor(yret_lo[:, 2 * b:2 * b + 2, :], bank(b, 2), yret_hi[:, 2 * b:2 * b + 2, :],
                                  ALU.subtract).then_inc(S("ret_lo"), 1)
            dve.wait_ge(S("ret_lo"), 4)
            dve.sem_inc(S("ret_done"), 2)
            behind("rest0")
            behind("rest1")
            dve.wait_ge(unit_used, FIRST["branch_ret"])
            for b in range(2):
                k = 4 + 2 * b
                dve.tensor_tensor(merged[:, k:k + 2, :], bank(6 + b, 2), sig_rw[:, k:k + 2, :],
                                  ALU.mult).then_inc(S("merged_rw"), 1)
            for j in range(4):
                ahead(FIRST["branch_ret"] + j)
                dve.wait_ge(unit_used, FIRST["branch_ret"] + j + 1)
                k = slice(2 * j, 2 * j + 2)
                if j >= 2:
                    dve.wait_ge(S("merged"), j - 1)
                dve.wait_ge(S("merged_rw"), 4)
                link(dve.tensor_tensor(mtmp[:, j % 2, :, :], bank(j, 2), sig_ret[:, k, :], ALU.mult))
                dve.tensor_tensor(merged[:, k, :], merged[:, k, :], mtmp[:, j % 2, :, :], ALU.add).then_inc(S("merged"), 1)
                dve.wait_ge(S("merged_hi"), j + 1)
                dve.tensor_tensor(x_lo[:, k, :], merged[:, k, :], x_hi[:, k, :], ALU.subtract).then_inc(S("merged_lo"), 1)
            run_ahead("mix_out", 2)

            def out_normed(n, last, row, row_sem, landed):
                def out(m):
                    dve.wait_ge(S("post_sq"), 4 * n + 2 * m + 2)
                    dve.scalar_tensor_tensor(out=norm_s[:, 22 + m:23 + m], in0=norm_s[:, 8 + 2 * m:9 + 2 * m],
                                             scalar=RMS_EPS, in1=norm_s[:, 9 + 2 * m:10 + 2 * m], op0=ALU.add,
                                             op1=ALU.add).then_inc(S("post_ms"), 1)
                    dve.wait_ge(S("post_rt"), 2 * n + m + 1)
                    dve.wait_ge(S(row_sem), landed)
                    for c in range(2):
                        cc = slice(c * 512, (c + 1) * 512)
                        ins = dve.scalar_tensor_tensor(out=xn[:, m, cc], in0=pb[4 + 2 * m + c][:, :],
                                                       scalar=norm_s[:, 24 + m:25 + m], in1=row[:, cc],
                                                       op0=ALU.mult, op1=ALU.mult)
                    link(ins)
                    for c in range(2):
                        cc = slice(c * 512, (c + 1) * 512)
                        dve.tensor_tensor(resid[:, m, cc], resid[:, m, cc], xn[:, m, cc],
                                          ALU.add).then_inc(S("resid_done"), 1)
                return out

            norm(1, "ffn_pre", out_normed(0, FIRST["conv_up"], row_mix, "mix_row", 48))
            dve.sem_inc(S("conv_gfree"), 2)
            dve.sem_inc(S("conv_vfree"), 2)
            dve.sem_inc(S("conv_hid"), 2)

            def conv_taps(j, it):
                side, b = j % 2, j // 2 % 2
                c = cval if side else cgate
                free = S("conv_vfree" if side else "conv_gfree")
                dve.wait_ge(S("conv_tap2"), at(2 * j + 2, it, 8))
                for i in range(2):
                    tile = at(22 * side + j // 2 * 2 + i + COL["conv1_w"] + 44, it, 4)
                    dve.scalar_tensor_tensor(out=c[:, b, i, 1:T], in0=bank(j % 4, 2)[:, i, 0:T - 1],
                                             scalar=cols[:, bass.ds(tile, 1)], in1=c[:, b, i, 1:T],
                                             op0=ALU.mult, op1=ALU.add).then_inc(S("conv_tap1"), 1)
                for i in range(2):
                    tile = at(22 * side + j // 2 * 2 + i + COL["conv1_w"], it, 4)
                    dve.wait_ge(S("conv_tap1"), at(2 * j + i + 1, it, 8))
                    ins = dve.scalar_tensor_tensor(out=c[:, b, i, 2:T], in0=bank(j % 4, 2)[:, i, 0:T - 2],
                                                   scalar=cols[:, bass.ds(tile, 1)], in1=c[:, b, i, 2:T],
                                                   op0=ALU.mult, op1=ALU.add)
                ins.then_inc(free, 1)
                if side:
                    dve.wait_ge(S("conv_gelu"), at(j // 2 + 1, it, 2))
                    dve.wait_ge(S("conv_vfree"), at(j // 2 + 3, it, 2))
                    dve.wait_ge(S("conv_hlo"), at(j // 2 + 1, it, 2))
                    dve.tensor_tensor(hid[:, b, :], gate[:, b, :], cval[:, b, :, :].rearrange("p i n -> p (i n)"),
                                      ALU.mult).then_inc(S("conv_hid"), 1)

            in_step("conv_up", conv_taps)
            run_ahead("conv_down", 2)

            def swiglu_mul(name):
                dve.sem_inc(S(name + "_hid"), 2)

                def body(j, it):
                    if j % 2 == 0:
                        return
                    b = j // 2 % 2
                    dve.wait_ge(unit_used, at(FIRST[name + "_up"] + j + 1, it, 4))
                    dve.wait_ge(S(name + "_gfree"), at(j // 2 + 3, it, 2))
                    dve.wait_ge(S(name + "_hlo"), at(j // 2 + 1, it, 2))
                    dve.tensor_tensor(hid[:, b, :], pb[j % 4][:, :], gate[:, b, :],
                                      ALU.mult).then_inc(S(name + "_hid"), 1)
                in_step(name + "_up", body)
                run_ahead(name + "_down", 2)

            def add_out(n, scale, last):
                def out(m):
                    dve.wait_ge(S("half_out"), n) if m == 0 else dve.wait_ge(unit_used, last)
                    for c in range(2):
                        r = resid[:, m, c * 512:(c + 1) * 512]
                        dve.scalar_tensor_tensor(out=r, in0=pb[4 + 2 * m + c][:, :], scalar=scale, in1=r, op0=ALU.mult,
                                                 op1=ALU.add).then_inc(S("resid_done"), 1)
                return out

            norm(2, "ffn1", out_normed(1, FIRST["ffn1_up"], row_ffn, "ffn_row", 16))
            swiglu_mul("ffn1")
            norm(3, "mix2", add_out(3, 0.5, FIRST["uvz"]))
            dve.wait_ge(S("dt_whi"), AGAIN["dt_whi"][1] + 1)
            dve.tensor_tensor(w_dt_lo[:, :, :], w_dt[:, :, :], w_dt_hi[:, :, :], ALU.subtract).then_inc(S("dt_wlo"), 1)
            run_ahead("uvz")
            ahead(FIRST["xbc"] - 1)
            dve.wait_ge(S("uvz_free"), 6)
            gstat = gm_s[:, 32:44]
            for m in range(NHALF):
                for c in range(2):
                    link(dve.bn_stats(gstat[:, 6 * c:6 * c + 6], vg_rm[:, m, c * 512:(c + 1) * 512]))
                link(dve.bn_aggr(gm_s[:, 2 * m:2 * m + 2], gstat))
            mvar = gm_s[:, 0:4].rearrange("p (m s) -> p m s", s=2)
            dve.tensor_scalar(gm_s[:, 18:20], mvar[:, :, 1], RMS_EPS, None, ALU.add).then_inc(S("gm_var"), 1)
            dve.wait_ge(S("dt_mm"), AGAIN["dt_mm"][1] + 1)
            bias = rows16[:, 0:1, :].to_broadcast([P, NHALF, 16])
            link(dve.tensor_tensor(dt_s[:, 0, :, :], pb[4][:, 0:32].rearrange("p (m h) -> p m h", m=2), bias, ALU.add))
            dve.scalar_tensor_tensor(out=dt_s[:, 1, :, :], in0=dt_s[:, 0, :, :], scalar=-1.0, in1=dt_s[:, 0, :, :],
                                     op0=ALU.mult, op1=ALU.min).then_inc(S("dt_na"), 1)
            dve.wait_ge(S("dt_e"), AGAIN["dt_e"][1] + 2)
            e, s_, z_, acc = (dt_s[:, k, :, :] for k in (2, 3, 4, 5))
            link(dve.tensor_scalar(s_, e, 2.0, None, ALU.add))
            link(dve.reciprocal(z_, s_))
            link(dve.tensor_tensor(s_, e, z_, ALU.mult))
            link(dve.tensor_tensor(z_, s_, s_, ALU.mult))
            link(dve.tensor_scalar(acc, z_, 2.0 / 17, 2.0 / 15, ALU.mult, ALU.add))
            for k in (13, 11, 9, 7, 5, 3, 1):
                link(dve.tensor_tensor(acc, acc, z_, ALU.mult))
                link(dve.tensor_scalar(acc, acc, 2.0 / k, None, ALU.add))
            link(dve.tensor_tensor(acc, acc, s_, ALU.mult))
            link(dve.scalar_tensor_tensor(out=acc, in0=dt_s[:, 0, :, :], scalar=0.0, in1=acc, op0=ALU.max, op1=ALU.add))
            dve.scalar_tensor_tensor(out=dt_s[:, 6, :, :], in0=acc, scalar=-1.0,
                                     in1=rows16[:, 1:2, :].to_broadcast([P, NHALF, 16]),
                                     op0=ALU.mult, op1=ALU.mult).then_inc(S("dt_adt"), 1)
            tri4 = consts[:, KIND["tri"]:KIND["tri"] + 1, :].to_broadcast([P, 4, P])
            dve.wait_ge(S("gm_wt"), AGAIN["gm_wt"][1] + 1)
            for b in range(2):
                dve.tensor_tensor(ws_t[:, 4 * b:4 * b + 4, :], bank(b, 4), tri4, ALU.mult).then_inc(S("gm_wtc"), 1)
            dve.wait_ge(S("gm_rt"), AGAIN["gm_rt"][1] + 1)
            dve.wait_ge(S("gm_small"), 48)
            for m in range(NHALF):
                ins = dve.tensor_scalar(vg_rm[:, m, :], vg_rm[:, m, :], gm_s[:, 2 * m:2 * m + 1], gm_s[:, 22 + m:23 + m],
                                        ALU.subtract, ALU.mult)
            link(ins)
            for m in range(NHALF):
                ins = dve.tensor_tensor(vg_rm[:, m, :], vg_rm[:, m, :], row_ln_g[:, :], ALU.mult)
            link(ins)
            for m in range(NHALF):
                ins = dve.tensor_tensor(vg_rm[:, m, :], vg_rm[:, m, :], row_ln_b[:, :], ALU.add)
            ins.then_inc(S("gm_v"), 1)
            for m, first in enumerate((2, 0)):
                dve.wait_ge(S("gm_mix"), AGAIN["gm_mix"][1] + m + 1)
                for h in range(8):
                    u = u_rm[:, m, h * P:(h + 1) * P]
                    ins = dve.scalar_tensor_tensor(out=u, in0=pb[first + h // 4][:, h % 4 * P:(h % 4 + 1) * P],
                                                   scalar=col("gm_b", h), in1=u, op0=ALU.add, op1=ALU.mult)
                ins.then_inc(S("gm_ya"), 1)
            dve.wait_ge(S("dt_cs"), AGAIN["dt_cs"][1] + 1)
            cs_p = pb[5][:, 0:32].rearrange("p (m h) -> p m h", m=2)
            dve.tensor_copy(dt_s[:, 7, :, :], cs_p).then_inc(S("dt_csd"), 1)
            dve.wait_ge(S("dt_csd"), 1)
            dve.tensor_tensor(dt_s[:, 8, :, :], pb[5][:, 32:64].rearrange("p (m h) -> p m h", m=2), dt_s[:, 7, :, :],
                              ALU.subtract).then_inc(S("dt_csd"), 1)
            dve.wait_ge(S("dt_csd"), 2)
            dve.sem_inc(S("dt_csd"), 1)
            dve.sem_inc(S("dt_used"), 1)
            dve.wait_ge(S("gm_sq"), AGAIN["gm_sq"][1] + 2)
            dve.tensor_scalar(gm_s[:, 26:28], gm_s[:, 24:26], 1.0 / D, RMS_EPS, ALU.mult, ALU.add).then_inc(S("gm_ms"), 1)
            dve.wait_ge(S("gm_rt"), AGAIN["gm_rt"][1] + 2)
            for m in range(NHALF):
                ins = dve.tensor_scalar(u_rm[:, m, :], u_rm[:, m, :], gm_s[:, 30 + m:31 + m], None, ALU.mult)
            ins.then_inc(S("gm_y"), 1)
            turned_lo(0, "gm_hi", (0, 1, 2, 3), "gm_out", y2_hi, y2_lo, "gm_lo")

            def xbc_taps(j, it):
                for i in range(2):
                    k = 2 * j + i
                    dve.wait_ge(S("xbc_tap3"), 2 * j + 2)
                    for back in (1, 2, 3):
                        n = 6 * j + 3 * i + back
                        if back > 1:
                            dve.wait_ge(S("xbc_taps"), n - 1)
                        dve.scalar_tensor_tensor(out=xbc_f[:, k, back:T], in0=bank(j % 4, 2)[:, i, 0:T - back],
                                                 scalar=col("conv2_w", 12 * (3 - back) + k), in1=xbc_f[:, k, back:T],
                                                 op0=ALU.mult, op1=ALU.add).then_inc(S("xbc_taps"), 1)

            in_step("xbc", xbc_taps)
            ahead(FIRST["mix2_out"] - 1)

            def heads16(ap):
                return ap.unsqueeze(2).to_broadcast([P, 16, 64])

            def by_head(ap):
                return ap.rearrange("p (h d) -> p h d", d=64)

            dve.wait_ge(S("ssm_xrm"), 1)
            link(dve.tensor_tensor(by_head(xd_rm[:, :]), by_head(xs_rm[:, 0, :]), heads16(dt_s[:, 5, 0, :]), ALU.mult))
            dve.wait_ge(S("dt_ecs"), AGAIN["dt_ecs"][1] + 1)
            dve.wait_ge(S("ssm_xrm"), 2)
            dve.wait_ge(S("ssm_tr"), 2)
            dve.tensor_tensor(by_head(y_rm[:, 1, :]), by_head(xd_rm[:, :]), heads16(dt_s[:, 10, 0, :]),
                              ALU.mult).then_inc(S("ssm_xds"), 1)
            tri2 = consts[:, KIND["tri"]:KIND["tri"] + 1, :].to_broadcast([P, 2, P])
            for m in range(NHALF):
                if m:
                    dve.wait_ge(S("ssm_y"), 2)
                    link(dve.tensor_tensor(by_head(xd_rm[:, :]), by_head(xs_rm[:, 1, :]), heads16(dt_s[:, 5, 1, :]),
                                           ALU.mult))
                dve.wait_ge(S("ssm_cb"), AGAIN["ssm_cb"][1] + m + 1)
                dve.tensor_tensor(cb[:, :, :], pb[4][:, 0:256].rearrange("p (g n) -> p g n", g=2), tri2,
                                  ALU.mult).then_inc(S("ssm_bmc"), 1)
                dve.wait_ge(S("ssm_bmc"), AGAIN["ssm_bmc"][1] + m + 2)
                if m:
                    dve.wait_ge(S("ssm_state"), AGAIN["ssm_state"][1] + 1)
                link(dve.tensor_tensor(by_head(y_rm[:, m, :]), by_head(xs_rm[:, m, :]), heads16(rows16[:, 2, :]),
                                       ALU.mult))
                for g in range(2):
                    n = 2 * m + g
                    dve.wait_ge(S("ssm_row"), AGAIN["ssm_row"][1] + n + 1)
                    if n:
                        dve.wait_ge(S("ssm_y"), n)
                    for b in range(2):
                        h = 8 * g + 4 * b
                        dve.tensor_tensor(att[:, 4 * b:4 * b + 4, :], bank(b, 4),
                                          dt_s[:, 7, m, h:h + 4].unsqueeze(2).to_broadcast([P, 4, P]),
                                          ALU.subtract).then_inc(S("ssm_diff"), 1)
                    dve.wait_ge(S("ssm_diff"), AGAIN["ssm_diff"][1] + 2 * n + 2)
                    dve.tensor_scalar(att[:, :, :], att[:, :, :], 0.0, None, ALU.min).then_inc(S("ssm_min"), 1)
                    dve.wait_ge(S("ssm_exp"), AGAIN["ssm_exp"][1] + n + 1)
                    dve.tensor_tensor(att[:, :, :], att[:, :, :], cb[:, g:g + 1, :].to_broadcast([P, 8, P]),
                                      ALU.mult).then_inc(S("ssm_att"), 1)
                    y = y_rm[:, m, g * 512:(g + 1) * 512]
                    dve.wait_ge(S("ssm_y"), n + 1)
                    ins = dve.tensor_tensor(y, y, pb[2][:, :], ALU.add)
                    if m:
                        link(ins)
                        dve.wait_ge(S("ssm_off"), AGAIN["ssm_off"][1] + g + 1)
                        tmp = xs_rm[:, 0, g * 512:(g + 1) * 512]
                        link(dve.tensor_tensor(by_head(tmp), by_head(pb[3][:, :]),
                                               dt_s[:, 9, 1, 8 * g:8 * g + 8].unsqueeze(2).to_broadcast([P, 8, 64]),
                                               ALU.mult))
                        ins = dve.tensor_tensor(y, y, tmp, ALU.add)
                    ins.then_inc(S("ssm_yadd"), 1)
            for m in range(NHALF):
                dve.wait_ge(S("ssm_yadd"), 4)
                dve.tensor_tensor(y_rm[:, m, :], y_rm[:, m, :], z_s[:, m, :], ALU.mult).then_inc(S("ssm_yz"), 1)
            dve.wait_ge(S("ssm_sq"), AGAIN["ssm_sq"][1] + 4)
            dve.tensor_scalar(dt_s[:, 11, 0, 4:8], dt_s[:, 11, 0, 0:4], 1.0 / 512, RMS_EPS, ALU.mult,
                              ALU.add).then_inc(S("ssm_ms"), 1)
            dve.wait_ge(S("ssm_rt"), AGAIN["ssm_rt"][1] + 1)
            for n in range(4):
                y = y_rm[:, n // 2, n % 2 * 512:(n % 2 + 1) * 512]
                dve.tensor_scalar(y, y, dt_s[:, 11, 0, 12 + n:13 + n], None, ALU.mult).then_inc(S("ssm_yn"), 1)
            turned_lo(0, "ssm_hi", (0, 1, 2, 3), "ssm", y2_hi[:, 8:16, :], y2_lo[:, 8:16, :], "ssm_lo")
            run_ahead("mix2_out", 2)
            norm(4, "ffn2", add_out(4, 1.0, FIRST["ffn2_up"]))
            swiglu_mul("ffn2")
            norm(5, "ple", add_out(5, 0.5, FIRST["ple_gate"]))
            run_ahead("ple_gate")
            dve.wait_ge(S("ple_hi"), 1)
            dve.tensor_tensor(p_lo[:, :, :], bank(0, 2), p_hi[:, :, :], ALU.subtract).then_inc(S("ple_lo"), 1)
            dve.wait_ge(S("ple_small"), 64)
            dve.wait_ge(unit_used, FIRST["ple_proj"])
            for m in range(NHALF):
                for c in range(2):
                    cc = slice(c * 512, (c + 1) * 512)
                    dve.tensor_tensor(gsig[:, m, cc], pb[4 + 2 * m + c][:, :], row_ple[:, cc],
                                      ALU.add).then_inc(S("ple_g"), 1)
            dve.wait_ge(unit_used, UNITS)
            for m in range(NHALF):
                dve.wait_ge(S("ple_sig"), m + 1)
                for c in range(2):
                    cc = slice(c * 512, (c + 1) * 512)
                    ins = dve.tensor_tensor(gsig[:, m, cc], pb[2 * m + c][:, :], gsig[:, m, cc], ALU.mult)
                link(ins)
                for c in range(2):
                    cc = slice(c * 512, (c + 1) * 512)
                    dve.tensor_tensor(resid[:, m, cc], resid[:, m, cc], gsig[:, m, cc],
                                      ALU.add).then_inc(S("resid_done"), 1)
            for m in range(NHALF):
                norm_scale(6, m)
                dve.wait_ge(S("norm_xn"), 2 * 6 + m + 1)
                dve.tensor_tensor(xn[:, m, :], xn[:, m, :], row_fin[:, :], ALU.mult).then_inc(S("out_ready"), 1)


_NAMES = ("x", "positions", "w_in", "rw_w2", "rw_a2", "rw_g2", "w_branch_rw", "w_branch_ret", "w_out", "ffn_w_up",
          "ffn_w_down", "p_2", "ffn1_w_gate_2", "ffn1_w_up_2", "ffn1_w_down_2", "w_in_2", "gm_w_s_2", "dt_bias_2",
          "a_log_2", "d_skip_2", "w_out_2", "ffn2_w_gate_2", "ffn2_w_up_2", "ffn2_w_down_2", "ple_w_gate_2",
          "ple_w_proj_2")


def laid_out(inputs):
    arrays = {}
    for name in _NAMES:
        a = np.asarray(inputs[name])
        keep = 1 if name in ("dt_bias_2", "a_log_2", "d_skip_2") else None
        if name == "positions":
            a = np.ascontiguousarray(a.reshape(NHALF, P).T)
        elif name == "p_2":
            a = a.reshape(T, -1)
        elif keep is None:
            a = a.reshape(a.shape[1:])
        arrays[name] = np.ascontiguousarray(a)
    packed = {
        "mix_pre": "norm_mix_pre", "ffn_pre": "norm_ffn_pre", "mu": "rw_mu", "w0": "rw_w0", "a0": "rw_a0",
        "k_k": "rw_k_k", "k_a": "rw_k_a", "r_k": "rw_r_k", "lnx_w": "rw_lnx_w", "lnx_b": "rw_lnx_b",
        "conv1_w": "ffn_conv_w", "conv1_b": "ffn_conv_b", "ffn1": "ffn1_norm_2", "mix2": "mix_norm_2",
        "gm_b": "gm_b_s_2", "gm_out": "gm_out_norm_2", "conv2_w": "conv_w_2", "conv2_b": "conv_b_2",
        "ssm": "ssm_norm_2", "ffn2": "ffn2_norm_2", "ple": "ple_norm_2",
    }
    arrays["cols"] = np.ascontiguousarray(
        np.concatenate([np.asarray(inputs[packed[name]]).reshape(n, P) for name, n in COLS]).T)
    rows = {"mix_post": "norm_mix_post", "ffn_post": "norm_ffn_post", "gm_ln_g": "gm_ln_g_2", "gm_ln_b": "gm_ln_b_2",
            "ple_b": "ple_b_gate_2", "final": "final_norm_2"}
    arrays["rows"] = np.ascontiguousarray(np.stack([np.asarray(inputs[rows[name]]).reshape(D) for name in ROWS]))
    arrays["consts"] = shape_constants()
    return arrays


def kernel(**inputs):
    import concourse.bacc as bacc
    from concourse.bass_utils import run_bass_kernel_spmd

    arrays = laid_out(inputs)
    nc = bacc.Bacc("TRN2", target_bir_lowering=False, num_devices=1)
    io = {name: nc.dram_tensor(f"in_{name}", a.shape, mybir.dt.from_np(a.dtype), kind="ExternalInput").ap()
          for name, a in arrays.items()}
    out = nc.dram_tensor("out", (T, D), F32, kind="ExternalOutput").ap()
    two_layers(nc, io, out)
    r = run_bass_kernel_spmd(nc, [{f"in_{n}": a for n, a in arrays.items()}], core_ids=[0])
    return r.results[0]["out"].reshape(1, T, D)
```

```python
from contextlib import ExitStack

import numpy as np

import concourse.bass as bass
from concourse import mybir

F32 = mybir.dt.float32
F32R = mybir.dt.float32r
I32 = mybir.dt.int32
ACT = mybir.ActivationFunctionType
ALU = mybir.AluOpType
AX_X = mybir.AxisListType.X

P = 128
T = 256
D = 1024
KD = D // P
NHALF = T // P
RW = 512
RW_COLS = 1792
RET_COLS = 3072
FF = 2816
KF = FF // P
PAIRS = FF // 256
XBC = 1536
DT_COL = 4608
RING = 4
UNIT = 2048

STREAM = (
    ("rw", RW_COLS // 256), ("ret", RET_COLS // 256), ("gates", 2 * D // 256),
    ("branch_rw", 2), ("branch_ret", 4), ("mix_out", 4), ("conv_up", 2 * PAIRS), ("conv_down", PAIRS),
    ("ffn1_up", 2 * PAIRS), ("ffn1_down", PAIRS), ("v", 4), ("u", 4), ("xbc", XBC // 256), ("z", 4),
    ("mix2_out", 8),
    ("ffn2_up", 2 * PAIRS), ("ple_proj", 1), ("ffn2_down", PAIRS), ("ple_gate", 4),
)
FIRST = {}
UNITS = 0
for _name, _n in STREAM:
    FIRST[_name] = UNITS
    UNITS += _n

AGAIN = {
    "dt_adt": ("rw_sq", 1), "dt_cs": ("rw_kk0", 1), "dt_e": ("rw_norm", 1), "dt_ecs": ("rw_normrt", 1),
    "dt_mm": ("rw_rk", 1), "dt_na": ("rw_abkr", 1), "dt_used": ("rw_bonus", 1), "dt_whi": ("rw_gnv", 1),
    "dt_wlo": ("rw_gnrt", 1), "gm_mix": ("rw_yn", 1), "gm_ms": ("rw_yg", 1), "gm_rt": ("rw_yhi", 1),
    "gm_sq": ("rw_init", 1), "gm_v": ("rw_lora", 2), "gm_var": ("rw_css", 2), "gm_wt": ("rw_sums", 2),
    "gm_wtc": ("rw_z", 3), "gm_y": ("rw_e", 3), "gm_ya": ("rw_sw", 4), "ssm_att": ("rw_as", 4),
    "ssm_bmc": ("rw_g", 2), "ssm_cb": ("rw_v", 2), "ssm_diff": ("rw_fd", 14), "ssm_exp": ("rw_tr", 2),
    "ssm_min": ("rw_l", 1), "ssm_ms": ("rw_lt", 2), "ssm_off": ("rw_xa", 1), "ssm_row": ("rw_xac", 2),
    "ssm_rt": ("rw_f", 7), "ssm_sq": ("rw_up", 3), "ssm_state": ("rw_xmv", 1), "ssm_stc": ("rw_w", 2),
    "ssm_xds": ("rw_yt", 2),
}

WEAVE = {
    "pm": 4, "low_rank": 4, "norms": 8, "keys": 8, "l": 4, "t0": 0, "t1": 1, "x1": 1, "t2": 1, "x2": 3,
    "t3": 1, "x3": 2, "t4": 2, "x4": 2, "t5": 2, "x5": 1, "xa": 1, "xmv": 2, "s0": 1, "u1": 0, "s1": 4,
    "u2": 1, "s2": 1, "u3": 1, "y": 4, "y2": 2, "yt": 3, "qk": 5, "sc0": 2, "o0": 3, "o1": 3,
    "stats": 4, "rest0": 3, "rest1": 4,
}
BEFORE = {}
_n = 0
for _step in WEAVE:
    BEFORE[_step] = _n
    _n += WEAVE[_step]
assert _n == 4 * (12 + 8 + 2), _n
POOL_SPLITS = (("low_rank", "norms", "keys"), ("xa", "xmv", "s0", "u1", "s1", "u2", "s2"))

WEAVE_2 = {"xs": 5, "bm": 5, "st": 6, "row": 3, "a0": 2, "a1": 2, "a2": 2, "a3": 0, "f0": 4, "f1": 3}
POOL_SPLITS_2 = ("xs", "bm", "st", "row", "a0", "a1", "a2", "a3")
BEFORE_2 = {}
_n = 0
for _step in WEAVE_2:
    BEFORE_2[_step] = _n
    _n += WEAVE_2[_step]
assert _n == 4 * (4 + 4), _n

COLS = (
    ("mix_pre", 8), ("ffn_pre", 8), ("mu", 14), ("w0", 4), ("a0", 4), ("k_k", 4), ("k_a", 4),
    ("r_k", 4), ("lnx_w", 4), ("lnx_b", 4), ("conv1_w", 3 * 44), ("conv1_b", 44), ("ffn1", 8),
    ("mix2", 8), ("gm_b", 8), ("gm_out", 8), ("conv2_w", 4 * 12), ("conv2_b", 12), ("ssm", 8),
    ("ffn2", 8), ("ple", 8),
)
COL = {}
NCOL = 0
for _name, _n in COLS:
    COL[_name] = NCOL
    NCOL += _n

ROWS = ("mix_post", "ffn_post", "gm_ln_g", "gm_ln_b", "ple_b", "final")

CHUNK = 64
LEVELS = 6
KIND = {"ident": 0, "causal": 1, "eye": 2, "tri": 3, "heads": 4, "level": 5, "decay": 5 + LEVELS // 2,
        "qdecay": 5 + LEVELS // 2 + 8, "small": 5 + LEVELS // 2 + 8 + 4}
NKIND = KIND["small"] + 1
SMALL_KDECAY, SMALL_INV = 0, 8
DECAY_SCALE = float(np.exp(-0.5))
RMS_EPS = 1e-6
TWO_PI = 2 * np.pi
PI_A = 6.28125
PI_B = 2029 / 2 ** 20
PI_C = float(TWO_PI - PI_A - PI_B)
ROUND = 12582912.0
PI_F32 = 3.1415925


AHEAD = RING - 1
TURN = RING


def shape_constants():
    s = np.arange(P)[:, None]
    t = np.arange(P)[None, :]
    sc, tc = s % CHUNK, np.arange(CHUNK)[None, :]
    out = np.zeros((P, NKIND, P), np.float32)
    out[:, KIND["ident"]] = np.eye(P)
    out[:, KIND["causal"], :CHUNK] = sc < tc
    out[:, KIND["causal"], CHUNK:] = sc <= tc
    out[:, KIND["eye"], :CHUNK] = sc == tc
    out[:, KIND["tri"]] = s <= t
    out[:, KIND["heads"]] = (s // CHUNK) == (t // CHUNK)
    for j in range(LEVELS):
        b = 1 << j
        out[:, KIND["level"] + j // 2, j % 2 * CHUNK:(j % 2 + 1) * CHUNK] = -1.0 * (
            (sc // (2 * b) == tc // (2 * b)) & (sc // b % 2 == 0) & (tc // b % 2 == 1))
    head = np.arange(8, dtype=np.float32)
    log_gamma = np.log1p(-np.exp2(np.float32(-5.0) - head)).astype(np.float32)
    rel = (t - s).astype(np.float32)
    for h in range(8):
        out[:, KIND["decay"] + h] = np.where(rel >= 0, np.exp(np.maximum(rel, 0) * log_gamma[h]), 0) * 0.125
    for tile in range(4):
        for q in range(2):
            row = np.exp((np.arange(P, dtype=np.float32) + 1) * log_gamma[2 * tile + q])
            out[64 * q:64 * q + 64, KIND["qdecay"] + tile] = row[None, :]
    small = out[:, KIND["small"]]
    small[:, SMALL_KDECAY:SMALL_KDECAY + 8] = np.exp((P - 1 - s).astype(np.float32) * log_gamma[None, :]) * 0.125
    small[:, SMALL_INV:SMALL_INV + 32] = np.float32(10000.0) ** (-np.arange(32, dtype=np.float32) / 32)
    return out.reshape(P, NKIND * P)


def two_layers(nc, io, out):
    x_d = io["x"]
    w_in, w_in_2 = io["w_in"], io["w_in_2"]
    w_up = io["ffn_w_up"]

    def k_rows(w):
        return w.rearrange("(k p) n -> p k n", p=P)

    w_in_k, w_in2_k, w_up_k = k_rows(w_in), k_rows(w_in_2), k_rows(w_up)
    brw_k, bret_k = k_rows(io["w_branch_rw"]), k_rows(io["w_branch_ret"])
    pair_k = {
        "conv_up": (w_up_k, w_up_k[:, :, FF:]),
        "ffn1_up": (k_rows(io["ffn1_w_gate_2"]), k_rows(io["ffn1_w_up_2"])),
        "ffn2_up": (k_rows(io["ffn2_w_gate_2"]), k_rows(io["ffn2_w_up_2"])),
    }
    row_w = {
        "mix_out": io["w_out"], "conv_down": io["ffn_w_down"], "ffn1_down": io["ffn1_w_down_2"],
        "mix2_out": io["w_out_2"], "ffn2_down": io["ffn2_w_down_2"], "ple_gate": io["ple_w_gate_2"],
        "ple_proj": io["ple_w_proj_2"],
    }

    ctx = ExitStack()
    with ctx:
        def sb(name, shape, dt=F32, scope=ctx):
            return scope.enter_context(nc.sbuf_tensor(name, shape, dt))

        sems = {}

        def sem(name):
            name = AGAIN.get(name, (name, 0))[0]
            if name not in sems:
                sems[name] = ctx.enter_context(nc.semaphore(name))
            return sems[name]

        w_hi = sb("w_hi", [P, RING, UNIT], F32R)
        x_hi = sb("x_hi", [P, KD, T], F32R)
        x_lo = sb("x_lo", [P, KD, T], F32R)
        resid = sb("resid", [P, NHALF, D])
        cols = sb("cols", [P, NCOL])
        consts = sb("consts", [P, 5, P])
        norm_s = sb("norm_s", [P, 32])
        ident = consts[:, 0, :]
        wr = ExitStack()
        w_raw = sb("w_raw", [P, RING, UNIT], F32, wr)
        wr.close()
        w_lo = sb("w_lo", [P, RING, UNIT], F32R)

        nx = ExitStack()
        xn = sb("xn", [P, NHALF, D], F32, nx)
        nx.close()

        m1 = ExitStack()
        yrw_hi = sb("yrw_hi", [P, 4, T], F32R, m1)
        yrw_lo = sb("yrw_lo", [P, 4, T], F32R, m1)
        q_rm = sb("q_rm", [P, NHALF, RW], F32, m1)
        kr_rm = sb("kr_rm", [P, NHALF, RW], F32, m1)
        vr_rm = sb("vr_rm", [P, NHALF, D], F32, m1)
        sg_rm = sb("sg_rm", [P, NHALF, D], F32, m1)
        sig_rw = sb("sig_rw", [P, 8, T], F32, m1)
        trig = sb("trig", [P, 6, NHALF, 32], F32, m1)
        posf = sb("posf", [P, 2, NHALF], F32, m1)
        posi = sb("posi", [P, NHALF], I32, m1)
        small = sb("small", [P, P], F32, m1)
        ra = ExitStack()
        pm = sb("pm", [P, 14, T], F32, ra)
        g_t = sb("g_t", [P, 4, T], F32, ra)
        bonus = sb("bonus", [P, 4, T], F32, ra)
        a_f = sb("a_f", [P, 4, T], F32, ra)
        b_f = sb("b_f", [P, 4, T], F32, ra)
        pc = sb("pc", [P, 4, 4], F32, ra)
        lvl = sb("lvl", [P, LEVELS, CHUNK], F32, ra)
        rb = ExitStack()
        e_pos = sb("e_pos", [P, 4, T], F32, rb)
        css = sb("css", [P, 4, T], F32, rb)
        kk = sb("kk", [P, 4, T], F32, rb)
        a_s = sb("a_s", [P, 4, T], F32, rb)
        t1 = sb("t1", [P, 4, T], F32, rb)
        sw = sb("sw", [P, 4, T], F32, rb)
        psh_flat = sb("psh", [P, 4 * (T + 1)], F32, rb)
        cmask = sb("cmask", [P, 4, T], F32, rb)
        act_w = sb("act_w", [P, 2, T], F32, rb)
        omka = sb("omka", [P, 4], F32, rb)
        small_w = sb("small_w", [P, 2, RW], F32, rb)
        psh = psh_flat[:, :].rearrange("p (b i n) -> p b i n", b=2, i=2)
        t2 = psh_flat[:, 0:4 * T].rearrange("p (i n) -> p i n", i=4)
        rb.close()
        rc = ExitStack()
        a_rm = sb("a_rm", [P, NHALF, RW], F32, rc)
        b_rm = sb("b_rm", [P, NHALF, RW], F32, rc)
        k_rm = sb("k_rm", [P, NHALF, RW], F32, rc)
        lm = sb("lm", [P, 16, CHUNK], F32, rc)
        xi = sb("xi", [P, 16, CHUNK], F32, rc)
        tp = sb("tp", [P, 16, CHUNK], F32, rc)
        xa = sb("xa", [P, 4, T], F32, rc)
        v_rm = sb("v_rm", [P, NHALF, RW], F32, rc)
        gm = sb("gm", [P, 16, CHUNK], F32, rc)
        st = sb("st", [P, 4, 4, 64], F32, rc)
        stmp = sb("stmp", [P, 4, 64], F32, rc)
        xt = resid[:, 0, :].rearrange("p (g n) -> p g n", g=16)
        g1 = xn[:, 0, :].rearrange("p (g n) -> p g n", g=16)
        g2 = xn[:, 1, :].rearrange("p (g n) -> p g n", g=16)
        wv = a_rm[:, :, :].rearrange("p h (g n) -> p (h g) n", g=8)
        lt = pm[:, 8:12, :].rearrange("p a (b n) -> p (a b) n", n=CHUNK)
        ys_v = pm[:, 8:12, :].rearrange("p (m a) n -> p m (a n)", m=2)
        rc.close()
        rd = ExitStack()
        yn = sb("yn", [P, NHALF, RW], F32, rd)
        yq = sb("yq", [P, NHALF, RW], F32, rd)
        gn = sb("gn", [P, 4, 16], F32, rd)
        ytmp = sb("ytmp", [P, 4, T], F32, rd)
        rd.close()
        ra.close()
        yret_hi = sb("yret_hi", [P, 8, T], F32R, m1)
        yret_lo = sb("yret_lo", [P, 8, T], F32R, m1)
        rot = resid[:, 1, 0:768].rearrange("p (k n) -> p k n", k=3)
        q_f = resid[:, 0, :].rearrange("p (a n) -> p a n", a=4)
        k_f = resid[:, 1, :].rearrange("p (a n) -> p a n", a=4)
        qd_f = sb("qd_f", [P, 4, P], F32, m1)
        rstate = sb("rstate", [P, 4, P], F32, m1)
        decay = sb("decay", [P, 12, P], F32, m1)
        ret_s = sb("ret_s", [P, 12, 16], F32, m1)
        sco = sb("sco", [P, 2, 4, P], F32, m1)
        sig_ret = sb("sig_ret", [P, 8, T], F32, m1)
        row_mix = sb("row_mix", [P, D], F32, m1)
        merged = sb("merged", [P, 8, T], F32, m1)
        mtmp = sb("mtmp", [P, 2, 2, T], F32, m1)
        m1.close()

        ff = ExitStack()
        h_hi = sb("h_hi", [P, KF, T], F32R, ff)
        h_lo = sb("h_lo", [P, KF, T], F32R, ff)
        gate = sb("gate", [P, 2, 512], F32, ff)
        hid = sb("hid", [P, 2, 512], F32, ff)
        cgate = sb("cgate", [P, 2, 2, T], F32, ff)
        cval = sb("cval", [P, 2, 2, T], F32, ff)
        row_ffn = sb("row_ffn", [P, D], F32, ff)
        p_hi = sb("p_hi", [P, 2, T], F32R, ff)
        p_lo = sb("p_lo", [P, 2, T], F32R, ff)
        p_rm = sb("p_rm", [P, NHALF, 256], F32, ff)
        proj = sb("proj", [P, NHALF, D], F32, ff)
        gsig = sb("gsig", [P, NHALF, D], F32, ff)
        row_ple = sb("row_ple", [P, D], F32, ff)
        row_fin = sb("row_fin", [P, D], F32, ff)
        ff.close()

        m2 = ExitStack()
        y2_hi = sb("y2_hi", [P, 16, T], F32R, m2)
        y2_lo = sb("y2_lo", [P, 16, T], F32R, m2)
        z_s = sb("z_s", [P, NHALF, D], F32, m2)
        dt_s = sb("dt_s", [P, 12, NHALF, 16], F32, m2)
        rows16 = sb("rows16", [P, 3, 16], F32, m2)
        w_dt = sb("w_dt", [P, KD, 16], F32, m2)
        w_dt_hi = sb("w_dt_hi", [P, KD, 16], F32R, m2)
        w_dt_lo = sb("w_dt_lo", [P, KD, 16], F32R, m2)
        u_rm = sb("u_rm", [P, NHALF, D], F32, m2)
        vg_rm = sb("vg_rm", [P, NHALF, D], F32, m2)
        ws_raw = sb("ws_raw", [P, 8, P], F32, m2)
        ws_t = sb("ws_t", [P, 8, P], F32, m2)
        gm_s = sb("gm_s", [P, 48], F32, m2)
        row_ln_g = sb("row_ln_g", [P, D], F32, m2)
        row_ln_b = sb("row_ln_b", [P, D], F32, m2)
        xbc_f = sb("xbc_f", [P, 12, T], F32, m2)
        xs_rm = sb("xs_rm", [P, NHALF, D], F32, m2)
        xd_rm = sb("xd_rm", [P, NHALF, D], F32, m2)
        bm_rm = sb("bm_rm", [P, 256], F32, m2)
        cb = sb("cb", [P, 4, P], F32, m2)
        sstate = sb("sstate", [P, 2, 512], F32, m2)
        att = (ws_raw, ws_t)
        y_rm = xbc_f[:, 0:8, :].rearrange("p (h a) n -> p h (a n)", h=2)
        m2.close()
        pb = [ctx.enter_context(nc.psum_tensor(f"bank{i}", [P, 512], F32)) for i in range(8)]

        def bank(i, a):
            return pb[i][:, :].rearrange("p (a n) -> p a n", a=a)

        def col(name, k, n=1):
            return cols[:, COL[name] + k:COL[name] + k + n]

        def at(n, it, per):
            return n if it is None else it * per + n

        def in_turns(eng, units, body):
            turns = units // TURN if units >= 2 * TURN else 0
            if turns:
                with eng.Fori(0, turns) as it:
                    for j in range(TURN):
                        body(j, it)
            for j in range(TURN * turns, units):
                body(j, None)

        raw_landed = [sem(f"raw_landed{i}") for i in range(RING)]
        hi_split, lo_split, unit_used = sem("hi_split"), sem("lo_split"), sem("unit_used")
        S = sem
        QUARTERS = [(m, c) for m in range(NHALF) for c in range(2)]
        OUT_LAST = [FIRST[name] for name in ("conv_up", "ffn1_up", "v", "ffn2_up", "ple_gate")] + [UNITS]

        def out_part(eng, n, m, c):
            if (m, c) != QUARTERS[-1]:
                eng.wait_ge(S("out_part"), 3 * (n - 1) + 2 * m + c + 1)
            else:
                eng.wait_ge(unit_used, OUT_LAST[n - 1])

        kc = io["consts"].rearrange("p (k n) -> p k n", n=P)
        block = ctx.enter_context(nc.Block())

        @block.sync
        def _(sp):
            for m in range(NHALF):
                sp.dma_start(resid[:, m, :], x_d[m * P:(m + 1) * P, :]).then_inc(S(f"x_landed{m}"), 16)
            sp.dma_start(ident, kc[:, 0, :]).then_inc(S("ident_landed"), 16)

            def load(u, it, nk, src):
                if u >= RING:
                    sp.wait_ge(unit_used, at(u - RING + 1, it, 4))
                dst = w_raw[:, u % RING, :].rearrange("p (k n) -> p k n", k=nk)
                sp.dma_start(dst, src).then_inc(raw_landed[u % RING], 16)
                if u == 0:
                    sp.dma_start(cols[:, :], io["cols"]).then_inc(S("cols_landed"), 16)
                if u == 1:
                    sp.dma_start(consts[:, 1:5, :], kc[:, 1:5, :]).then_inc(S("consts_landed"), 16)

            def columns(name, w, first, nk, width):
                def body(j, it):
                    per_block = KD // nk
                    c = at(first + (j // per_block) * width, it, 4 // per_block * width)
                    k = j % per_block * nk
                    load(FIRST[name] + j, it, nk, w[:, k:k + nk, bass.ds(c, width)])
                in_turns(sp, dict(STREAM)[name], body)

            def pairs(name):
                def body(j, it):
                    load(FIRST[name] + j, it, 8, pair_k[name][j % 2][:, :, bass.ds(at(j // 2 * 256, it, 512), 256)])
                in_turns(sp, 2 * PAIRS, body)

            def rows(name):
                def body(j, it):
                    src = row_w[name][bass.ds(at(j * 256, it, 1024), 256), :]
                    load(FIRST[name] + j, it, 2, src.rearrange("(k p) n -> p k n", p=P))
                in_turns(sp, dict(STREAM)[name], body)

            columns("rw", w_in_k, 0, 8, 256)
            columns("ret", w_in_k, RW_COLS, 4, 512)
            columns("gates", w_in_k, RW_COLS + RET_COLS, 8, 256)
            for j in range(2):
                load(FIRST["branch_rw"] + j, None, 4, brw_k[:, :, j * 512:(j + 1) * 512])
            columns("branch_ret", bret_k, 0, 8, 256)
            rows("mix_out")
            pairs("conv_up")
            rows("conv_down")
            pairs("ffn1_up")
            rows("ffn1_down")
            columns("v", w_in2_k, D, 4, 512)
            columns("u", w_in2_k, 0, 4, 512)
            columns("xbc", w_in2_k, 3 * D, 8, 256)
            columns("z", w_in2_k, 2 * D, 4, 512)
            rows("mix2_out")
            pairs("ffn2_up")
            rows("ple_proj")
            rows("ffn2_down")
            rows("ple_gate")
            for n, (m, c) in enumerate(QUARTERS):
                cc = slice(c * 512, (c + 1) * 512)
                sp.wait_ge(S("out_ready"), n + 1)
                sp.dma_start(out[m * P:(m + 1) * P, cc], xn[:, m, cc]).then_inc(S("out_stored"), 16)
            sp.wait_ge(S("out_stored"), 64)

        @block.gpsimd
        def _(pool):
            def row_of(name):
                return io["rows"][ROWS.index(name):ROWS.index(name) + 1, :].to_broadcast([P, D])

            steps = [0]

            def link(ins):
                steps[0] += 1
                ins.then_inc(S("pool_step"), 1)
                pool.wait_ge(S("pool_step"), steps[0])

            def rsqrt(dst, src, ready, count, signal):
                pool.wait_ge(S(ready), count)
                pool.tensor_tensor(dst, src, norm_s[:, 12:12 + src.shape[-1]], ALU.pow).then_inc(S(signal), 1)

            def norm(n, post=None):
                for m in range(NHALF):
                    if post is not None:
                        rsqrt(norm_s[:, 24 + m:25 + m], norm_s[:, 22 + m:23 + m], "post_ms", 2 * post + m + 1, "post_rt")
                    rsqrt(norm_s[:, 6 + m:7 + m], norm_s[:, 2 + m:3 + m], "norm_ms", 2 * n + m + 1, "norm_rt")

            link(pool.memset(norm_s[:, 12:16], -0.5))
            norm(0)
            pool.dma_start(small[:, :], kc[:, KIND["small"], :]).then_inc(S("trig_small"), 16)
            pool.dma_start(posi[:, :], io["positions"]).then_inc(S("trig_small"), 16)
            pool.dma_start(lvl[:, :, :], kc[:, KIND["level"]:KIND["level"] + LEVELS // 2, :].rearrange(
                "p a (b n) -> p (a b) n", n=CHUNK)).then_inc(S("rw_small"), 16)
            pool.dma_start(small_w[0:64, 0, :], io["rw_w2"]).then_inc(S("rw_small"), 16)
            pool.dma_start(small_w[64:128, 0, :], io["rw_a2"]).then_inc(S("rw_small"), 16)
            pool.dma_start(small_w[:, 1, :], io["rw_g2"]).then_inc(S("rw_small"), 16)
            def split_behind(before, steps, first="ret", quarters=BEFORE):
                u = FIRST[first] + before // 4 + AHEAD
                for step in steps:
                    while u < FIRST[first] + quarters[step] // 4 + AHEAD:
                        pool.wait_ge(hi_split, u + 1)
                        pool.wait_ge(lo_split, u)
                        pool.tensor_tensor(w_lo[:, u % RING, :], w_raw[:, u % RING, :], w_hi[:, u % RING, :],
                                           ALU.subtract).then_inc(lo_split, 1)
                        u += 1

            split_behind(-4, POOL_SPLITS[0])
            pool.wait_ge(S("rw_small"), 64)
            pool.wait_ge(S("rw_lt"), 2)
            for j in range(LEVELS):
                if j:
                    pool.wait_ge(S("rw_t"), j)
                if j == 1:
                    pool.wait_ge(S("rw_xd"), 1)
                pool.tensor_tensor(lm[:, :, :], lt, lvl[:, j:j + 1, :].to_broadcast([P, 16, CHUNK]),
                                   ALU.mult).then_inc(S("rw_lm"), 1)
            split_behind(BEFORE["x5"], POOL_SPLITS[1])
            pool.wait_ge(S("ret_sin"), 1)
            for i, src in enumerate((q_rm, kr_rm)):
                pool.wait_ge(S("ret_free"), i + 1)
                for m in range(NHALF):
                    z = src[:, m, :].rearrange("p (h two d) -> p h two d", two=2, d=32)
                    z1, z2 = z[:, :, 0, :], z[:, :, 1, :]
                    sin, cos = (trig[:, k, m:m + 1, :].to_broadcast([P, 8, 32]) for k in (4, 5))
                    a, b, c = (rot[:, k, :].rearrange("p (h d) -> p h d", h=8) for k in range(3))
                    pool.tensor_tensor(a, z1, cos, ALU.mult)
                    pool.tensor_tensor(b, z2, sin, ALU.mult)
                    link(pool.tensor_tensor(c, z1, sin, ALU.mult))
                    link(pool.tensor_tensor(z1, a, b, ALU.subtract))
                    link(pool.tensor_tensor(a, z2, cos, ALU.mult))
                    link(pool.tensor_tensor(z2, c, a, ALU.add))
                pool.sem_inc(S("ret_rot"), 1)
            pool.wait_ge(S("rw_done"), 1)
            pool.dma_start(decay[:, :, :], kc[:, KIND["decay"]:KIND["small"], :]).then_inc(S("ret_small"), 16)
            pool.dma_start(row_mix[:, :], row_of("mix_post")).then_inc(S("mix_row"), 16)
            pool.wait_ge(S("ret_tr"), 4)
            k0 = kr_rm[:, 0, :].rearrange("p (h d) -> p h d", h=8)
            pool.tensor_tensor(k0, k0, small[:, SMALL_KDECAY:SMALL_KDECAY + 8].unsqueeze(2).to_broadcast([P, 8, 64]),
                               ALU.mult).then_inc(S("ret_kd"), 1)
            pool.wait_ge(S("ret_done"), 2)
            for m in range(NHALF):
                pool.dma_start(resid[:, m, :], x_d[m * P:(m + 1) * P, :]).then_inc(S("mix_row"), 16)

            def split_hidden(name):
                def body(j, it):
                    p, b = at(j, it, 4), j % 2
                    pool.wait_ge(S(name + "_hid"), at(j + 3, it, 4))
                    pool.tensor_copy(h_hi[:, bass.ds(at(2 * j, it, 8), 2), :],
                                     hid[:, b, :].rearrange("p (i n) -> p i n", i=2)).then_inc(S(name + "_hhi"), 1)
                    pool.wait_ge(S(name + "_hhi"), at(j + 1, it, 4))
                    pool.tensor_tensor(h_lo[:, bass.ds(at(2 * j, it, 8), 2), :],
                                       hid[:, b, :].rearrange("p (i n) -> p i n", i=2),
                                       h_hi[:, bass.ds(at(2 * j, it, 8), 2), :],
                                       ALU.subtract).then_inc(S(name + "_hlo"), 1)
                pool.sem_inc(S(name + "_hlo"), 2)
                in_turns(pool, PAIRS, body)

            norm(1, post=0)
            pool.wait_ge(S("norm_tr"), 8)
            pool.dma_start(row_ffn[:, :], row_of("ffn_post")).then_inc(S("ffn_row"), 16)
            split_hidden("conv")
            norm(2, post=1)
            split_hidden("ffn1")
            norm(3)
            pool.wait_ge(S("norm_tr"), 16)
            pool.dma_start(w_dt[:, :, :], w_in2_k[:, :, DT_COL:DT_COL + 16]).then_inc(S("dt_small"), 16)
            for i, name in enumerate(("dt_bias_2", "a_log_2", "d_skip_2")):
                pool.dma_start(rows16[:, i, :], io[name].to_broadcast([P, 16])).then_inc(S("dt_small"), 16)
            pool.dma_start(ws_raw[:, :, :], io["gm_w_s_2"].rearrange("h t s -> t h s")).then_inc(S("gm_small"), 16)
            pool.dma_start(row_ln_g[:, :], row_of("gm_ln_g")).then_inc(S("gm_small"), 16)
            pool.dma_start(row_ln_b[:, :], row_of("gm_ln_b")).then_inc(S("gm_small"), 16)
            rsqrt(gm_s[:, 22:24], gm_s[:, 18:20], "gm_var", AGAIN["gm_var"][1] + 1, "gm_rt")
            pool.wait_ge(S("gm_small"), 48)
            for m in range(NHALF):
                pool.wait_ge(S("gm_vn"), m + 1)
                link(pool.tensor_tensor(vg_rm[:, m, :], vg_rm[:, m, :], row_ln_g[:, :], ALU.mult))
                pool.tensor_tensor(vg_rm[:, m, :], vg_rm[:, m, :], row_ln_b[:, :], ALU.add).then_inc(S("gm_v"), 1)
            rsqrt(gm_s[:, 30:32], gm_s[:, 26:28], "gm_ms", AGAIN["gm_ms"][1] + 1, "gm_rt")
            split_behind(-4, POOL_SPLITS_2, "z", BEFORE_2)
            rsqrt(dt_s[:, 11, 0, 12:16], dt_s[:, 11, 0, 4:8], "ssm_ms", AGAIN["ssm_ms"][1] + 1, "ssm_rt")
            norm(4)
            pool.wait_ge(S("norm_tr"), 20)
            for m in range(NHALF):
                pool.dma_start(p_rm[:, m, :], io["p_2"][m * P:(m + 1) * P, :]).then_inc(S("ple_small"), 16)
            pool.dma_start(row_ple[:, :], row_of("ple_b")).then_inc(S("ple_small"), 16)
            pool.dma_start(row_fin[:, :], row_of("final")).then_inc(S("ple_small"), 16)
            split_hidden("ffn2")
            norm(5)
            norm(6)

        @block.tensor
        def _(pe):
            def mm3_t(dst, w_slot, c0, x_h, x_l, first, last):
                for n, (w, x) in enumerate(((w_hi, x_h), (w_hi, x_l), (w_lo, x_h))):
                    mm = pe.matmul(dst, w[:, w_slot, c0:c0 + P], x, start=(first and n == 0), stop=(last and n == 2))
                return mm

            def unit_t(u, it, nk, x_h, x_l, banks, part=None, ready=None):
                if not part:
                    pe.wait_ge(lo_split, at(u + 1, it, 4))
                tiles = [(c, k) for c in range(UNIT // nk // P) for k in range(nk)]
                for c, k in tiles if part is None else tiles[4 * part:4 * part + 4]:
                    if ready and c == 0:
                        ready(k)
                    mm = mm3_t(pb[banks[c // 2]][:, c % 2 * T:c % 2 * T + T], u % RING, k * (UNIT // nk) + c * P,
                               x_h[:, k, :], x_l[:, k, :], k == 0, k == nk - 1)
                if part in (None, 3):
                    mm.then_inc(unit_used, 1)

            def unit_r(u, it, nk, k0, ktotal, x_h, x_l, banks, part=None):
                if not part:
                    pe.wait_ge(lo_split, at(u + 1, it, 4))
                width = UNIT // nk
                tiles = [(k, m) for k in range(nk) for m in range(NHALF)]
                for k, m in tiles if part is None else tiles[part * nk // 2:(part + 1) * nk // 2]:
                    for c in range(width // 512):
                        for n, (x, w) in enumerate(((x_h, w_hi), (x_h, w_lo), (x_l, w_hi))):
                            o = k * width + c * 512
                            mm = pe.matmul(pb[banks[m][c]][:, :], x[:, k0 + k, m * P:(m + 1) * P],
                                           w[:, u % RING, o:o + 512], start=(k0 + k == 0 and n == 0),
                                           stop=(k0 + k == ktotal - 1 and n == 2))
                if part in (None, 3):
                    mm.then_inc(unit_used, 1)

            def fill(step):
                for n in range(BEFORE[step], BEFORE[step] + WEAVE[step]):
                    j, part = divmod(n, 4)
                    u = FIRST["ret"] + j
                    if part == 0:
                        def read(signal, count, unit):
                            assert 4 * (unit + 1) <= BEFORE[step], (step, j)
                            pe.wait_ge(S(signal), count)
                        if j < 12 and j % 2 == 0 and j >= 4:
                            read("ret_free", j // 2 - 1, j - 3)
                        elif 12 <= j < 16:
                            read("ret_free", 5 + (j - 12) // 2, 9 + (j - 12) // 2 * 2)
                        elif 16 <= j < 20:
                            read("gates_ev", j - 15, j - 4)
                        elif j >= 20:
                            pe.wait_ge(S("rw_done"), 1)
                            read("gates_ev", 6 + 2 * (j - 20), 17 + 2 * (j - 20))
                    if j < 12:
                        b = j // 2 % 2
                        unit_r(u, None, 4, 4 * (j % 2), 8, x_hi, x_lo, ((4 + 2 * b,), (5 + 2 * b,)), part)
                    elif j < 20:
                        unit_t(u, None, 8, x_hi, x_lo, (4 + j % 4,), part)
                    else:
                        unit_t(u, None, 4, yrw_hi, yrw_lo, (4 + 2 * (j - 20), 5 + 2 * (j - 20)), part)

            OUT = ((4, 5), (6, 7))

            def out_rows(name, ktotal, x_h, x_l, ready=None, first=0):
                units = dict(STREAM)[name]
                u = FIRST[name] + units - 2
                for j in range(first, units - 2):
                    if ready:
                        ready(j)
                    unit_r(FIRST[name] + j, None, 2, 2 * j, ktotal, x_h, x_l, OUT)
                if ready:
                    ready(units - 1)
                pe.wait_ge(lo_split, u + 2)
                for m, c in QUARTERS:
                    for k in range(4):
                        k_all = 2 * units - 4 + k
                        for n, (x, w) in enumerate(((x_h, w_hi), (x_h, w_lo), (x_l, w_hi))):
                            o = k % 2 * D + c * 512
                            mm = pe.matmul(pb[OUT[m][c]][:, :], x[:, k_all, m * P:(m + 1) * P],
                                           w[:, (u + k // 2) % RING, o:o + 512], start=False,
                                           stop=(k == 3 and n == 2))
                    if (m, c) != QUARTERS[-1]:
                        mm.then_inc(S("out_part"), 1)
                mm.then_inc(unit_used, 2)

            def turn_normed(src, signal):
                for b in range(4):
                    for i in range(2):
                        for m in range(NHALF):
                            k = 2 * b + i
                            tr = pe.transpose(pb[b][:, i * T + m * P:i * T + (m + 1) * P],
                                              src[:, m, k * P:(k + 1) * P], ident)
                    tr.then_inc(S(signal), 1)

            def norm(n):
                if n == 5:
                    pe.wait_ge(S("ple_proj"), 4)
                for m in range(NHALF):
                    for k in range(KD):
                        if k % 4 == 0:
                            pe.wait_ge(S("norm_xn"), 4 * n + 2 * m + k // 4 + 1)
                        tr = pe.transpose(pb[k // 2][:, k % 2 * T + m * P:k % 2 * T + (m + 1) * P],
                                          xn[:, m, k * P:(k + 1) * P], ident)
                        if m and k % 2:
                            tr.then_inc(S("norm_tr"), 1)

            def normed(n):
                return lambda k: pe.wait_ge(S("norm_lo"), 8 * n + max(k + 1, 2))

            pe.wait_ge(S("ident_landed"), 16)
            norm(0)
            for j in range(7):
                if j >= 4:
                    pe.wait_ge(S("rw_cp"), j - 3)
                unit_t(FIRST["rw"] + j, None, 8, x_hi, x_lo, (j % 4,), ready=None if j else normed(0))
            fill("pm")
            pe.wait_ge(S("consts_landed"), 16)
            pe.wait_ge(S("rw_small"), 64)
            pe.wait_ge(S("rw_lora"), 2)
            pe.wait_ge(S("rw_pm"), 14)

            def low_rank(first_bank, left, right):
                for t in range(4):
                    mm = pe.matmul(pb[first_bank + t // 2][:, t % 2 * T:t % 2 * T + T], left[:, t * P:(t + 1) * P],
                                   right, start=True, stop=True)
                mm.then_inc(S("rw_z"), 1)

            def head_sums(first_bank, src):
                for t in range(4):
                    mm = pe.matmul(pb[first_bank + t // 2][:, t % 2 * T:t % 2 * T + T], consts[:, KIND["heads"], :],
                                   src[:, t, :], start=True, stop=True)
                mm.then_inc(S("rw_sums"), 1)

            low_rank(0, small_w[0:64, 0, :], act_w[0:64, 0, :])
            pe.wait_ge(S("rw_sq"), 1)
            head_sums(2, t2)
            fill("low_rank")
            pe.wait_ge(S("rw_sw"), 4)
            low_rank(0, small_w[64:128, 0, :], pm[64:128, 12, :])
            pe.wait_ge(S("rw_norm"), 1)
            low_rank(2, small_w[:, 1, :], act_w[:, 1, :])
            fill("norms")

            def by_token(src, first_bank):
                for m in range(NHALF):
                    for t in range(4):
                        tr = pe.transpose(pb[first_bank + m][:, t * P:(t + 1) * P], src[:, t, m * P:(m + 1) * P],
                                          ident)
                return tr

            pe.wait_ge(S("rw_g"), 2)
            by_token(pm[:, 8:12, :], 2).then_inc(S("rw_tr"), 2)
            pe.wait_ge(S("rw_as"), 4)
            pe.wait_ge(S("rw_rk"), 1)
            head_sums(0, t1)
            fill("keys")

            HEADS = [(q, t) for q in range(2) for t in range(4)]
            BLOCKS = [(q, m, t) for q in range(2) for m in range(NHALF) for t in range(4)]

            def against(first_bank, left, right):
                for q, m, t in BLOCKS:
                    f = slice(64 * q, 64 * q + 64)
                    for e in range(2):
                        tok = slice(m * P + 64 * e, m * P + 64 * e + 64)
                        o = (4 * m + t) * 64
                        mm = pe.matmul(pb[first_bank + q][64 * e:64 * e + 64, o:o + 64], left[f, t, tok],
                                       right[f, t, tok], start=True, stop=True)
                return mm

            def of_block(x, q, m, t, e):
                return x[64 * e:64 * e + 64, 8 * q + 4 * m + t, :]

            def of_token(x, q, m, t, e):
                h = 2 * t + q
                return x[64 * e:64 * e + 64, m, h * 64:h * 64 + 64]

            def in_blocks(first_bank, left, right, start=True, stop=True):
                for q, m, t in BLOCKS:
                    for e in range(2):
                        o = (4 * m + t) * 64
                        mm = pe.matmul(pb[first_bank + q][64 * e:64 * e + 64, o:o + 64], left(q, m, t, e),
                                       right(q, m, t, e), start=start, stop=stop)
                return mm

            def blocks_of(x):
                return lambda *a: of_block(x, *a)

            def tokens_of(x):
                return lambda *a: of_token(x, *a)

            def eye(q, m, t, e):
                return consts[64 * e:64 * e + 64, KIND["eye"], 0:CHUNK]

            pe.wait_ge(S("rw_bonus"), 1)
            pe.wait_ge(S("rw_abkr"), 1)
            against(0, b_f, a_f).then_inc(S("rw_l"), 1)
            fill("l")
            for j in range(LEVELS):
                pe.wait_ge(S("rw_lm"), j + 1)
                if j:
                    pe.wait_ge(S("rw_xd"), j)
                in_blocks(0, blocks_of(lm), blocks_of(xi) if j else eye).then_inc(S("rw_t"), 1)
                if j == 0:
                    pe.wait_ge(S("rw_v"), 2)
                    mm = against(2, pm[:, 4:8, :], a_f)
                elif j == 1:
                    pe.wait_ge(S("rw_fd"), 2)
                    mm = by_token(pm[:, 4:8, :], 2)
                elif j == 2:
                    mm = by_token(a_f, 2)
                elif j == 3:
                    mm = by_token(b_f, 2)
                elif j == 4:
                    mm = in_blocks(2, blocks_of(gm), tokens_of(v_rm))
                else:
                    mm = against(2, b_f, pm[:, 0:4, :])
                mm.then_inc(S("rw_f"), 1)
                fill(f"t{j}")
                if j == 0:
                    continue
                pe.wait_ge(S("rw_tp"), 2 * j)
                pe.wait_ge(S("rw_fd"), 2 * j + 2)
                if j < LEVELS - 1:
                    in_blocks(2, blocks_of(xt), blocks_of(tp))
                in_blocks(0, blocks_of(tp), blocks_of(xt)).then_inc(S("rw_x"), 1)
                if j == LEVELS - 1:
                    against(2, pm[:, 4:8, :], pm[:, 0:4, :]).then_inc(S("rw_f"), 1)
                fill(f"x{j}")
            pe.wait_ge(S("rw_xd"), LEVELS)
            for q, m, t in BLOCKS:
                for e in range(2):
                    mm = pe.matmul(pb[e][64 * q:64 * q + 64, (4 * m + t) * 64:(4 * m + t) * 64 + 64],
                                   of_token(a_rm, q, m, t, e), of_block(xt, q, m, t, e), start=True, stop=True)
            mm.then_inc(S("rw_xa"), 1)
            fill("xa")
            pe.wait_ge(S("rw_fd"), 14)
            in_blocks(2, blocks_of(xt), blocks_of(gm)).then_inc(S("rw_xmv"), 1)
            fill("xmv")
            pe.wait_ge(S("rw_w"), 2)
            pe.wait_ge(S("rw_xac"), 2)
            for c in range(4):
                m, e = divmod(c, 2)
                tok = slice(64 * e, 64 * e + 64)
                if c:
                    pe.wait_ge(S("rw_st"), c)
                    for t in range(4):
                        for q in range(2):
                            f = slice(64 * q, 64 * q + 64)
                            mm = pe.matmul(pb[2 + q][tok, t * 64:t * 64 + 64], xa[f, t, c * 64:c * 64 + 64],
                                           st[f, c, t, :], start=True, stop=True)
                    mm.then_inc(S("rw_up"), 1)
                    fill(f"u{c}")
                    pe.wait_ge(S("rw_u"), c)
                if c < 3:
                    for q, t in HEADS:
                        dst = pb[0][64 * q:64 * q + 64, t * 64:t * 64 + 64]
                        pe.matmul(dst, of_token(b_rm, q, m, t, e), of_block(wv, q, m, t, e), start=True, stop=False)
                        mm = pe.matmul(dst, of_token(k_rm, q, m, t, e), of_token(v_rm, q, m, t, e), start=False,
                                       stop=True)
                    mm.then_inc(S("rw_s"), 1)
                    fill(f"s{c}")
            for q, m, t in BLOCKS:
                for e in range(2):
                    dst = pb[q][64 * e:64 * e + 64, (4 * m + t) * 64:(4 * m + t) * 64 + 64]
                    pe.matmul(dst, of_block(g2, q, m, t, e), of_token(v_rm, q, m, t, e), start=True, stop=False)
                    mm = pe.matmul(dst, of_block(g1, q, m, t, e), of_block(wv, q, m, t, e), start=False, stop=True)
            mm.then_inc(S("rw_yp"), 1)
            for q, t in HEADS:
                f = slice(64 * q, 64 * q + 64)
                for c in range(1, 4):
                    m, e = divmod(c, 2)
                    mm = pe.matmul(pb[2 + q][64 * e:64 * e + 64, (4 * m + t) * 64:(4 * m + t) * 64 + 64],
                                   pm[f, t, c * 64:c * 64 + 64], st[f, c, t, :], start=True, stop=True)
            mm.then_inc(S("rw_yp"), 1)
            fill("y")
            fill("y2")
            pe.wait_ge(S("rw_yn"), 1)
            for b in range(2):
                for i in range(2):
                    for m in range(NHALF):
                        tr = pe.transpose(pb[b][:, i * T + m * P:i * T + (m + 1) * P],
                                          yn[:, m, (2 * b + i) * P:(2 * b + i + 1) * P], ident)
                tr.then_inc(S("rw_yt"), 1)
            fill("yt")

            pe.wait_ge(S("rw_ln"), 4)
            for i, src in enumerate((q_rm, kr_rm)):
                pe.wait_ge(S("ret_rot"), i + 1)
                for b in range(2):
                    for t in (2 * b, 2 * b + 1):
                        for m in range(NHALF):
                            tr = pe.transpose(pb[2 * i + b][:, t % 2 * T + m * P:t % 2 * T + (m + 1) * P],
                                              src[:, m, t * P:(t + 1) * P], ident)
                    tr.then_inc(S("ret_tr"), 1)
            fill("qk")

            def scores(m):
                for t in range(4):
                    for q in range(2):
                        f = slice(64 * q, 64 * q + 64)
                        mm = pe.matmul(pb[2 + q][:, t * P:(t + 1) * P], k_f[f, t, m * P:(m + 1) * P],
                                       q_f[f, t, m * P:(m + 1) * P], start=True, stop=True)
                mm.then_inc(S("ret_s"), 1)

            pe.wait_ge(S("ret_qf"), 2)
            pe.wait_ge(S("ret_kf"), 2)
            scores(0)
            pe.wait_ge(S("ret_free"), 4)
            pe.wait_ge(S("ret_kd"), 1)
            for q, t in HEADS:
                h = 2 * t + q
                mm = pe.matmul(pb[0][64 * q:64 * q + 64, t * P:(t + 1) * P], kr_rm[:, 0, h * 64:h * 64 + 64],
                               vr_rm[:, 0, h * P:(h + 1) * P], start=True, stop=True)
            mm.then_inc(S("ret_r"), 1)
            fill("sc0")
            pe.wait_ge(S("ret_rc"), 1)
            for m in range(NHALF):
                pe.wait_ge(S("ret_sc"), 2 * m + 2)
                if m:
                    pe.wait_ge(S("ret_qd"), 1)
                for h in range(8):
                    q, t = h % 2, h // 2
                    dst = pb[2 * m + q][:, t * P:(t + 1) * P]
                    mm = pe.matmul(dst, sco[:, q, t, :], vr_rm[:, m, h * P:(h + 1) * P], start=True, stop=not m)
                    if m:
                        mm = pe.matmul(dst, qd_f[64 * q:64 * q + 64, t, :], rstate[64 * q:64 * q + 64, t, :],
                                       start=False, stop=True)
                mm.then_inc(S("ret_o"), 1)
                if m == 0:
                    scores(1)
                fill(f"o{m}")
            fill("stats")
            pe.wait_ge(S("ret_y"), 1)
            for b in range(4):
                for i in range(2):
                    for m in range(NHALF):
                        k = 2 * b + i
                        tr = pe.transpose(pb[b][:, i * T + m * P:i * T + (m + 1) * P],
                                          sg_rm[:, m, k * P:(k + 1) * P], ident)
                tr.then_inc(S("ret_yt"), 1)
            fill("rest0")
            fill("rest1")
            pe.wait_ge(S("ret_done"), 2)
            for j in range(4):
                unit_t(FIRST["branch_ret"] + j, None, 8, yret_hi, yret_lo, (j,))
            pe.wait_ge(S("merged_rw"), 4)
            out_rows("mix_out", 8, x_hi, x_lo, ready=lambda j: pe.wait_ge(S("merged_lo"), j + 1))

            def up_pairs(name, taken_gate, taken_val, n):
                def body(j, it):
                    if name == "ffn2_up" and j == 2 * PAIRS - 2:
                        pe.wait_ge(S("ple_small"), 64)
                        for k in range(2):
                            for m in range(NHALF):
                                tr = pe.transpose(pb[4][:, k * T + m * P:k * T + (m + 1) * P],
                                                  p_rm[:, m, k * P:(k + 1) * P], ident)
                        tr.then_inc(S("ple_tr"), 1)
                    pe.wait_ge(S(taken_val if j % 2 else taken_gate), at(j // 2 + 1, it, 2))
                    unit_t(FIRST[name] + j, it, 8, x_hi, x_lo, (j % 4,), ready=None if j else normed(n))
                in_turns(pe, 2 * PAIRS, body)

            def hidden_ready(name):
                return lambda j: pe.wait_ge(S(name + "_hlo"), j + 3)

            norm(1)
            up_pairs("conv_up", "conv_gfree", "conv_vfree", 1)
            out_rows("conv_down", KF, h_hi, h_lo, ready=hidden_ready("conv"))
            norm(2)
            up_pairs("ffn1_up", "ffn1_gfree", "ffn1_hid", 2)
            out_rows("ffn1_down", KF, h_hi, h_lo, ready=hidden_ready("ffn1"))
            norm(3)

            def column_block(name, b, free):
                if free:
                    pe.wait_ge(S("uvz_free"), free)
                for j in (2 * b, 2 * b + 1):
                    unit_r(FIRST[name] + j, None, 4, 4 * (j % 2), 8, x_hi, x_lo, ((4 + 2 * b,), (5 + 2 * b,)))

            pe.wait_ge(S("norm_lo"), 32)
            column_block("v", 0, 0)
            column_block("v", 1, 0)
            pe.wait_ge(S("dt_wlo"), AGAIN["dt_wlo"][1] + 1)
            for m in range(NHALF):
                for k in range(KD):
                    for n, (x, w) in enumerate(((x_hi, w_dt_hi), (x_hi, w_dt_lo), (x_lo, w_dt_hi))):
                        mm = pe.matmul(pb[0][:, 16 * m:16 * m + 16], x[:, k, m * P:(m + 1) * P], w[:, k, :],
                                       start=(k == 0 and n == 0), stop=(k == KD - 1 and n == 2))
            mm.then_inc(S("dt_mm"), 1)
            pe.wait_ge(S("gm_small"), 48)
            for h in range(8):
                tr = pe.transpose(pb[1 + h // 4][:, h % 4 * P:(h % 4 + 1) * P], ws_raw[:, h, :], ident)
            tr.then_inc(S("gm_wt"), 1)
            column_block("u", 0, 1)
            column_block("u", 1, 2)
            pe.wait_ge(S("dt_adt"), AGAIN["dt_adt"][1] + 1)
            pe.matmul(pb[3][:, 0:32], consts[:, KIND["tri"], :], dt_s[:, 6, :, :], start=True, stop=True)
            pe.matmul(pb[3][:, 32:64], consts[:, KIND["tri"], P - 1:P].to_broadcast([P, P]), dt_s[:, 6, :, :],
                      start=True, stop=True).then_inc(S("dt_cs"), 1)
            pe.wait_ge(S("gm_wtc"), AGAIN["gm_wtc"][1] + 2)
            for m in range(NHALF):
                if m:
                    pe.wait_ge(S("dt_used"), AGAIN["dt_used"][1] + 1)
                pe.wait_ge(S("gm_v"), AGAIN["gm_v"][1] + m + 1)
                for h in range(8):
                    mm = pe.matmul(pb[2 * m + h // 4][:, h % 4 * P:(h % 4 + 1) * P], ws_t[:, h, :],
                                   vg_rm[:, m, h * P:(h + 1) * P], start=True, stop=True)
                mm.then_inc(S("gm_mix"), 1)
            for j in range(6):
                if j < 4:
                    pe.wait_ge(S("uvz_free"), 3 + j // 2)
                else:
                    pe.wait_ge(S("xbc_taps"), 6 * (j - 3))
                if j == 5:
                    pe.wait_ge(S("gm_y"), AGAIN["gm_y"][1] + 1)
                    turn_normed(u_rm, "gm_tr")
                unit_t(FIRST["xbc"] + j, None, 8, x_hi, x_lo, (4 + j % 4,))

            def fill_2(step):
                for n in range(BEFORE_2[step], BEFORE_2[step] + WEAVE_2[step]):
                    j, part = divmod(n, 4)
                    if j < 4:
                        b = j // 2
                        if part == 0 and j % 2 == 0:
                            pe.wait_ge(S("xbc_taps"), 36 if b else 24)
                        unit_r(FIRST["z"] + j, None, 4, 4 * (j % 2), 8, x_hi, x_lo, ((6 - 2 * b,), (7 - 2 * b,)), part)
                    else:
                        if part == 0 and j == 4:
                            assert BEFORE_2[step] == 16
                            pe.wait_ge(S("uvz_free"), 6)
                        unit_r(FIRST["mix2_out"] + j - 4, None, 2, 2 * (j - 4), 16, y2_hi, y2_lo, OUT, part)

            fill_2("xs")
            pe.wait_ge(S("gm_lo"), 8)
            pe.wait_ge(S("xbc_silu"), 6)
            for m in range(NHALF):
                for t in range(8):
                    tr = pe.transpose(pb[2 * m + t // 4][:, t % 4 * P:(t % 4 + 1) * P], xbc_f[:, t, m * P:(m + 1) * P],
                                      ident)
                tr.then_inc(S("ssm_tr"), 1)
            fill_2("bm")
            pe.wait_ge(S("ssm_xrm"), 2)
            for g in range(2):
                tr = pe.transpose(pb[0][:, g * P:(g + 1) * P], xbc_f[:, 8 + g, 0:P], ident)
            tr.then_inc(S("ssm_tr"), 1)
            for m in range(NHALF):
                for g in range(2):
                    mm = pe.matmul(pb[1][:, (2 * m + g) * P:(2 * m + g + 1) * P], xbc_f[:, 8 + g, m * P:(m + 1) * P],
                                   xbc_f[:, 10 + g, m * P:(m + 1) * P], start=True, stop=True)
            mm.then_inc(S("ssm_cb"), 1)
            fill_2("st")
            pe.wait_ge(S("ssm_bmc"), AGAIN["ssm_bmc"][1] + 1)
            pe.wait_ge(S("ssm_xds"), AGAIN["ssm_xds"][1] + 1)
            for g in range(2):
                mm = pe.matmul(pb[2 + g][:, :], bm_rm[:, g * P:(g + 1) * P], y_rm[:, 1, g * 512:(g + 1) * 512],
                               start=True, stop=True)
            mm.then_inc(S("ssm_state"), 1)

            def decay_rows(n):
                m, g = divmod(n, 2)
                for i in range(8):
                    mm = pe.matmul(pb[i // 4][:, i % 4 * P:(i % 4 + 1) * P],
                                   dt_s[:, 6, m, 8 * g + i:8 * g + i + 1].to_broadcast([P, P]),
                                   consts[:, KIND["tri"], :], start=True, stop=True)
                mm.then_inc(S("ssm_row"), 1)

            pe.wait_ge(S("ssm_cbc"), 1)
            decay_rows(0)
            fill_2("row")
            pe.wait_ge(S("ssm_stc"), AGAIN["ssm_stc"][1] + 2)
            for n in range(4):
                m, g = divmod(n, 2)
                if n < 3:
                    pe.wait_ge(S("ssm_diff"), AGAIN["ssm_diff"][1] + 2 * n + 2)
                    decay_rows(n + 1)
                if n:
                    pe.wait_ge(S("ssm_yadd"), n)
                if m:
                    pe.matmul(pb[3][:, :], xbc_f[:, 10 + g, P:T], sstate[:, g, :], start=True,
                              stop=True).then_inc(S("ssm_off"), 1)
                fill_2(f"a{n}")
                pe.wait_ge(S("ssm_att"), AGAIN["ssm_att"][1] + n + 1)
                for i in range(8):
                    h = 8 * g + i
                    mm = pe.matmul(pb[2][:, i * 64:i * 64 + 64], att[n % 2][:, i, :], xd_rm[:, m, h * 64:h * 64 + 64],
                                   start=True, stop=True)
                mm.then_inc(S("ssm_y"), 1)
            fill_2("f0")
            fill_2("f1")
            pe.wait_ge(S("ssm_yn"), 4)
            turn_normed(y_rm, "ssm_ytr")
            out_rows("mix2_out", 16, y2_hi, y2_lo, first=4, ready=lambda j: pe.wait_ge(S("ssm_lo"), 2 * j - 6))
            norm(4)
            up_pairs("ffn2_up", "ffn2_gfree", "ffn2_hid", 4)
            u = FIRST["ple_proj"]
            pe.wait_ge(lo_split, u + 1)
            pe.wait_ge(S("ple_lo"), 1)
            for m in range(NHALF):
                pe.wait_ge(S("ffn2_hid"), 2 + PAIRS - 1 + m)
                for k in range(2):
                    for c in range(2):
                        for n, (x, w) in enumerate(((p_hi, w_hi), (p_hi, w_lo), (p_lo, w_hi))):
                            o = k * D + c * 512
                            mm = pe.matmul(pb[2 - 2 * m + c][:, :], x[:, k, m * P:(m + 1) * P],
                                           w[:, u % RING, o:o + 512], start=(k == 0 and n == 0),
                                           stop=(k == 1 and n == 2))
            mm.then_inc(unit_used, 1)
            out_rows("ffn2_down", KF, h_hi, h_lo, ready=hidden_ready("ffn2"))
            norm(5)
            out_rows("ple_gate", 8, x_hi, x_lo, ready=lambda j: pe.wait_ge(S("norm_lo"), 42 + 2 * j))

        @block.scalar
        def _(act):
            nxt = [0]

            def split(u, it=None):
                act.wait_ge(raw_landed[u % RING], at(16 * (u // RING + 1), it, 16))
                if u >= RING:
                    act.wait_ge(unit_used, at(u - RING + 1, it, 4))
                act.activation(w_hi[:, u % RING, :], w_raw[:, u % RING, :], ACT.Copy).then_inc(hi_split, 1)

            def ahead(u):
                while nxt[0] < min(u + AHEAD, UNITS):
                    split(nxt[0])
                    nxt[0] += 1

            def in_step(name, body):
                def step(j, it):
                    if it is None:
                        ahead(FIRST[name] + j)
                    else:
                        split(FIRST[name] + j + AHEAD - 1, it)
                    body(j, it)
                    if it is not None and j == 3:
                        nxt[0] = FIRST[name] + units // 4 * 4 + AHEAD - 1
                units = dict(STREAM)[name]
                ahead(FIRST[name] - 1)
                in_turns(act, units, step)

            def run_ahead(name, but=0):
                for j in range(dict(STREAM)[name] - but):
                    ahead(FIRST[name] + j)

            def norm(n):
                for m in range(NHALF):
                    out_squares(n, m)
                    for c in range(2):
                        if n:
                            act.wait_ge(S("resid_done"), 4 * (n - 1) + 2 * m + c + 1)
                        else:
                            act.wait_ge(S(f"x_landed{m}"), 16)
                        act.activation(xn[:, m, c * 512:(c + 1) * 512], resid[:, m, c * 512:(c + 1) * 512], ACT.Square,
                                       scale=1.0 / 32, accum_out=norm_s[:, 16 + 2 * m + c:17 + 2 * m + c]
                                       ).then_inc(S("norm_ss"), 1)

            def out_squares(n, m):
                if n == 6:
                    for c in range(2):
                        act.wait_ge(S("ple_g"), 2 * m + c + 1)
                        act.activation(gsig[:, m, c * 512:(c + 1) * 512], gsig[:, m, c * 512:(c + 1) * 512],
                                       ACT.Sigmoid).then_inc(S("ple_sig"), 1)
                if n not in (1, 2):
                    return
                for c in range(2):
                    out_part(act, n, m, c)
                    act.activation(xn[:, m, c * 512:(c + 1) * 512], pb[4 + 2 * m + c][:, :], ACT.Square,
                                   scale=1.0 / 32, accum_out=norm_s[:, 8 + 2 * m + c:9 + 2 * m + c]
                                   ).then_inc(S("post_sq"), 1)

            def turned_hi(base, turned, banks, name, dst, signal):
                for k in range(8):
                    act.wait_ge(S(turned), base + k // 2 + 1)
                    act.activation(dst[:, k, :], bank(banks[k // 2], 2)[:, k % 2, :], ACT.Copy,
                                   scale=col(name, k)).then_inc(S(signal), 1)

            def norm_split(n, name):
                turned_hi(4 * n, "norm_tr", (0, 1, 2, 3), name, x_hi, "norm_hi")

            norm(0)
            split(0)
            nxt[0] = 1
            act.wait_ge(S("cols_landed"), 16)
            norm_split(0, "mix_pre")
            ahead(-1)

            def rw_copy(j, it):
                act.wait_ge(unit_used, FIRST["rw"] + j + 1)
                if j >= 2:
                    act.wait_ge(S("rw_pm"), 2 * (j - 1))
                act.wait_ge(S("rw_init"), 1)
                act.activation(psh[:, j % 2, :, 1:T + 1], bank(j % 4, 2), ACT.Copy).then_inc(S("rw_cp"), 1)

            in_step("rw", rw_copy)
            ahead(FIRST["ret"] - 1)
            act.wait_ge(S("ret_trig"), 1)
            act.activation(trig[:, 4:6, :, :], trig[:, 2:4, :, :], ACT.Sin).then_inc(S("ret_sin"), 1)

            def block_copy(b, used, dst, func):
                for m in range(NHALF):
                    ins = act.activation(dst[:, m, :], pb[4 + 2 * (b % 2) + m][:, :], func)
                ins.then_inc(S(used), 1)

            ret_dst = (q_rm, kr_rm, vr_rm[:, :, 0:512], vr_rm[:, :, 512:1024], sg_rm[:, :, 0:512],
                       sg_rm[:, :, 512:1024])
            evacuated = [0]

            def behind(step):
                done = BEFORE[step] // 4
                while evacuated[0] < done:
                    j = evacuated[0]
                    if j >= 12 or j % 2:
                        act.wait_ge(unit_used, FIRST["ret"] + j + 1)
                    if j < 12 and j % 2:
                        block_copy(j // 2, "ret_free", ret_dst[j // 2], ACT.Copy if j < 8 else ACT.Silu)
                    elif 12 <= j < 20:
                        if j == 16:
                            act.wait_ge(S("rw_done"), 1)
                        dst = sig_rw if j < 16 else sig_ret
                        act.activation(dst[:, 2 * (j % 4):2 * (j % 4) + 2, :], bank(4 + j % 4, 2),
                                       ACT.Sigmoid).then_inc(S("gates_ev"), 1)
                    evacuated[0] += 1
                ahead(FIRST["ret"] + done)

            act.wait_ge(S("rw_pm"), 14)
            act.activation(act_w[0:64, 0, :], pm[0:64, 12, :], ACT.Tanh).then_inc(S("rw_lora"), 1)
            act.activation(act_w[:, 1, :], pm[:, 13, :], ACT.Sigmoid).then_inc(S("rw_lora"), 1)
            act.wait_ge(S("rw_kk0"), 1)
            act.activation(t2, t1[:, :, :], ACT.Square).then_inc(S("rw_sq"), 1)
            act.wait_ge(S("rw_z"), 1)
            for t in range(4):
                act.activation(sw[:, t, :], bank(t // 2, 2)[:, t % 2, :], ACT.Sigmoid,
                               bias=col("w0", t)).then_inc(S("rw_sw"), 1)
            act.wait_ge(S("rw_norm"), 1)
            act.activation(t2, t2, ACT.Sqrt).then_inc(S("rw_normrt"), 1)
            behind("low_rank")
            act.wait_ge(S("rw_z"), 2)
            for t in range(4):
                act.activation(a_s[:, t, :], bank(t // 2, 2)[:, t % 2, :], ACT.Sigmoid,
                               bias=col("a0", t)).then_inc(S("rw_as"), 1)
            act.wait_ge(S("rw_z"), 3)
            for b in range(2):
                act.activation(g_t[:, 2 * b:2 * b + 2, :], bank(2 + b, 2), ACT.Copy).then_inc(S("rw_g"), 1)
            act.wait_ge(S("rw_css"), 2)
            act.activation(e_pos[:, :, :], css[:, :, :], ACT.Exp, scale=-DECAY_SCALE).then_inc(S("rw_e"), 1)
            act.wait_ge(S("rw_e"), 1)
            act.activation(css[:, :, :], css[:, :, :], ACT.Exp, scale=DECAY_SCALE).then_inc(S("rw_e"), 1)
            act.activation(b_f[:, :, :], b_f[:, :, :], ACT.Exp, scale=-DECAY_SCALE).then_inc(S("rw_e"), 1)
            behind("norms")
            act.wait_ge(S("rw_tr"), 2)
            for m in range(NHALF):
                act.activation(v_rm[:, m, :], pb[2 + m][:, :], ACT.Copy).then_inc(S("rw_v"), 1)
            behind("keys")
            behind("l")
            behind("t0")
            for j in range(1, LEVELS):
                act.wait_ge(S("rw_t"), j + 1)
                for q in range(2):
                    act.activation(tp[:, 8 * q:8 * q + 8, :], bank(q, 8), ACT.Copy).then_inc(S("rw_tp"), 1)
                behind(f"t{j}")
                behind(f"x{j}")
            act.wait_ge(S("rw_xa"), 1)
            for e in range(2):
                dst = xa[:, :, :].rearrange("p t (m e n) -> p m t e n", m=2, e=2)[:, :, :, e, :]
                act.activation(dst, pb[e][:, :].rearrange("p (m t n) -> p m t n", m=2, t=4),
                               ACT.Copy).then_inc(S("rw_xac"), 1)
            for step in ("xa", "xmv", "s0", "u1", "s1", "u2", "s2", "u3"):
                behind(step)
            act.wait_ge(S("rw_yp"), 1)
            for q in range(2):
                dst = ys_v.rearrange("p m (t q d) -> p m t q d", t=4, q=2)[:, :, :, q, :]
                act.activation(dst, pb[q][:, :].rearrange("p (m t d) -> p m t d", m=2, t=4),
                               ACT.Copy).then_inc(S("rw_y"), 1)
            behind("y")
            act.wait_ge(S("rw_gnv"), 1)
            act.activation(gn[:, 2, :], gn[:, 1, :], ACT.Sqrt).then_inc(S("rw_gnrt"), 1)
            behind("y2")
            for t in range(4):
                act.wait_ge(S("rw_yt"), t // 2 + 1)
                act.activation(ytmp[:, t, :], bank(t // 2, 2)[:, t % 2, :], ACT.Identity, bias=col("lnx_b", t),
                               scale=col("lnx_w", t)).then_inc(S("rw_ln"), 1)
            act.wait_ge(S("rw_yg"), 1)
            act.activation(yrw_hi[:, :, :], ytmp[:, :, :], ACT.Copy).then_inc(S("rw_yhi"), 1)
            behind("yt")

            for b in range(2):
                act.wait_ge(S("ret_tr"), b + 1)
                act.activation(q_f[:, 2 * b:2 * b + 2, :], bank(b, 2), ACT.Copy).then_inc(S("ret_qf"), 1)
            behind("qk")
            act.wait_ge(S("ret_r"), 1)
            act.activation(rstate[:, :, :], bank(0, 4), ACT.Copy).then_inc(S("ret_rc"), 1)
            behind("sc0")
            behind("o0")
            behind("o1")
            act.wait_ge(S("ret_var"), 1)
            act.activation(ret_s[:, 9, :], ret_s[:, 8, :], ACT.Sqrt).then_inc(S("ret_rt"), 1)
            behind("stats")
            for b in range(4):
                act.wait_ge(S("ret_yt"), b + 1)
                act.activation(yret_hi[:, 2 * b:2 * b + 2, :], bank(b, 2), ACT.Copy).then_inc(S("ret_yhi"), 1)
            behind("rest0")
            behind("rest1")
            for j in range(4):
                ahead(FIRST["branch_ret"] + j)
                act.wait_ge(S("merged"), j + 1)
                act.activation(x_hi[:, 2 * j:2 * j + 2, :], merged[:, 2 * j:2 * j + 2, :],
                               ACT.Copy).then_inc(S("merged_hi"), 1)
            run_ahead("mix_out", 1)

            norm(1)
            norm_split(1, "ffn_pre")
            def conv_first_tap(j, it):
                side, b = j % 2, j // 2 % 2
                act.wait_ge(unit_used, at(FIRST["conv_up"] + j + 1, it, 4))
                act.wait_ge(S("conv_hid"), at(j // 2 + 1, it, 2))
                for i in range(2):
                    tile = at(22 * side + j // 2 * 2 + i, it, 4)
                    act.activation((cval if side else cgate)[:, b, i, :], bank(j % 4, 2)[:, i, :], ACT.Identity,
                                   bias=cols[:, bass.ds(tile + COL["conv1_b"], 1)],
                                   scale=cols[:, bass.ds(tile + COL["conv1_w"] + 88, 1)]).then_inc(S("conv_tap2"), 1)
                if side:
                    act.wait_ge(S("conv_vfree"), at(j // 2 + 3, it, 2))
                    act.activation(gate[:, b, :].rearrange("p (i n) -> p i n", i=2), cgate[:, b, :, :],
                                   ACT.Gelu_apprx_tanh).then_inc(S("conv_gelu"), 1)

            in_step("conv_up", conv_first_tap)
            run_ahead("conv_down", 1)

            def swiglu_gate(name):
                act.sem_inc(S(name + "_gfree"), 2)

                def body(j, it):
                    if name == "ffn2" and j == 2 * PAIRS - 2:
                        act.wait_ge(S("ple_tr"), 1)
                        act.activation(p_hi[:, :, :], bank(4, 2), ACT.Copy).then_inc(S("ple_hi"), 1)
                    if j % 2:
                        return
                    b = j // 2 % 2
                    act.wait_ge(unit_used, at(FIRST[name + "_up"] + j + 1, it, 4))
                    act.wait_ge(S(name + "_hid"), at(j // 2 + 1, it, 2))
                    act.activation(gate[:, b, :], pb[j % 4][:, :], ACT.Silu).then_inc(S(name + "_gfree"), 1)
                in_step(name + "_up", body)
                if name == "ffn2":
                    ahead(FIRST["ple_proj"])
                    act.wait_ge(unit_used, FIRST["ffn2_down"])
                    for m in range(NHALF):
                        for c in range(2):
                            act.activation(proj[:, m, c * 512:(c + 1) * 512], pb[2 - 2 * m + c][:, :],
                                           ACT.Copy).then_inc(S("ple_proj"), 1)
                run_ahead(name + "_down", 1)

            norm(2)
            norm_split(2, "ffn1")
            swiglu_gate("ffn1")
            norm(3)
            norm_split(3, "mix2")
            act.wait_ge(S("dt_small"), 64)
            act.activation(w_dt_hi[:, :, :], w_dt[:, :, :], ACT.Copy).then_inc(S("dt_whi"), 1)
            blocks = ((vg_rm, 0), (vg_rm, 1), (u_rm, 0), (u_rm, 1), (z_s, 0), (z_s, 1))

            def uvz_copy(b):
                dst, c = blocks[b]
                block_copy(b if b < 4 else b + 1, "uvz_free", dst[:, :, c * 512:(c + 1) * 512], ACT.Gelu if b < 4 else ACT.Silu)

            ahead(FIRST["v"] - 1)
            for j in range(8):
                ahead(FIRST["v"] + j)
                if j % 2:
                    act.wait_ge(unit_used, FIRST["v"] + j + 1)
                    uvz_copy(j // 2)
                if j == 5:
                    act.wait_ge(S("dt_na"), AGAIN["dt_na"][1] + 1)
                    act.activation(dt_s[:, 2, :, :], dt_s[:, 1, :, :], ACT.Exp).then_inc(S("dt_e"), 1)
                    act.activation(rows16[:, 1, :], rows16[:, 1, :], ACT.Exp).then_inc(S("dt_e"), 1)

            def xbc_first_tap(j, it):
                if j == 5:
                    turned_hi(0, "gm_tr", (0, 1, 2, 3), "gm_out", y2_hi, "gm_hi")
                act.wait_ge(unit_used, FIRST["xbc"] + j + 1)
                for i in range(2):
                    k = 2 * j + i
                    act.activation(xbc_f[:, k, :], bank(4 + j % 4, 2)[:, i, :], ACT.Identity, bias=col("conv2_b", k),
                                   scale=col("conv2_w", 36 + k)).then_inc(S("xbc_tap3"), 1)
                if j in (1, 2):
                    m = j - 1
                    act.wait_ge(S("gm_ya"), AGAIN["gm_ya"][1] + m + 1)
                    act.activation(vg_rm[:, m, :], u_rm[:, m, :], ACT.Square,
                                   accum_out=gm_s[:, 24 + m:25 + m]).then_inc(S("gm_sq"), 1)

            in_step("xbc", xbc_first_tap)

            def behind_2(step):
                done = BEFORE_2[step] // 4
                while z_copied[0] < min(done // 2, 2):
                    act.wait_ge(unit_used, FIRST["z"] + 2 * z_copied[0] + 2)
                    uvz_copy(4 + z_copied[0])
                    z_copied[0] += 1
                ahead(FIRST["z"] + done)

            z_copied = [0]
            ahead(FIRST["z"] - 1)
            for j in range(6):
                act.wait_ge(S("xbc_taps"), 6 * j + 6)
                act.activation(xbc_f[:, 2 * j:2 * j + 2, :], xbc_f[:, 2 * j:2 * j + 2, :],
                               ACT.Silu).then_inc(S("xbc_silu"), 1)
            behind_2("xs")
            act.wait_ge(S("dt_csd"), 3)
            act.activation(dt_s[:, 9:11, :, :], dt_s[:, 7:9, :, :], ACT.Exp).then_inc(S("dt_ecs"), 1)
            for m in range(NHALF):
                act.wait_ge(S("ssm_tr"), m + 1)
                for b in range(2):
                    ins = act.activation(xs_rm[:, m, b * 512:(b + 1) * 512], pb[2 * m + b][:, :], ACT.Copy)
                ins.then_inc(S("ssm_xrm"), 1)
            behind_2("bm")
            act.wait_ge(S("ssm_tr"), 3)
            act.activation(bm_rm[:, :], pb[0][:, 0:256], ACT.Copy).then_inc(S("ssm_bmc"), 1)
            behind_2("st")
            act.wait_ge(S("ssm_state"), AGAIN["ssm_state"][1] + 1)
            for g in range(2):
                act.activation(sstate[:, g, :], pb[2 + g][:, :], ACT.Copy).then_inc(S("ssm_stc"), 1)
            behind_2("row")
            behind_2("a0")
            for n in range(4):
                act.wait_ge(S("ssm_min"), AGAIN["ssm_min"][1] + n + 1)
                act.activation(att[n % 2][:, :, :], att[n % 2][:, :, :], ACT.Exp).then_inc(S("ssm_exp"), 1)
                if n:
                    behind_2(f"a{n}")
            behind_2("f0")
            for m in range(NHALF):
                for g in range(2):
                    act.wait_ge(S("ssm_yz"), m + 1)
                    act.activation(xs_rm[:, m, g * 512:(g + 1) * 512], y_rm[:, m, g * 512:(g + 1) * 512], ACT.Square,
                                   accum_out=dt_s[:, 11, 0, 2 * m + g:2 * m + g + 1]).then_inc(S("ssm_sq"), 1)
            turned_hi(0, "ssm_ytr", (0, 1, 2, 3), "ssm", y2_hi[:, 8:16, :], "ssm_hi")
            behind_2("f1")
            for u in range(FIRST["mix2_out"] + 4, FIRST["mix2_out"] + 7):
                ahead(u)
            norm(4)
            norm_split(4, "ffn2")
            swiglu_gate("ffn2")
            norm(5)
            norm_split(5, "ple")
            run_ahead("ple_gate", 1)
            norm(6)

        @block.vector
        def _(dve):
            nxt, steps = [0], [0]

            def link(ins):
                steps[0] += 1
                ins.then_inc(S("dve_step"), 1)
                dve.wait_ge(S("dve_step"), steps[0])

            def split(u, it=None):
                dve.wait_ge(hi_split, at(u + 1, it, 4))
                dve.tensor_tensor(w_lo[:, u % RING, :], w_raw[:, u % RING, :], w_hi[:, u % RING, :],
                                  ALU.subtract).then_inc(lo_split, 1)

            def ahead(u):
                while nxt[0] < min(u + AHEAD, UNITS):
                    split(nxt[0])
                    nxt[0] += 1

            def in_step(name, body):
                def step(j, it):
                    if it is None:
                        ahead(FIRST[name] + j)
                    else:
                        split(FIRST[name] + j + AHEAD - 1, it)
                    body(j, it)
                    if it is not None and j == 3:
                        nxt[0] = FIRST[name] + units // 4 * 4 + AHEAD - 1
                units = dict(STREAM)[name]
                ahead(FIRST[name] - 1)
                in_turns(dve, units, step)

            def run_ahead(name, but=0):
                for j in range(dict(STREAM)[name] - but):
                    ahead(FIRST[name] + j)

            def sum_squares(n, m):
                dve.wait_ge(S("norm_ss"), 4 * n + 2 * m + 2)
                dve.scalar_tensor_tensor(out=norm_s[:, 2 + m:3 + m], in0=norm_s[:, 16 + 2 * m:17 + 2 * m], scalar=RMS_EPS,
                                         in1=norm_s[:, 17 + 2 * m:18 + 2 * m], op0=ALU.add,
                                         op1=ALU.add).then_inc(S("norm_ms"), 1)

            def norm_scale(n, m):
                sum_squares(n, m)
                dve.wait_ge(S("norm_rt"), 2 * n + m + 1)
                for c in range(2):
                    cc = slice(c * 512, (c + 1) * 512)
                    dve.tensor_scalar(xn[:, m, cc], resid[:, m, cc], norm_s[:, 6 + m:7 + m], None,
                                      ALU.mult).then_inc(S("norm_xn"), 1)

            def turned_lo(base, hi, banks, name, dst_hi, dst, signal):
                for k in range(8):
                    dve.wait_ge(S(hi), base + k // 2 * 2 + 2)
                    dve.scalar_tensor_tensor(out=dst[:, k, :], in0=bank(banks[k // 2], 2)[:, k % 2, :],
                                             scalar=col(name, k), in1=dst_hi[:, k, :], op0=ALU.mult,
                                             op1=ALU.subtract).then_inc(S(signal), 1)

            def norm(n, name, out):
                for m in range(NHALF):
                    out(m)
                    norm_scale(n, m)
                if n == 0:
                    dve.wait_ge(S("cols_landed"), 16)
                    split(0)
                    nxt[0] = 1
                turned_lo(8 * n, "norm_hi", (0, 1, 2, 3), name, x_hi, x_lo, "norm_lo")

            norm(0, "mix_pre", lambda m: None)
            ahead(-1)
            dve.wait_ge(S("trig_small"), 32)
            link(dve.tensor_copy(posf[:, 0, :], posi[:, :]))
            inv = small[:, SMALL_INV:SMALL_INV + 32]
            for m in range(NHALF):
                ins = dve.tensor_scalar(trig[:, 0, m, :], inv, posf[:, 0, m:m + 1], None, ALU.mult)
            link(ins)
            for i, quarter in enumerate((0.0, 0.25)):
                turns, rest = trig[:, 1, :, :], trig[:, 2 + i, :, :]
                link(dve.tensor_scalar(turns, trig[:, 0, :, :], 1.0 / TWO_PI, quarter, ALU.mult, ALU.add))
                link(dve.tensor_scalar(turns, turns, ROUND, None, ALU.add))
                link(dve.tensor_scalar(turns, turns, ROUND, None, ALU.subtract))
                src = trig[:, 0, :, :]
                for part in (PI_A, PI_B, PI_C):
                    link(dve.scalar_tensor_tensor(out=rest, in0=turns, scalar=-part, in1=src, op0=ALU.mult, op1=ALU.add))
                    src = rest
                link(dve.tensor_scalar(rest, rest, quarter * TWO_PI, PI_F32, ALU.add, ALU.min))
                ins = dve.tensor_scalar(rest, rest, -PI_F32, None, ALU.max)
                link(ins)
            dve.tensor_scalar(trig[:, 0, :, :], trig[:, 0, :, :], 0.0, None, ALU.add).then_inc(S("ret_trig"), 1)

            link(dve.memset(cmask[:, :, :], 1.0))
            dve.memset(cmask[:, :, :].rearrange("p a (c n) -> p (a c) n", n=CHUNK)[:, :, 0:1], 0.0)
            dve.memset(psh_flat[:, :].rearrange("p (g n) -> p g n", g=4)[:, :, 0:1], 0.0).then_inc(S("rw_init"), 1)

            def shift_mix(j, it):
                dve.wait_ge(S("rw_cp"), j + 1)
                now, before = psh[:, j % 2, :, 1:T + 1], psh[:, j % 2, :, 0:T]
                if j >= 1:
                    dve.wait_ge(S("rw_pm"), 2 * j)
                link(dve.tensor_tensor(act_w[:, :, :], before, now, ALU.subtract))
                for i in range(2):
                    dve.scalar_tensor_tensor(out=pm[:, 2 * j + i, :], in0=act_w[:, i, :], scalar=col("mu", 2 * j + i),
                                             in1=now[:, i, :], op0=ALU.mult, op1=ALU.add).then_inc(S("rw_pm"), 1)

            in_step("rw", shift_mix)
            dve.wait_ge(S("consts_landed"), 16)
            ahead(FIRST["ret"] - 1)
            link(dve.tensor_scalar(omka[:, :], col("k_a", 0, 4), -1.0, 1.0, ALU.mult, ALU.add))
            dve.wait_ge(S("rw_pm"), 14)
            for t in range(4):
                ins = dve.tensor_scalar(t1[:, t, :], pm[:, 4 + t, :], col("k_k", t), None, ALU.mult)
            ins.then_inc(S("rw_kk0"), 1)
            dve.wait_ge(S("rw_kk0"), 1)
            merged_rw = [0]

            def behind(step):
                done = BEFORE[step] // 4
                while 20 + merged_rw[0] < done:
                    j = merged_rw[0]
                    dve.wait_ge(unit_used, FIRST["branch_rw"] + j + 1)
                    dve.wait_ge(S("gates_ev"), 4)
                    for b in range(2):
                        k = 4 * j + 2 * b
                        dve.tensor_tensor(merged[:, k:k + 2, :], bank(4 + 2 * j + b, 2), sig_rw[:, k:k + 2, :],
                                          ALU.mult).then_inc(S("merged_rw"), 1)
                    merged_rw[0] += 1
                if step in POOL_SPLITS[0] + POOL_SPLITS[1]:
                    nxt[0] = FIRST["ret"] + done + AHEAD
                    return
                if step in ("l", "u3"):
                    dve.wait_ge(lo_split, nxt[0])
                ahead(FIRST["ret"] + done)

            dve.wait_ge(S("rw_sw"), 4)
            dve.tensor_tensor_scan(css[:, :, :].rearrange("p a n -> p (a n)"), cmask[:, :, :].rearrange("p a n -> p (a n)"),
                                   sw[:, :, :].rearrange("p a n -> p (a n)"), 0.0, ALU.mult,
                                   ALU.add).then_inc(S("rw_css"), 1)
            dve.wait_ge(S("rw_sums"), 1)
            for b in range(2):
                ins = dve.tensor_scalar(t2[:, 2 * b:2 * b + 2, :], bank(2 + b, 2), 1e-24, None, ALU.max)
            ins.then_inc(S("rw_norm"), 1)
            dve.wait_ge(S("rw_css"), 1)
            dve.tensor_tensor(b_f[:, :, :], css[:, :, :], sw[:, :, :], ALU.subtract).then_inc(S("rw_css"), 1)
            dve.wait_ge(S("rw_normrt"), 1)
            link(dve.reciprocal(kk[:, :, :], t2))
            link(dve.tensor_tensor(kk[:, :, :], kk[:, :, :], t1[:, :, :], ALU.mult))
            behind("low_rank")
            dve.wait_ge(S("rw_as"), 4)
            for t in range(4):
                ins = dve.tensor_scalar(t1[:, t, :], a_s[:, t, :], col("k_a", t), omka[:, t:t + 1], ALU.mult, ALU.add)
            link(ins)
            link(dve.tensor_tensor(pm[:, 4:8, :], pm[:, 4:8, :], t1[:, :, :], ALU.mult))
            for t in range(4):
                ins = dve.scalar_tensor_tensor(out=t1[:, t, :], in0=pm[:, t, :], scalar=col("r_k", t),
                                               in1=pm[:, 4 + t, :], op0=ALU.mult, op1=ALU.mult)
            ins.then_inc(S("rw_rk"), 1)
            behind("norms")
            dve.wait_ge(S("rw_e"), 3)
            dve.tensor_copy(pc[:, :, :], e_pos[:, :, :].rearrange("p a (c n) -> p a c n", n=CHUNK)[:, :, :, CHUNK - 1])
            link(dve.tensor_tensor(a_f[:, :, :], kk[:, :, :], b_f[:, :, :], ALU.mult))
            link(dve.tensor_tensor(b_f[:, :, :], kk[:, :, :], a_s[:, :, :], ALU.mult))
            dve.tensor_tensor(b_f[:, :, :], b_f[:, :, :], css[:, :, :], ALU.mult)
            dve.wait_ge(S("rw_rk"), 1)
            dve.tensor_tensor(pm[:, 4:8, :], pm[:, 4:8, :], css[:, :, :], ALU.mult)
            dve.tensor_tensor(pm[:, 0:4, :], pm[:, 0:4, :], e_pos[:, :, :], ALU.mult).then_inc(S("rw_abkr"), 1)
            dve.wait_ge(S("rw_sums"), 2)
            for b in range(2):
                ins = dve.tensor_tensor(bonus[:, 2 * b:2 * b + 2, :], bank(b, 2), pm[:, 8 + 2 * b:10 + 2 * b, :],
                                        ALU.mult)
            ins.then_inc(S("rw_bonus"), 1)
            behind("keys")

            def causal(k):
                return consts[:, KIND["causal"]:KIND["causal"] + 1, k * CHUNK:(k + 1) * CHUNK].to_broadcast([P, 8, CHUNK])

            strict, incl = causal(0), causal(1)
            eye = consts[:, KIND["eye"]:KIND["eye"] + 1, 0:CHUNK].to_broadcast([P, 8, CHUNK])

            def masked(dst, first_bank, mask, signal):
                for q in range(2):
                    dve.tensor_tensor(dst[:, 8 * q:8 * q + 8, :], bank(first_bank + q, 8), mask,
                                      ALU.mult).then_inc(S(signal), 1)

            def copied(dst, first_bank, signal):
                for i in range(2):
                    dve.tensor_copy(dst[i], pb[first_bank + i][:, :]).then_inc(S(signal), 1)

            dve.wait_ge(S("rw_l"), 1)
            dve.wait_ge(S("rw_bonus"), 1)
            dve.wait_ge(S("rw_tr"), 2)
            masked(lt, 0, strict, "rw_lt")
            behind("l")
            for j in range(LEVELS):
                if j == 0:
                    dve.wait_ge(S("rw_t"), 1)
                    for q in range(2):
                        g = slice(8 * q, 8 * q + 8)
                        dve.tensor_tensor(xi[:, g, :], bank(q, 8), eye, ALU.add)
                        ins = dve.tensor_tensor(xt[:, g, :], lm[:, g, :], eye, ALU.add)
                    ins.then_inc(S("rw_xd"), 1)
                dve.wait_ge(S("rw_f"), j + 1)
                if j in (0, 5):
                    masked(gm if j == 0 else g1, 2, strict if j == 0 else incl, "rw_fd")
                elif j == 4:
                    copied([gm[:, 8 * i:8 * i + 8, :].rearrange("p g n -> p (g n)") for i in range(2)], 2, "rw_fd")
                else:
                    dst = (k_rm, a_rm, b_rm)[j - 1]
                    copied([dst[:, i, :] for i in range(2)], 2, "rw_fd")
                behind(f"t{j}")
                if j == 0:
                    continue
                dve.wait_ge(S("rw_xd"), j)
                dve.wait_ge(S("rw_x"), j)
                for q in range(2):
                    g = slice(8 * q, 8 * q + 8)
                    if j < LEVELS - 1:
                        dve.tensor_tensor(xi[:, g, :], bank(2 + q, 8), xi[:, g, :], ALU.add)
                    ins = dve.tensor_tensor(xt[:, g, :], bank(q, 8), xt[:, g, :], ALU.add)
                ins.then_inc(S("rw_xd"), 1)
                if j == LEVELS - 1:
                    dve.wait_ge(S("rw_f"), 7)
                    masked(g2, 2, incl, "rw_fd")
                behind(f"x{j}")
            behind("xa")
            dve.wait_ge(S("rw_xmv"), 1)
            for q in range(2):
                dve.tensor_scalar(wv[:, 8 * q:8 * q + 8, :], bank(2 + q, 8), -1.0, None, ALU.mult).then_inc(S("rw_w"), 1)
            behind("xmv")
            dve.wait_ge(S("rw_w"), 2)
            for c in range(4):
                m, e = divmod(c, 2)
                tok = slice(64 * e, 64 * e + 64)
                if c:
                    dve.wait_ge(S("rw_up"), c)
                    for q in range(2):
                        u = wv[tok, 8 * q + 4 * m:8 * q + 4 * m + 4, :]
                        ins = dve.tensor_tensor(u, u, pb[2 + q][tok, 0:256].rearrange("p (t d) -> p t d", t=4),
                                                ALU.subtract)
                    ins.then_inc(S("rw_u"), 1)
                    behind(f"u{c}")
                if c < 3:
                    dve.wait_ge(S("rw_s"), c + 1)
                    src = pb[0][:, 0:256].rearrange("p (t d) -> p t d", t=4)
                    if c:
                        link(dve.tensor_tensor(stmp[:, :, :], src, st[:, c, :, :], ALU.add))
                        src = stmp[:, :, :]
                    dve.tensor_tensor(st[:, c + 1, :, :], src,
                                      pc[:, :, c:c + 1].to_broadcast([P, 4, 64]), ALU.mult).then_inc(S("rw_st"), 1)
                    dve.wait_ge(S("rw_st"), c + 1)
                    behind(f"s{c}")
            dve.wait_ge(S("rw_y"), 2)
            dve.wait_ge(S("rw_yp"), 2)
            for m, e0 in ((0, 1), (1, 0)):
                for q in range(2):
                    rows_ = slice(64 * e0, P)
                    y = ys_v[rows_, m, :].rearrange("p (t q d) -> p t q d", t=4, q=2)[:, :, q, :]
                    ins = dve.tensor_tensor(y, y, pb[2 + q][rows_, m * 256:m * 256 + 256].rearrange(
                        "p (t d) -> p t d", t=4), ALU.add)
            link(ins)
            y16 = ys_v.rearrange("p m (h d) -> p (m h) d", h=8)
            n16 = yn[:, :, :].rearrange("p m (h d) -> p (m h) d", h=8)
            q16 = yq[:, :, :].rearrange("p m (h d) -> p (m h) d", h=8)

            def over_head(k):
                return gn[:, k, :].unsqueeze(2).to_broadcast([P, 16, 64])

            link(dve.tensor_reduce(gn[:, 0, :], y16, AX_X, ALU.add))
            link(dve.tensor_scalar(gn[:, 0, :], gn[:, 0, :], 1.0 / 64, None, ALU.mult))
            link(dve.tensor_tensor(n16, y16, over_head(0), ALU.subtract))
            link(dve.tensor_tensor(q16, n16, n16, ALU.mult))
            link(dve.tensor_reduce(gn[:, 1, :], q16, AX_X, ALU.add))
            dve.tensor_scalar(gn[:, 1, :], gn[:, 1, :], 1.0 / 64, 64e-5, ALU.mult, ALU.add).then_inc(S("rw_gnv"), 1)
            behind("y")
            dve.wait_ge(S("rw_gnrt"), 1)
            link(dve.reciprocal(gn[:, 3, :], gn[:, 2, :]))
            dve.tensor_tensor(n16, n16, over_head(3), ALU.mult).then_inc(S("rw_yn"), 1)
            behind("y2")
            dve.wait_ge(S("rw_ln"), 4)
            link(dve.tensor_tensor(ytmp[:, :, :], ytmp[:, :, :], bonus[:, :, :], ALU.add))
            dve.tensor_tensor(ytmp[:, :, :], ytmp[:, :, :], g_t[:, :, :], ALU.mult).then_inc(S("rw_yg"), 1)
            dve.wait_ge(S("rw_yhi"), 1)
            dve.tensor_tensor(yrw_lo[:, :, :], ytmp[:, :, :], yrw_hi[:, :, :], ALU.subtract).then_inc(S("rw_done"), 1)
            behind("yt")

            for b in range(2):
                dve.wait_ge(S("ret_tr"), 3 + b)
                dve.tensor_copy(k_f[:, 2 * b:2 * b + 2, :], bank(2 + b, 2)).then_inc(S("ret_kf"), 1)
            behind("qk")
            dve.wait_ge(S("ret_qf"), 2)
            dve.wait_ge(S("ret_small"), 16)
            dve.tensor_tensor(qd_f[:, :, :], q_f[:, :, P:T], decay[:, 8:12, :], ALU.mult).then_inc(S("ret_qd"), 1)
            masks = decay[:, 0:8, :].rearrange("p (t q) n -> p q t n", q=2)
            for m in range(NHALF):
                dve.wait_ge(S("ret_s"), m + 1)
                if m:
                    dve.wait_ge(S("ret_o"), 1)
                for q in range(2):
                    dve.tensor_tensor(sco[:, q, :, :], bank(2 + q, 4), masks[:, q, :, :], ALU.mult).then_inc(S("ret_sc"), 1)
                behind(("sc0", "o0")[m])
            stats = ret_s[:, 0:6, :].rearrange("p a b -> p (a b)").rearrange("p (h s) -> p h s", s=6)
            mv = ret_s[:, 6:8, :].rearrange("p a b -> p (a b)").rearrange("p (h s) -> p h s", s=2)

            def o_of(m, h):
                return pb[2 * m + h % 2][:, h // 2 * P:(h // 2 + 1) * P]

            for m in range(NHALF):
                dve.wait_ge(S("ret_o"), m + 1)
                for h in range(8):
                    ins = dve.bn_stats(stats[:, 8 * m + h, :], o_of(m, h))
            link(ins)
            for n in range(16):
                ins = dve.bn_aggr(mv[:, n, :], stats[:, n, :])
            link(ins)
            dve.tensor_scalar(ret_s[:, 8, :], mv[:, :, 1], 1e-5, None, ALU.add).then_inc(S("ret_var"), 1)
            behind("o1")
            dve.wait_ge(S("ret_rt"), 1)
            link(dve.reciprocal(ret_s[:, 10, :], ret_s[:, 9, :]))
            sg16 = sg_rm[:, :, :].rearrange("p m (h e) -> p (m h) e", h=8)
            dve.wait_ge(S("ret_free"), 6)
            link(dve.tensor_tensor(sg16, sg16, ret_s[:, 10, :].unsqueeze(2).to_broadcast([P, 16, P]), ALU.mult))
            for m in range(NHALF):
                for h in range(8):
                    n = 8 * m + h
                    ins = dve.scalar_tensor_tensor(out=sg16[:, n, :], in0=o_of(m, h), scalar=mv[:, n, 0:1],
                                                   in1=sg16[:, n, :], op0=ALU.subtract, op1=ALU.mult)
            ins.then_inc(S("ret_y"), 1)
            behind("stats")
            for b in range(4):
                dve.wait_ge(S("ret_yhi"), b + 1)
                dve.tensor_tensor(yret_lo[:, 2 * b:2 * b + 2, :], bank(b, 2), yret_hi[:, 2 * b:2 * b + 2, :],
                                  ALU.subtract).then_inc(S("ret_lo"), 1)
            dve.wait_ge(S("ret_lo"), 4)
            dve.sem_inc(S("ret_done"), 2)
            behind("rest0")
            behind("rest1")
            dve.wait_ge(unit_used, FIRST["branch_ret"])
            for b in range(2):
                k = 4 + 2 * b
                dve.tensor_tensor(merged[:, k:k + 2, :], bank(6 + b, 2), sig_rw[:, k:k + 2, :],
                                  ALU.mult).then_inc(S("merged_rw"), 1)
            for j in range(4):
                ahead(FIRST["branch_ret"] + j)
                dve.wait_ge(unit_used, FIRST["branch_ret"] + j + 1)
                k = slice(2 * j, 2 * j + 2)
                if j >= 2:
                    dve.wait_ge(S("merged"), j - 1)
                dve.wait_ge(S("merged_rw"), 4)
                link(dve.tensor_tensor(mtmp[:, j % 2, :, :], bank(j, 2), sig_ret[:, k, :], ALU.mult))
                dve.tensor_tensor(merged[:, k, :], merged[:, k, :], mtmp[:, j % 2, :, :], ALU.add).then_inc(S("merged"), 1)
                dve.wait_ge(S("merged_hi"), j + 1)
                dve.tensor_tensor(x_lo[:, k, :], merged[:, k, :], x_hi[:, k, :], ALU.subtract).then_inc(S("merged_lo"), 1)
            run_ahead("mix_out", 1)

            def out_normed(n, row, row_sem, landed):
                def out(m):
                    dve.wait_ge(S("post_sq"), 4 * n + 2 * m + 2)
                    dve.scalar_tensor_tensor(out=norm_s[:, 22 + m:23 + m], in0=norm_s[:, 8 + 2 * m:9 + 2 * m],
                                             scalar=RMS_EPS, in1=norm_s[:, 9 + 2 * m:10 + 2 * m], op0=ALU.add,
                                             op1=ALU.add).then_inc(S("post_ms"), 1)
                    dve.wait_ge(S("post_rt"), 2 * n + m + 1)
                    dve.wait_ge(S(row_sem), landed)
                    for c in range(2):
                        cc = slice(c * 512, (c + 1) * 512)
                        ins = dve.scalar_tensor_tensor(out=xn[:, m, cc], in0=pb[4 + 2 * m + c][:, :],
                                                       scalar=norm_s[:, 24 + m:25 + m], in1=row[:, cc],
                                                       op0=ALU.mult, op1=ALU.mult)
                    link(ins)
                    for c in range(2):
                        cc = slice(c * 512, (c + 1) * 512)
                        dve.tensor_tensor(resid[:, m, cc], resid[:, m, cc], xn[:, m, cc],
                                          ALU.add).then_inc(S("resid_done"), 1)
                return out

            norm(1, "ffn_pre", out_normed(0, row_mix, "mix_row", 48))
            dve.sem_inc(S("conv_gfree"), 2)
            dve.sem_inc(S("conv_vfree"), 2)
            dve.sem_inc(S("conv_hid"), 2)

            def conv_taps(j, it):
                side, b = j % 2, j // 2 % 2
                c = cval if side else cgate
                free = S("conv_vfree" if side else "conv_gfree")
                dve.wait_ge(S("conv_tap2"), at(2 * j + 2, it, 8))
                for i in range(2):
                    tile = at(22 * side + j // 2 * 2 + i + COL["conv1_w"] + 44, it, 4)
                    dve.scalar_tensor_tensor(out=c[:, b, i, 1:T], in0=bank(j % 4, 2)[:, i, 0:T - 1],
                                             scalar=cols[:, bass.ds(tile, 1)], in1=c[:, b, i, 1:T],
                                             op0=ALU.mult, op1=ALU.add).then_inc(S("conv_tap1"), 1)
                for i in range(2):
                    tile = at(22 * side + j // 2 * 2 + i + COL["conv1_w"], it, 4)
                    dve.wait_ge(S("conv_tap1"), at(2 * j + i + 1, it, 8))
                    ins = dve.scalar_tensor_tensor(out=c[:, b, i, 2:T], in0=bank(j % 4, 2)[:, i, 0:T - 2],
                                                   scalar=cols[:, bass.ds(tile, 1)], in1=c[:, b, i, 2:T],
                                                   op0=ALU.mult, op1=ALU.add)
                ins.then_inc(free, 1)
                if side:
                    dve.wait_ge(S("conv_gelu"), at(j // 2 + 1, it, 2))
                    dve.wait_ge(S("conv_vfree"), at(j // 2 + 3, it, 2))
                    dve.wait_ge(S("conv_hlo"), at(j // 2 + 1, it, 2))
                    dve.tensor_tensor(hid[:, b, :], gate[:, b, :], cval[:, b, :, :].rearrange("p i n -> p (i n)"),
                                      ALU.mult).then_inc(S("conv_hid"), 1)

            in_step("conv_up", conv_taps)
            run_ahead("conv_down", 1)

            def swiglu_mul(name):
                dve.sem_inc(S(name + "_hid"), 2)

                def body(j, it):
                    if name == "ffn2" and j == 2 * PAIRS - 2:
                        dve.wait_ge(S("ple_hi"), 1)
                        dve.tensor_tensor(p_lo[:, :, :], bank(4, 2), p_hi[:, :, :], ALU.subtract).then_inc(S("ple_lo"), 1)
                    if j % 2 == 0:
                        return
                    b = j // 2 % 2
                    dve.wait_ge(unit_used, at(FIRST[name + "_up"] + j + 1, it, 4))
                    dve.wait_ge(S(name + "_gfree"), at(j // 2 + 3, it, 2))
                    dve.wait_ge(S(name + "_hlo"), at(j // 2 + 1, it, 2))
                    dve.tensor_tensor(hid[:, b, :], pb[j % 4][:, :], gate[:, b, :],
                                      ALU.mult).then_inc(S(name + "_hid"), 1)
                in_step(name + "_up", body)
                if name == "ffn2":
                    ahead(FIRST["ple_proj"])
                run_ahead(name + "_down", 1)

            def add_out(n, scale):
                def out(m):
                    for c in range(2):
                        out_part(dve, n, m, c)
                        r = resid[:, m, c * 512:(c + 1) * 512]
                        dve.scalar_tensor_tensor(out=r, in0=pb[4 + 2 * m + c][:, :], scalar=scale, in1=r, op0=ALU.mult,
                                                 op1=ALU.add).then_inc(S("resid_done"), 1)
                return out

            norm(2, "ffn1", out_normed(1, row_ffn, "ffn_row", 16))
            swiglu_mul("ffn1")
            norm(3, "mix2", add_out(3, 0.5))
            dve.wait_ge(S("dt_whi"), AGAIN["dt_whi"][1] + 1)
            dve.tensor_tensor(w_dt_lo[:, :, :], w_dt[:, :, :], w_dt_hi[:, :, :], ALU.subtract).then_inc(S("dt_wlo"), 1)
            for j in range(4):
                ahead(FIRST["v"] + j)
            dve.wait_ge(S("uvz_free"), 2)
            gstat = gm_s[:, 32:44]
            for m in range(NHALF):
                for c in range(2):
                    link(dve.bn_stats(gstat[:, 6 * c:6 * c + 6], vg_rm[:, m, c * 512:(c + 1) * 512]))
                link(dve.bn_aggr(gm_s[:, 2 * m:2 * m + 2], gstat))
            mvar = gm_s[:, 0:4].rearrange("p (m s) -> p m s", s=2)
            dve.tensor_scalar(gm_s[:, 18:20], mvar[:, :, 1], RMS_EPS, None, ALU.add).then_inc(S("gm_var"), 1)
            dve.wait_ge(S("dt_mm"), AGAIN["dt_mm"][1] + 1)
            bias = rows16[:, 0:1, :].to_broadcast([P, NHALF, 16])
            link(dve.tensor_tensor(dt_s[:, 0, :, :], pb[0][:, 0:32].rearrange("p (m h) -> p m h", m=2), bias, ALU.add))
            dve.scalar_tensor_tensor(out=dt_s[:, 1, :, :], in0=dt_s[:, 0, :, :], scalar=-1.0, in1=dt_s[:, 0, :, :],
                                     op0=ALU.mult, op1=ALU.min).then_inc(S("dt_na"), 1)
            dve.wait_ge(S("gm_rt"), AGAIN["gm_rt"][1] + 1)
            for m in range(NHALF):
                dve.tensor_scalar(vg_rm[:, m, :], vg_rm[:, m, :], gm_s[:, 2 * m:2 * m + 1], gm_s[:, 22 + m:23 + m],
                                  ALU.subtract, ALU.mult).then_inc(S("gm_vn"), 1)
            tri4 = consts[:, KIND["tri"]:KIND["tri"] + 1, :].to_broadcast([P, 4, P])
            dve.wait_ge(S("gm_wt"), AGAIN["gm_wt"][1] + 1)
            for b in range(2):
                dve.tensor_tensor(ws_t[:, 4 * b:4 * b + 4, :], bank(1 + b, 4), tri4, ALU.mult).then_inc(S("gm_wtc"), 1)
            ahead(FIRST["u"])
            ahead(FIRST["u"] + 1)
            dve.wait_ge(S("dt_e"), AGAIN["dt_e"][1] + 2)
            e, s_, z_, acc = (dt_s[:, k, :, :] for k in (2, 3, 4, 5))
            link(dve.tensor_scalar(s_, e, 2.0, None, ALU.add))
            link(dve.reciprocal(z_, s_))
            link(dve.tensor_tensor(s_, e, z_, ALU.mult))
            link(dve.tensor_tensor(z_, s_, s_, ALU.mult))
            link(dve.tensor_scalar(acc, z_, 2.0 / 17, 2.0 / 15, ALU.mult, ALU.add))
            for k in (13, 11, 9, 7, 5, 3, 1):
                link(dve.tensor_tensor(acc, acc, z_, ALU.mult))
                link(dve.tensor_scalar(acc, acc, 2.0 / k, None, ALU.add))
            link(dve.tensor_tensor(acc, acc, s_, ALU.mult))
            link(dve.scalar_tensor_tensor(out=acc, in0=dt_s[:, 0, :, :], scalar=0.0, in1=acc, op0=ALU.max, op1=ALU.add))
            dve.scalar_tensor_tensor(out=dt_s[:, 6, :, :], in0=acc, scalar=-1.0,
                                     in1=rows16[:, 1:2, :].to_broadcast([P, NHALF, 16]),
                                     op0=ALU.mult, op1=ALU.mult).then_inc(S("dt_adt"), 1)
            ahead(FIRST["u"] + 2)
            ahead(FIRST["u"] + 3)
            dve.wait_ge(S("dt_cs"), AGAIN["dt_cs"][1] + 1)
            cs_p = pb[3][:, 0:32].rearrange("p (m h) -> p m h", m=2)
            dve.tensor_copy(dt_s[:, 7, :, :], cs_p).then_inc(S("dt_csd"), 1)
            dve.wait_ge(S("dt_csd"), 1)
            dve.tensor_tensor(dt_s[:, 8, :, :], pb[3][:, 32:64].rearrange("p (m h) -> p m h", m=2), dt_s[:, 7, :, :],
                              ALU.subtract).then_inc(S("dt_csd"), 1)
            dve.wait_ge(S("dt_csd"), 2)
            dve.sem_inc(S("dt_csd"), 1)
            dve.sem_inc(S("dt_used"), 1)

            def gated(m):
                dve.wait_ge(S("gm_mix"), AGAIN["gm_mix"][1] + m + 1)
                dve.wait_ge(S("uvz_free"), 4)
                for h in range(8):
                    u = u_rm[:, m, h * P:(h + 1) * P]
                    ins = dve.scalar_tensor_tensor(out=u, in0=pb[2 * m + h // 4][:, h % 4 * P:(h % 4 + 1) * P],
                                                   scalar=col("gm_b", h), in1=u, op0=ALU.add, op1=ALU.mult)
                ins.then_inc(S("gm_ya"), 1)

            def gating_norm():
                dve.wait_ge(S("gm_sq"), AGAIN["gm_sq"][1] + 2)
                dve.tensor_scalar(gm_s[:, 26:28], gm_s[:, 24:26], 1.0 / D, RMS_EPS, ALU.mult,
                                  ALU.add).then_inc(S("gm_ms"), 1)
                dve.wait_ge(S("gm_rt"), AGAIN["gm_rt"][1] + 2)
                for m in range(NHALF):
                    ins = dve.tensor_scalar(u_rm[:, m, :], u_rm[:, m, :], gm_s[:, 30 + m:31 + m], None, ALU.mult)
                ins.then_inc(S("gm_y"), 1)

            def xbc_taps(j, it):
                if j == 5:
                    turned_lo(0, "gm_hi", (0, 1, 2, 3), "gm_out", y2_hi, y2_lo, "gm_lo")
                if j < 2:
                    gated(j)
                for i in range(2):
                    k = 2 * j + i
                    dve.wait_ge(S("xbc_tap3"), 2 * j + 2)
                    for back in (1, 2, 3):
                        n = 6 * j + 3 * i + back
                        if back > 1:
                            dve.wait_ge(S("xbc_taps"), n - 1)
                        dve.scalar_tensor_tensor(out=xbc_f[:, k, back:T], in0=bank(4 + j % 4, 2)[:, i, 0:T - back],
                                                 scalar=col("conv2_w", 12 * (3 - back) + k), in1=xbc_f[:, k, back:T],
                                                 op0=ALU.mult, op1=ALU.add).then_inc(S("xbc_taps"), 1)
                if j == 3:
                    gating_norm()

            in_step("xbc", xbc_taps)
            ahead(FIRST["z"] - 1)

            def behind_2(step):
                if step in POOL_SPLITS_2:
                    nxt[0] = FIRST["z"] + BEFORE_2[step] // 4 + AHEAD
                    return
                if step == "f0":
                    dve.wait_ge(lo_split, nxt[0])
                ahead(FIRST["z"] + BEFORE_2[step] // 4)

            def heads16(ap):
                return ap.unsqueeze(2).to_broadcast([P, 16, 64])

            def by_head(ap):
                return ap.rearrange("p (h d) -> p h d", d=64)

            behind_2("xs")
            dve.wait_ge(S("ssm_xrm"), 1)
            link(dve.tensor_tensor(by_head(xd_rm[:, 0, :]), by_head(xs_rm[:, 0, :]), heads16(dt_s[:, 5, 0, :]), ALU.mult))
            dve.wait_ge(S("dt_ecs"), AGAIN["dt_ecs"][1] + 1)
            dve.wait_ge(S("ssm_xrm"), 2)
            dve.wait_ge(S("ssm_tr"), 2)
            dve.tensor_tensor(by_head(y_rm[:, 1, :]), by_head(xd_rm[:, 0, :]), heads16(dt_s[:, 10, 0, :]),
                              ALU.mult).then_inc(S("ssm_xds"), 1)
            behind_2("bm")
            dve.wait_ge(S("ssm_cb"), AGAIN["ssm_cb"][1] + 1)
            tri4 = consts[:, KIND["tri"]:KIND["tri"] + 1, :].to_broadcast([P, 4, P])
            dve.tensor_tensor(cb[:, :, :], bank(1, 4), tri4, ALU.mult).then_inc(S("ssm_cbc"), 1)
            dve.tensor_tensor(by_head(xd_rm[:, 1, :]), by_head(xs_rm[:, 1, :]), heads16(dt_s[:, 5, 1, :]), ALU.mult)
            behind_2("st")

            def decays(n):
                m, g = divmod(n, 2)
                a = att[n % 2]
                dve.wait_ge(S("ssm_row"), AGAIN["ssm_row"][1] + n + 1)
                if n >= 2:
                    dve.wait_ge(S("ssm_y"), n - 1)
                for b in range(2):
                    h = 8 * g + 4 * b
                    dve.tensor_tensor(a[:, 4 * b:4 * b + 4, :], bank(b, 4),
                                      dt_s[:, 7, m, h:h + 4].unsqueeze(2).to_broadcast([P, 4, P]),
                                      ALU.subtract).then_inc(S("ssm_diff"), 1)
                dve.wait_ge(S("ssm_diff"), AGAIN["ssm_diff"][1] + 2 * n + 2)
                dve.tensor_scalar(a[:, :, :], a[:, :, :], 0.0, None, ALU.min).then_inc(S("ssm_min"), 1)

            decays(0)
            dve.tensor_tensor(by_head(y_rm[:, 0, :]), by_head(xs_rm[:, 0, :]), heads16(rows16[:, 2, :]), ALU.mult)
            dve.wait_ge(S("ssm_state"), AGAIN["ssm_state"][1] + 1)
            link(dve.tensor_tensor(by_head(y_rm[:, 1, :]), by_head(xs_rm[:, 1, :]), heads16(rows16[:, 2, :]),
                                   ALU.mult))
            behind_2("row")
            dve.wait_ge(S("ssm_cbc"), 1)
            for n in range(4):
                m, g = divmod(n, 2)
                dve.wait_ge(S("ssm_exp"), AGAIN["ssm_exp"][1] + n + 1)
                dve.tensor_tensor(att[n % 2][:, :, :], att[n % 2][:, :, :], cb[:, n:n + 1, :].to_broadcast([P, 8, P]),
                                  ALU.mult).then_inc(S("ssm_att"), 1)
                if n < 3:
                    decays(n + 1)
                behind_2(f"a{n}")
                y = y_rm[:, m, g * 512:(g + 1) * 512]
                dve.wait_ge(S("ssm_y"), n + 1)
                ins = dve.tensor_tensor(y, y, pb[2][:, :], ALU.add)
                if m:
                    link(ins)
                    dve.wait_ge(S("ssm_off"), AGAIN["ssm_off"][1] + g + 1)
                    tmp = xs_rm[:, 0, g * 512:(g + 1) * 512]
                    link(dve.tensor_tensor(by_head(tmp), by_head(pb[3][:, :]),
                                           dt_s[:, 9, 1, 8 * g:8 * g + 8].unsqueeze(2).to_broadcast([P, 8, 64]),
                                           ALU.mult))
                    ins = dve.tensor_tensor(y, y, tmp, ALU.add)
                ins.then_inc(S("ssm_yadd"), 1)
            dve.wait_ge(S("uvz_free"), 6)
            for m in range(NHALF):
                dve.wait_ge(S("ssm_yadd"), 4)
                dve.tensor_tensor(y_rm[:, m, :], y_rm[:, m, :], z_s[:, m, :], ALU.mult).then_inc(S("ssm_yz"), 1)
            behind_2("f0")
            dve.wait_ge(S("ssm_sq"), AGAIN["ssm_sq"][1] + 4)
            dve.tensor_scalar(dt_s[:, 11, 0, 4:8], dt_s[:, 11, 0, 0:4], 1.0 / 512, RMS_EPS, ALU.mult,
                              ALU.add).then_inc(S("ssm_ms"), 1)
            dve.wait_ge(S("ssm_rt"), AGAIN["ssm_rt"][1] + 1)
            for n in range(4):
                y = y_rm[:, n // 2, n % 2 * 512:(n % 2 + 1) * 512]
                dve.tensor_scalar(y, y, dt_s[:, 11, 0, 12 + n:13 + n], None, ALU.mult).then_inc(S("ssm_yn"), 1)
            turned_lo(0, "ssm_hi", (0, 1, 2, 3), "ssm", y2_hi[:, 8:16, :], y2_lo[:, 8:16, :], "ssm_lo")
            behind_2("f1")
            for u in range(FIRST["mix2_out"] + 4, FIRST["mix2_out"] + 7):
                ahead(u)
            norm(4, "ffn2", add_out(4, 1.0))
            swiglu_mul("ffn2")
            norm(5, "ple", add_out(5, 0.5))
            run_ahead("ple_gate", 1)
            def gate_bias(m):
                for c in range(2):
                    cc = slice(c * 512, (c + 1) * 512)
                    out_part(dve, 6, m, c)
                    dve.tensor_tensor(gsig[:, m, cc], pb[4 + 2 * m + c][:, :], row_ple[:, cc],
                                      ALU.add).then_inc(S("ple_g"), 1)

            gate_bias(0)
            for m in range(NHALF):
                for c in range(2):
                    cc = slice(c * 512, (c + 1) * 512)
                    dve.wait_ge(S("ple_sig"), 2 * m + c + 1)
                    link(dve.tensor_tensor(gsig[:, m, cc], proj[:, m, cc], gsig[:, m, cc], ALU.mult))
                    dve.tensor_tensor(resid[:, m, cc], resid[:, m, cc], gsig[:, m, cc],
                                      ALU.add).then_inc(S("resid_done"), 1)
                sum_squares(6, m)
                if m == 0:
                    gate_bias(1)
                dve.wait_ge(S("norm_rt"), 2 * 6 + m + 1)
                for c in range(2):
                    cc = slice(c * 512, (c + 1) * 512)
                    dve.scalar_tensor_tensor(out=xn[:, m, cc], in0=resid[:, m, cc], scalar=norm_s[:, 6 + m:7 + m],
                                             in1=row_fin[:, cc], op0=ALU.mult, op1=ALU.mult).then_inc(S("out_ready"), 1)


_NAMES = ("x", "positions", "w_in", "rw_w2", "rw_a2", "rw_g2", "w_branch_rw", "w_branch_ret", "w_out", "ffn_w_up",
          "ffn_w_down", "p_2", "ffn1_w_gate_2", "ffn1_w_up_2", "ffn1_w_down_2", "w_in_2", "gm_w_s_2", "dt_bias_2",
          "a_log_2", "d_skip_2", "w_out_2", "ffn2_w_gate_2", "ffn2_w_up_2", "ffn2_w_down_2", "ple_w_gate_2",
          "ple_w_proj_2")


def laid_out(inputs):
    arrays = {}
    for name in _NAMES:
        a = np.asarray(inputs[name])
        keep = 1 if name in ("dt_bias_2", "a_log_2", "d_skip_2") else None
        if name == "positions":
            a = np.ascontiguousarray(a.reshape(NHALF, P).T)
        elif name == "p_2":
            a = a.reshape(T, -1)
        elif keep is None:
            a = a.reshape(a.shape[1:])
        arrays[name] = np.ascontiguousarray(a)
    packed = {
        "mix_pre": "norm_mix_pre", "ffn_pre": "norm_ffn_pre", "mu": "rw_mu", "w0": "rw_w0", "a0": "rw_a0",
        "k_k": "rw_k_k", "k_a": "rw_k_a", "r_k": "rw_r_k", "lnx_w": "rw_lnx_w", "lnx_b": "rw_lnx_b",
        "conv1_w": "ffn_conv_w", "conv1_b": "ffn_conv_b", "ffn1": "ffn1_norm_2", "mix2": "mix_norm_2",
        "gm_b": "gm_b_s_2", "gm_out": "gm_out_norm_2", "conv2_w": "conv_w_2", "conv2_b": "conv_b_2",
        "ssm": "ssm_norm_2", "ffn2": "ffn2_norm_2", "ple": "ple_norm_2",
    }
    arrays["cols"] = np.ascontiguousarray(
        np.concatenate([np.asarray(inputs[packed[name]]).reshape(n, P) for name, n in COLS]).T)
    rows = {"mix_post": "norm_mix_post", "ffn_post": "norm_ffn_post", "gm_ln_g": "gm_ln_g_2", "gm_ln_b": "gm_ln_b_2",
            "ple_b": "ple_b_gate_2", "final": "final_norm_2"}
    arrays["rows"] = np.ascontiguousarray(np.stack([np.asarray(inputs[rows[name]]).reshape(D) for name in ROWS]))
    arrays["consts"] = shape_constants()
    return arrays


def kernel(**inputs):
    import concourse.bacc as bacc
    from concourse.bass_utils import run_bass_kernel_spmd

    arrays = laid_out(inputs)
    nc = bacc.Bacc("TRN2", target_bir_lowering=False, num_devices=1)
    io = {name: nc.dram_tensor(f"in_{name}", a.shape, mybir.dt.from_np(a.dtype), kind="ExternalInput").ap()
          for name, a in arrays.items()}
    out = nc.dram_tensor("out", (T, D), F32, kind="ExternalOutput").ap()
    two_layers(nc, io, out)
    r = run_bass_kernel_spmd(nc, [{f"in_{n}": a for n, a in arrays.items()}], core_ids=[0])
    return r.results[0]["out"].reshape(1, T, D)
```
